# Optimizing a Trainium2 kernel written in Bass

```python
import math, functools
import jax, jax.numpy as jnp
from jax import lax
import numpy as np

D_MODEL = 1024
BATCH = 1
SEQ = 1024
DEPTH = 1
DEC_BATCH = 8
DEC_SEQ = 4
PAST_LEN = 4096
PAGE_SIZE = 128

N_META = 16
POOL_WIDTH = D_MODEL // 2
POOL_WINDOWS = (2, 4, 8, 16)
POOL_GROUPS = len(POOL_WINDOWS)
POOL_GROUP_DIM = POOL_WIDTH // POOL_GROUPS
POOL_STATE = max(POOL_WINDOWS) - 1
HEAD_DIM = 64
N_HEADS = (D_MODEL // 2) // HEAD_DIM
N_KV_HEADS = 2
GROUP = N_HEADS // N_KV_HEADS
WINDOW = 128
ATTN_BLOCK = 128
ATTN_SCALE = HEAD_DIM ** -0.5
NUM_BUCKETS = 32
MAX_DISTANCE = 128
Q_DIM = N_HEADS * HEAD_DIM
KV_DIM = N_KV_HEADS * HEAD_DIM
OFF_Q = POOL_WIDTH
OFF_K = OFF_Q + Q_DIM
OFF_V = OFF_K + KV_DIM
OFF_GA = OFF_V + KV_DIM
OFF_GB = OFF_GA + D_MODEL
IN_DIM = OFF_GB + D_MODEL
PEER_HEADS = 8
N_KEYS = 128
N_EXPERTS = N_KEYS * N_KEYS
PEER_TOPK = 16
PEER_QDIM = 256
PEER_HALF = PEER_QDIM // 2
PEER_BLOCK = 128
ALPHA = (2 * DEPTH) ** 0.25
BETA = (8 * DEPTH) ** -0.25
LN_EPS = 1e-5

kernel_name = 'hybrid_pool_swa_peer_step'

def layer_norm(x, g, b):
    xf = x.astype(jnp.float32)
    mu = jnp.mean(xf, axis=-1, keepdims=True)
    var = jnp.mean(jnp.square(xf - mu), axis=-1, keepdims=True)
    return ((xf - mu) * lax.rsqrt(var + LN_EPS) * g + b).astype(x.dtype)

def rel_bucket(dist):
    n = jnp.maximum(dist, 0)
    max_exact = NUM_BUCKETS // 2
    large = max_exact + (jnp.log(jnp.maximum(n, max_exact).astype(jnp.float32) / max_exact)
                         / math.log(MAX_DISTANCE / max_exact)
                         * (NUM_BUCKETS - max_exact)).astype(jnp.int32)
    large = jnp.minimum(large, NUM_BUCKETS - 1)
    return jnp.where(n < max_exact, n, large)

def rel_bias(table, dist):
    b = table[rel_bucket(dist)].astype(jnp.float32)
    b = jnp.moveaxis(b, -1, 0)
    return b.reshape(N_KV_HEADS, GROUP, *dist.shape)

def sink_softmax(s, sink):
    sk = sink.astype(jnp.float32).reshape(N_KV_HEADS, GROUP, 1, 1)
    m = jnp.maximum(jnp.max(s, axis=-1, keepdims=True), sk)
    e = jnp.exp(s - m)
    return e / (jnp.sum(e, axis=-1, keepdims=True) + jnp.exp(sk - m))

def pool_mixer(p_new, p_prev, pos0, w_pool_mix, pool_scale):
    B, S, _ = p_new.shape
    ext = jnp.concatenate([p_prev, p_new], axis=1)
    cs = jnp.cumsum(ext.astype(jnp.float32), axis=1)
    cs = jnp.concatenate([jnp.zeros_like(cs[:, :1]), cs], axis=1)
    end = cs[:, POOL_STATE + 1:]
    pos = pos0 + jnp.arange(S)
    outs = []
    for g, w in enumerate(POOL_WINDOWS):
        sl = slice(g * POOL_GROUP_DIM, (g + 1) * POOL_GROUP_DIM)
        start = cs[:, POOL_STATE + 1 - w:POOL_STATE + 1 - w + S, sl]
        cnt = jnp.minimum(w, pos + 1).astype(jnp.float32)[None, :, None]
        outs.append((end[..., sl] - start) / cnt)
    pooled = jnp.stack(outs, axis=2) - p_new.reshape(B, S, POOL_GROUPS, POOL_GROUP_DIM).astype(jnp.float32)
    mixed = jnp.einsum('bsgc,gcd->bsgd', pooled.astype(p_new.dtype), w_pool_mix).reshape(B, S, POOL_WIDTH)
    return mixed * pool_scale, ext[:, -POOL_STATE:]

def swa_prompt(q, k, v, sink, rel_table):
    B, T = q.shape[:2]
    pad = (-T) % ATTN_BLOCK
    Tp = T + pad
    nb = Tp // ATTN_BLOCK
    padf = lambda a: jnp.pad(a, ((0, 0), (pad, 0), (0, 0), (0, 0)))
    qb = padf(q).reshape(B, nb, ATTN_BLOCK, N_KV_HEADS, GROUP, HEAD_DIM)
    kb = padf(k).reshape(B, nb, ATTN_BLOCK, N_KV_HEADS, HEAD_DIM)
    vb = padf(v).reshape(B, nb, ATTN_BLOCK, N_KV_HEADS, HEAD_DIM)
    shift = lambda a: jnp.concatenate([jnp.zeros_like(a[:, :1]), a[:, :-1]], axis=1)
    kk = jnp.concatenate([shift(kb), kb], axis=2)
    vv = jnp.concatenate([shift(vb), vb], axis=2)
    qi = jnp.arange(ATTN_BLOCK)[:, None]
    kj = jnp.arange(2 * ATTN_BLOCK)[None, :]
    dist = ATTN_BLOCK + qi - kj
    kpos = (jnp.arange(nb)[:, None] - 1) * ATTN_BLOCK + jnp.arange(2 * ATTN_BLOCK)[None, :] - pad
    mask = ((dist >= 0) & (dist < WINDOW))[None] & (kpos >= 0)[:, None, :]
    bias = rel_bias(rel_table, dist)
    s = jnp.einsum('bnqkgd,bnskd->bnkgqs', qb, kk).astype(jnp.float32) * ATTN_SCALE + bias
    s = jnp.where(mask[None, :, None, None], s, -jnp.inf)
    p = sink_softmax(s, sink)
    o = jnp.einsum('bnkgqs,bnskd->bnqkgd', p.astype(vv.dtype), vv).reshape(B, Tp, Q_DIM)[:, pad:]
    w = min(WINDOW, T)
    return o, k[:, -w:], v[:, -w:]

def swa_sample(q, k, v, ck, cv, sink, rel_table, pos0):
    B, S = q.shape[:2]
    W = ck.shape[1]
    kk = jnp.concatenate([ck, k], axis=1)
    vv = jnp.concatenate([cv, v], axis=1)
    qpos = pos0 + jnp.arange(S)
    kpos = jnp.concatenate([pos0 - W + jnp.arange(W), qpos])
    dist = qpos[:, None] - kpos[None, :]
    mask = (dist >= 0) & (dist < WINDOW)
    bias = rel_bias(rel_table, dist)
    qg = q.reshape(B, S, N_KV_HEADS, GROUP, HEAD_DIM)
    s = jnp.einsum('bqkgd,bskd->bkgqs', qg, kk).astype(jnp.float32) * ATTN_SCALE + bias
    s = jnp.where(mask, s, -jnp.inf)
    p = sink_softmax(s, sink)
    o = jnp.einsum('bkgqs,bskd->bqkgd', p.astype(vv.dtype), vv).reshape(B, S, Q_DIM)
    return o, kk[:, -W:], vv[:, -W:]

def peer(x, w_query, sub_keys, expert_u, expert_v):
    B, T, D = x.shape
    n = B * T
    pad = (-n) % PEER_BLOCK
    xt = jnp.pad(x.reshape(n, D), ((0, pad), (0, 0))).reshape(-1, PEER_BLOCK, D)

    def block(xb):
        q = (xb @ w_query).reshape(PEER_BLOCK, PEER_HEADS, 2, PEER_HALF)
        sc = jnp.einsum('thcd,hcnd->thcn', q, sub_keys).astype(jnp.float32)
        top_s, top_i = lax.top_k(sc, PEER_TOPK)
        cand = top_s[:, :, 0, :, None] + top_s[:, :, 1, None, :]
        cand_idx = top_i[:, :, 0, :, None] * N_KEYS + top_i[:, :, 1, None, :]
        best_s, best_j = lax.top_k(cand.reshape(PEER_BLOCK, PEER_HEADS, -1), PEER_TOPK)
        idx = jnp.take_along_axis(cand_idx.reshape(PEER_BLOCK, PEER_HEADS, -1), best_j, axis=-1)
        gate = jax.nn.softmax(best_s, axis=-1)
        u = jnp.take(expert_u, idx, axis=0)
        h = jax.nn.gelu(jnp.einsum('td,thkd->thk', xb, u).astype(jnp.float32), approximate=False)
        wgt = (gate * h).astype(xb.dtype)
        return jnp.einsum('thk,thkd->td', wgt, jnp.take(expert_v, idx, axis=0))

    y = lax.map(block, xt).reshape(-1, D)[:n]
    return y.reshape(B, T, D)

def layer_step(x, pool_prev, pos0, attn_fn, w_in, w_pool_mix, pool_scale, w_up_pool, w_up_attn,
               w_out, ln1_g, ln1_b, peer_w_query, peer_sub_keys, peer_u, peer_v, ln2_g, ln2_b):
    B, T, _ = x.shape
    z = x @ w_in
    p = z[..., :OFF_Q]
    q = z[..., OFF_Q:OFF_K].reshape(B, T, N_HEADS, HEAD_DIM)
    k = z[..., OFF_K:OFF_V].reshape(B, T, N_KV_HEADS, HEAD_DIM)
    v = z[..., OFF_V:OFF_GA].reshape(B, T, N_KV_HEADS, HEAD_DIM)
    g_pool = jax.nn.sigmoid(z[..., OFF_GA:OFF_GB])
    g_attn = jax.nn.sigmoid(z[..., OFF_GB:])
    pool_out, pool_state = pool_mixer(p, pool_prev, pos0, w_pool_mix, pool_scale)
    attn_out, k_state, v_state = attn_fn(q, k, v)
    m = g_pool * (pool_out @ w_up_pool) + g_attn * (attn_out @ w_up_attn)
    x = layer_norm(ALPHA * x + m @ w_out, ln1_g, ln1_b)
    x = layer_norm(ALPHA * x + peer(x, peer_w_query, peer_sub_keys, peer_u, peer_v), ln2_g, ln2_b)
    return x, k_state, v_state, pool_state

def setup_inputs(seed: int = 0) -> dict:
    key = jax.random.key(seed)
    ks = jax.random.split(key, 24)
    nrm = lambda k, shape, scale: jax.random.normal(k, shape, jnp.float32) * scale
    w_cache = min(WINDOW, PAST_LEN)
    return {
        'x_prompt': nrm(ks[0], (BATCH, SEQ, D_MODEL), 1.0),
        'x_sample': nrm(ks[1], (DEC_BATCH, DEC_SEQ, D_MODEL), 1.0),
        'cache_k': nrm(ks[2], (DEPTH, DEC_BATCH, w_cache, N_KV_HEADS, HEAD_DIM), 1.0),
        'cache_v': nrm(ks[3], (DEPTH, DEC_BATCH, w_cache, N_KV_HEADS, HEAD_DIM), 1.0),
        'state_pool': nrm(ks[4], (DEPTH, DEC_BATCH, POOL_STATE, POOL_WIDTH), 1.0),
        'meta_tokens': nrm(ks[5], (N_META, D_MODEL), 1.0),
        'rel_bias_table': nrm(ks[6], (NUM_BUCKETS, N_HEADS), 0.5),
        'w_in': nrm(ks[7], (DEPTH, D_MODEL, IN_DIM), D_MODEL ** -0.5),
        'w_pool_mix': nrm(ks[8], (DEPTH, POOL_GROUPS, POOL_GROUP_DIM, POOL_GROUP_DIM), POOL_GROUP_DIM ** -0.5),
        'pool_scale': 1.0 + nrm(ks[9], (DEPTH, POOL_WIDTH), 0.1),
        'attn_sinks': nrm(ks[10], (DEPTH, N_HEADS), 1.0),
        'w_up_pool': nrm(ks[11], (DEPTH, POOL_WIDTH, D_MODEL), POOL_WIDTH ** -0.5),
        'w_up_attn': nrm(ks[12], (DEPTH, Q_DIM, D_MODEL), Q_DIM ** -0.5),
        'w_out': nrm(ks[13], (DEPTH, D_MODEL, D_MODEL), BETA * D_MODEL ** -0.5),
        'ln1_g': 1.0 + nrm(ks[14], (DEPTH, D_MODEL), 0.02),
        'ln1_b': nrm(ks[15], (DEPTH, D_MODEL), 0.02),
        'peer_w_query': nrm(ks[16], (DEPTH, D_MODEL, PEER_HEADS * PEER_QDIM), D_MODEL ** -0.5),
        'peer_sub_keys': nrm(ks[17], (DEPTH, PEER_HEADS, 2, N_KEYS, PEER_HALF), PEER_HALF ** -0.5),
        'peer_u': nrm(ks[18], (DEPTH, N_EXPERTS, D_MODEL), D_MODEL ** -0.5),
        'peer_v': nrm(ks[19], (DEPTH, N_EXPERTS, D_MODEL), BETA),
        'ln2_g': 1.0 + nrm(ks[20], (DEPTH, D_MODEL), 0.02),
        'ln2_b': nrm(ks[21], (DEPTH, D_MODEL), 0.02),
    }

def reference(x_prompt, x_sample, cache_k, cache_v, state_pool, meta_tokens, rel_bias_table, w_in,
              w_pool_mix, pool_scale, attn_sinks, w_up_pool, w_up_attn, w_out, ln1_g, ln1_b,
              peer_w_query, peer_sub_keys, peer_u, peer_v, ln2_g, ln2_b):
    B = x_prompt.shape[0]
    meta = jnp.broadcast_to(meta_tokens.astype(x_prompt.dtype)[None], (B, N_META, D_MODEL))
    xp = jnp.concatenate([meta, x_prompt], axis=1)
    xs = x_sample
    kps, vps, sps, kss, vss, sss = [], [], [], [], [], []
    for l in range(DEPTH):
        lw = (w_in[l], w_pool_mix[l], pool_scale[l], w_up_pool[l], w_up_attn[l], w_out[l],
              ln1_g[l], ln1_b[l], peer_w_query[l], peer_sub_keys[l], peer_u[l], peer_v[l],
              ln2_g[l], ln2_b[l])
        attn_p = functools.partial(swa_prompt, sink=attn_sinks[l], rel_table=rel_bias_table)
        pool_zero = jnp.zeros((B, POOL_STATE, POOL_WIDTH), xp.dtype)
        xp, kp, vp, sp = layer_step(xp, pool_zero, 0, attn_p, *lw)
        attn_s = functools.partial(swa_sample, ck=cache_k[l], cv=cache_v[l], sink=attn_sinks[l],
                                   rel_table=rel_bias_table, pos0=PAST_LEN)
        xs, ksm, vsm, ssm = layer_step(xs, state_pool[l], PAST_LEN, attn_s, *lw)
        kps.append(kp); vps.append(vp); sps.append(sp)
        kss.append(ksm); vss.append(vsm); sss.append(ssm)
    return (xp[:, N_META:], xs, jnp.stack(kps), jnp.stack(vps), jnp.stack(sps),
            jnp.stack(kss), jnp.stack(vss), jnp.stack(sss))


_drawn_inputs = setup_inputs


def setup_inputs(seed=0):
    import zlib

    import numpy as np

    out = dict(_drawn_inputs(seed))
    spreads = {}
    factors = {'meta_tokens': 2.724, 'attn_sinks': 8.0, 'ln2_g': 2.948, 'ln2_b': 2.748}
    for name, (base, spread) in spreads.items():
        noise = np.random.default_rng([zlib.crc32(name.encode()), seed]).standard_normal(out[name].shape)
        drawn = base * np.exp(spread * noise) if base else spread * noise
        out[name] = __import__('jax').numpy.asarray(drawn.astype(out[name].dtype))
    for name, factor in factors.items():
        out[name] = (out[name] * factor).astype(out[name].dtype)
    return out
```

```python
from contextlib import ExitStack
from functools import partial

import concourse.bass as bass
from concourse import mybir

F32 = mybir.dt.float32
I32 = mybir.dt.int32
U32 = mybir.dt.uint32
ALU = mybir.AluOpType
ACT = mybir.ActivationFunctionType
AX = mybir.AxisListType

P = 128
D = 1024
DC = D // P
GROUPS = 4
BLK = 2
GN = BLK * P
META = 16
SAMP = 32
SEQS = 8
DSEQ = 4
X0 = META + SAMP
COLS = X0 + GN
HD = 64
HPK = 4
WIN = 128
HIST = 16
PSTATE = 15
SCALE = HD ** -0.5
ALPHA = 2.0 ** 0.25
EPS = 1e-5
NEG = -1e30
HEADS = 8
TOPK = 16
SLOTS = HEADS * TOPK
RING = 8
BODY = 2 * RING
BATCH = 4

WR = 4
POS_K, POS_V, POS_IN, POS_UP, POS_OUT, POS_QRY, POS_END = 0, 1, 4, 28, 36, 44, 60
HOLES = (2, 3)
UNITS = POS_END - len(HOLES)
N_IN = POS_UP - POS_IN
N_UP = POS_OUT - POS_UP
N_OUT = POS_QRY - POS_OUT
N_QRY = POS_END - POS_QRY
PROJ = 2 + N_IN


def ordinal(pos):
    return pos if pos < HOLES[0] else pos - len(HOLES)


def loads_upto(pos):
    return sum(1 for n in range(pos % WR, pos + 1, WR) if n not in HOLES)


LOADS = [loads_upto(POS_END - WR + s) for s in range(WR)]


def wait(eng, sem, value):
    if not isinstance(value, int) or value > 0:
        eng.wait_ge(sem, value)


def hold(eng, sem, value):
    eng.wait_ge(sem, value)
    eng.nop(nofuse=True)


def nth(g, b):
    return b + 1 if isinstance(g, int) and g == 0 else g * BLK + (b + 2)


def first(g):
    return isinstance(g, int) and g == 0


def layer_kernel(nc, xT, xT_extra, x_rows, xs_rows, w_a, w_q, uv, table, sinks, sink_rows, w_mix, pool_scale,
                 ln1_g, ln1_b, ln2_g, ln2_b, ckT, cv_rows, cache_v, stT,
                 ident_c, flip_c, onehot_c, linemask_c, sel_c, smask_c, iota_c,
                 line_scratch, y_prompt, y_sample, k_prompt, v_prompt, pool_prompt, k_sample, v_sample, pool_sample):
    with ExitStack() as ctx:
        def sb(name, shape, dt=F32):
            return ctx.enter_context(nc.sbuf_tensor(name, shape, dt))

        def sem(name):
            return ctx.enter_context(nc.semaphore(name))

        ident = sb("ident", [P, P])
        alpha_i = sb("alpha_i", [P, P])
        zeros = sb("zeros", [P, P])
        iota = sb("iota", [P, TOPK])
        bias = sb("bias", [P, HEADS, 2 * P])
        sink = sb("sink", [P, HEADS])
        wmix = sb("wmix", [P, 4, P])
        pscale = sb("pscale", [P, 4])
        ln2g = sb("ln2g", [P, D])
        ln2b = sb("ln2b", [P, D])
        wring = sb("wring", [P, WR, D + P])
        xm = sb("xm", [P, DC, COLS])
        poolT = sb("poolT", [P, 4, HIST + GN])
        pooled = sb("pooled", [P, 4, SAMP + GN])
        qT = sb("qT", [P, 4, SAMP + GN])
        kT = sb("kT", [P, P + GN])
        vR = sb("vR", [P, BLK + 1, P])
        big = sb("big", [P, 3 * 2048])
        att = sb("att", [P, 3072])
        amx = sb("amx", [P, 2, 4])
        anm = sb("anm", [P, 2, 4])
        ads = sb("ads", [P, 2, 4])
        aden = sb("aden", [P, 2, 4])
        stats = sb("stats", [P, 12])
        moments = sb("moments", [P, 4])
        stats2 = sb("stats2", [P, 12])
        moments2 = sb("moments2", [P, 4])
        qyT = sb("qyT", [P, 2, SAMP + GN])
        x1n = sb("x1n", [P, BLK, D])
        x1c = sb("x1c", [P, BLK, D])
        x1s = sb("x1s", [SAMP, D])
        idxn = sb("idxn", [P, BLK, SLOTS], I32)
        idxc = sb("idxc", [P, BLK, SLOTS], I32)
        idxs = sb("idxs", [SAMP, SLOTS], I32)
        gaten = sb("gaten", [P, BLK, SLOTS])
        gatec = sb("gatec", [P, BLK, SLOTS])
        gates_s = sb("gates_s", [SAMP, SLOTS])
        idx8 = [sb(f"idx8_{n}", [P, RING], I32) for n in range(2)]
        tops = sb("tops", [P, HEADS, 2, TOPK])
        topi = sb("topi", [P, HEADS, 2, TOPK], U32)
        topf = sb("topf", [P, HEADS, 2, TOPK])
        bests = sb("bests", [P, HEADS, TOPK])
        bestj = sb("bestj", [P, HEADS, TOPK], U32)
        jpart = sb("jpart", [P, SLOTS], U32)
        jf = sb("jf", [P, SLOTS])
        ipart = sb("ipart", [P, 2, SLOTS])
        gsum = sb("gsum", [P, HEADS])
        hdot = sb("hdot", [P, 2, BATCH])
        hgelu = sb("hgelu", [P, 2, BATCH])
        hw = sb("hw", [P, 2, BATCH])
        diag = sb("diag", [P, RING, P])
        ring = sb("ring", [P, RING, 2 * D])

        def early(tile, off, *dims):
            size = 1
            for d in dims:
                size *= d
            ap = ring[:, tile, off:off + size]
            if len(dims) == 2:
                return ap.rearrange("p (a b) -> p a b", a=dims[0])
            if len(dims) == 3:
                return ap.rearrange("p (a b c) -> p a b c", a=dims[0], b=dims[1])
            return ap

        kX = early(0, 0, SEQS, WIN + DSEQ)
        sPool = early(1, 0, 4, SEQS, PSTATE + DSEQ)
        sT1 = early(1, 640, SEQS, PSTATE + DSEQ)
        sT2 = early(1, 832, SEQS, PSTATE + DSEQ)
        sQ = early(1, 1024, 4, 32)
        sBias = early(2, 0, 2, 288)
        sS = early(2, 576, 2, 288)
        sPT = early(2, 1152, 2, 384)
        sV = early(1, 1152, P)
        vX = early(3, 0, SEQS, P)
        sMask = early(3, 1024, 2, 288)
        sSmall = early(3, 1600, 16)
        sSink = early(3, 1620, 2)
        flip = early(4, 0, P)
        onehot = early(4, 128, 384)
        lmask = early(4, 512, 384)
        line = early(4, 896, 384)
        tab = early(4, 1280, HEADS)
        sel = early(5, 0, HEADS, P)

        def scores_of(b):
            return big[:, b * 2048:(b + 1) * 2048]

        gates = big[:, 0:16 * (SAMP + GN)].rearrange("p (a b) -> p a b", a=16)
        S = [att[:, 0:1024], att[:, 1024:2048]]
        PT = att[:, 2048:3072]
        t1 = att[:, 0:4 * (HIST + GN)].rearrange("p (a b) -> p a b", a=4)
        t2 = att[:, 4 * (HIST + GN):8 * (HIST + GN)].rearrange("p (a b) -> p a b", a=4)
        ln1g, ln1b = att[:, 0:1024], att[:, 1024:2048]

        pj = [ctx.enter_context(nc.psum_tensor(f"pj{n}", [P, 512], F32)) for n in range(2)]
        acc = ctx.enter_context(nc.psum_tensor("acc", [P, D], F32))
        wide = [ctx.enter_context(nc.psum_tensor(f"wide{n}", [P, D], F32)) for n in range(2)]

        consts = sem("consts")
        bias_in = sem("bias_in")
        early_in = sem("early_in")
        built = sem("built")
        line_ps, line_sb, line_st, line_ld = sem("line_ps"), sem("line_sb"), sem("line_st"), sem("line_ld")
        bias_ps, bias_sb, sbias_ps, sbias_sb = sem("bias_ps"), sem("bias_sb"), sem("sbias_ps"), sem("sbias_sb")
        w_in_sem = [sem(f"w_tile{n}") for n in range(WR)]
        xt_in = sem("xt_in")
        xr_in = sem("xr_in")
        xs_in = sem("xs_in")
        ln1_in = sem("ln1_in")
        unit_done = sem("unit_done")
        proj_evac = sem("proj_evac")
        gate_sig = sem("gate_sig")
        pool_ready = sem("pool_ready")
        mix_done, mix_evac = sem("mix_done"), sem("mix_evac")
        score_ready, max_ready, exp_done = sem("score_ready"), sem("max_ready"), sem("exp_done")
        p_ready, pt_ready, pt_evac = sem("p_ready"), sem("pt_ready"), sem("pt_evac")
        o_ready, o_evac = sem("o_ready"), sem("o_evac")
        sq_ready, s_score, s_max, s_exp, s_p = sem("sq_ready"), sem("s_score"), sem("s_max"), sem("s_exp"), sem("s_p")
        s_pt, s_pt_evac, s_o, s_o_evac = sem("s_pt"), sem("s_pt_evac"), sem("s_o"), sem("s_o_evac")
        up_read, m_ready = sem("up_read"), sem("m_ready")
        y_read, ln1_var, ln1_std, x1_ready = sem("y_read"), sem("ln1_var"), sem("ln1_std"), sem("x1_ready")
        xt_ready, xt_evac = sem("xt_ready"), sem("xt_evac")
        qry_ready, qry_evac, sc_evac = sem("qry_ready"), sem("qry_evac"), sem("sc_evac")
        gmax_ready, gexp_done = sem("gmax_ready"), sem("gexp_done")
        cur_ready = sem("cur_ready")
        samp_ready = sem("samp_ready")
        carried = sem("carried")
        idx_ready = sem("idx_ready")
        gathered = [sem(f"gathered{n}") for n in range(RING)]
        slot_free = sem("slot_free")
        dot_done, gelu_done, w_ready, diag_done = sem("dot_done"), sem("gelu_done"), sem("w_ready"), sem("diag_done")
        acc_done, acc_read = sem("acc_done"), sem("acc_read")
        ln2_var, ln2_std, y_ready = sem("ln2_var"), sem("ln2_std"), sem("y_ready")
        y_out = [sem(f"y_out{n}") for n in range(BLK)]
        ys_out = sem("ys_out")
        states_out = sem("states_out")
        early_out = sem("early_out")

        N_CONSTS = 8

        def lo(g, width):
            return 0 if first(g) else width

        block = ctx.enter_context(nc.Block())

        @block.sync
        def _(sp):
            for dst, src in ((ident[:, :], ident_c), (iota[:, :], iota_c),
                             (sink[:, :], sinks.partition_broadcast(P)), (wmix[:, :, :], w_mix),
                             (pscale[:, :], pool_scale), (ln2g[:, :], ln2_g.partition_broadcast(P)),
                             (ln2b[:, :], ln2_b.partition_broadcast(P)), (flip, flip_c)):
                sp.dma_start(dst, src).then_inc(consts, 16)

            def load_unit(g, pos, it=0):
                before = pos - WR if pos - WR not in HOLES else pos - 2 * WR
                if before >= 0:
                    wait(sp, unit_done, g * UNITS + it * WR + (ordinal(before) + 1))
                elif not first(g):
                    wait(sp, unit_done, g * UNITS + (ordinal(before + POS_END) + 1 - UNITS))
                s = pos % WR
                if pos >= POS_QRY:
                    dst, src = wring[:, s, :], w_q[bass.ds(it * WR + (pos - POS_QRY), 1)]
                else:
                    dst, src = wring[:, s, 0:D], w_a[bass.ds(it * WR + ordinal(pos), 1)]
                sp.dma_start(dst, src.rearrange("o p f -> (o p) f")).then_inc(w_in_sem[s], 16)

            def load_loop(g, pos, n):
                if pos == POS_IN:
                    for k in range(WR):
                        load_unit(g, pos + k)
                    pos, n = pos + WR, n - WR
                with nc.sync.Fori(0, n // WR) as it:
                    for k in range(WR):
                        load_unit(g, pos + k, it)

            def load_group(g):
                wait(sp, unit_done, g * UNITS)
                if first(g):
                    sp.dma_start(xm[:, :, 0:X0], xT_extra).then_inc(xt_in, 16)
                    sp.dma_start(xm[:, :, X0:COLS], xT[0]).then_inc(xt_in, 16)
                else:
                    sp.dma_start(xm[:, :, X0:COLS],
                                 xT[bass.ds(g, 1)].rearrange("o p c n -> (o p) c n")).then_inc(xt_in, 16)
                load_unit(g, POS_K)
                load_unit(g, POS_V)
                load_loop(g, POS_IN, N_IN)
                wait(sp, cur_ready, g)
                for b in range(BLK):
                    sp.dma_start(x1n[:, b, :],
                                 x_rows[bass.ds(g * BLK + b, 1)].rearrange("o p d -> (o p) d")).then_inc(xr_in, 16)
                load_loop(g, POS_UP, N_UP)
                wait(sp, o_ready, g * 4 + 4)
                wait(sp, s_pt, 2)
                sp.dma_start(ln1g, ln1_g.partition_broadcast(P)).then_inc(ln1_in, 16)
                sp.dma_start(ln1b, ln1_b.partition_broadcast(P)).then_inc(ln1_in, 16)
                load_loop(g, POS_OUT, N_OUT)
                load_loop(g, POS_QRY, N_QRY)

            def store_pair(g):
                for b in range(BLK):
                    wait(sp, y_ready, (g - 1) * BLK + (b + 1))
                    dst = y_prompt[bass.ds((g - 1) * BLK + b, 1)].rearrange("o p d -> (o p) d")
                    sp.dma_start(dst, x1c[:, b, :]).then_inc(y_out[b], 16)

            for dst, src in ((onehot[0:32], onehot_c), (lmask[0:HEADS], linemask_c), (tab[0:32], table),
                             (sel[0:DSEQ], sel_c)):
                sp.dma_start(dst, src).then_inc(bias_in, 16)
            sp.wait_ge(line_sb, 1)
            sp.dma_start(line_scratch, line[0:HEADS]).then_inc(line_st, 16)
            sp.wait_ge(line_st, 16)
            window = bass.AP(line_scratch.tensor, 0, [[1, P], [384, HEADS], [1, 2 * P]])
            sp.dma_start(att[:, 0:2048].rearrange("p (h j) -> p h j", h=HEADS), window).then_inc(line_ld, 16)
            for s in range(SEQS):
                sp.dma_start(kX[:, s, 0:WIN], ckT[:, s, :]).then_inc(early_in, 16)
            sp.dma_start(vX, cv_rows).then_inc(early_in, 16)
            for c in range(4):
                sp.dma_start(sPool[:, c, :, 0:PSTATE], stT[:, c]).then_inc(early_in, 16)
            sp.dma_start(sMask, smask_c).then_inc(early_in, 16)
            sp.dma_start(sSink, sink_rows).then_inc(early_in, 16)
            sp.dma_start(x1s[:, :], xs_rows).then_inc(xs_in, 16)
            load_group(0)
            sp.dma_start(v_sample[:, 0:WIN - DSEQ, :], cache_v[:, DSEQ:WIN, :]).then_inc(states_out, 16)
            sp.wait_ge(proj_evac, PROJ)
            sp.dma_start(k_sample, kX[:, :, DSEQ:DSEQ + WIN]).then_inc(early_out, 16)
            for s in range(SEQS):
                sp.dma_start(v_sample[s, WIN - DSEQ:WIN, :], sV[DSEQ * s:DSEQ * s + DSEQ]).then_inc(early_out, 16)
            for c in range(4):
                sp.dma_start(pool_sample[:, c], sPool[:, c, :, DSEQ:DSEQ + PSTATE]).then_inc(early_out, 16)

            with nc.sync.Fori(1, GROUPS) as g:
                load_group(g)
                store_pair(g)
            sp.wait_ge(carried, GROUPS)
            sp.dma_start(k_prompt, kT[:, 0:P]).then_inc(states_out, 16)
            sp.dma_start(v_prompt, vR[:, 0, :]).then_inc(states_out, 16)
            sp.dma_start(pool_prompt, poolT[:, :, HIST - PSTATE:HIST]).then_inc(states_out, 16)
            store_pair(GROUPS)
            sp.wait_ge(y_ready, GROUPS * BLK + 1)
            sp.dma_start(y_sample, x1s[:, :]).then_inc(ys_out, 16)
            sp.wait_ge(states_out, 64)
            sp.wait_ge(early_out, 13 * 16)
            for b in range(BLK):
                sp.wait_ge(y_out[b], 16 * GROUPS)
            sp.wait_ge(ys_out, 16)

        @block.gpsimd
        def _(pool):
            def gather_block(n, idx, rows):
                with nc.gpsimd.Fori(0, SLOTS // BODY) as it:
                    for half in range(2):
                        nc.gpsimd.tensor_copy(idx8[half][0:rows, :], idx[:, bass.ds(it * BODY + half * RING, RING)])\
                            .then_inc(idx_ready, 1)
                        hold(pool, idx_ready, n * (SLOTS // RING) + it * 2 + (half + 1))
                        for k in range(RING):
                            hold(pool, slot_free, n * SLOTS + it * BODY + (half * RING + k + 1))
                            pool.indirect_dma_start(
                                ring[0:rows, k, :], None, uv,
                                bass.IndirectOffsetOnAxis(ap=idx8[half][0:rows, k:k + 1], axis=0))\
                                .then_inc(gathered[k], 16)

            def gather_pair(g):
                hold(pool, cur_ready, g)
                for b in range(BLK):
                    gather_block((g - 1) * BLK + b, idxc[:, b, :], P)

            pool.wait_ge(early_out, 13 * 16)
            with nc.gpsimd.Fori(1, GROUPS) as g:
                gather_pair(g)
            gather_pair(GROUPS)
            pool.wait_ge(samp_ready, 1)
            gather_block(GROUPS * BLK, idxs[:, :], SAMP)

        @block.scalar
        def _(act):
            copy = ACT.Copy

            for n in range(2):
                act.wait_ge(bias_ps, n + 1)
                nc.scalar.activation(bias[:, 4 * n:4 * n + 4, :].rearrange("p h j -> p (h j)"), wide[n][:, :], copy)\
                    .then_inc(bias_sb, 1)

            def evac(g, n, src, dst, also=()):
                act.wait_ge(unit_done, g * UNITS + (n + 1))
                for s, d in also:
                    nc.scalar.activation(d, s, copy)
                nc.scalar.activation(dst, src, copy).then_inc(proj_evac, 1)

            def exps(g, i):
                act.wait_ge(max_ready, g * 4 + (i + 1))
                for h in range(HPK):
                    s = S[i % 2][:, h * 256:(h + 1) * 256]
                    nc.scalar.activation(s, s, ACT.Exp, bias=anm[:, i % 2, h:h + 1], accum_out=aden[:, i % 2, h:h + 1])
                nc.scalar.activation(ads[:, i % 2, :], ads[:, i % 2, :], ACT.Exp).then_inc(exp_done, 1)

            def attention(g):
                for i in range(4):
                    b, kv = divmod(i, 2)
                    exps(g, i)
                    for n in range(4):
                        c = 4 * i + n
                        evac(g, 10 + c, pj[c % 2][:, lo(g, X0) + META * first(g):COLS],
                             gates[:, c, lo(g, SAMP):])
                    act.wait_ge(pt_ready, g * 4 + (i + 1))
                    wait(act, o_ready, g * 4 + i)
                    nc.scalar.activation(PT, wide[1][:, :], copy).then_inc(pt_evac, 1)
                    act.wait_ge(o_ready, g * 4 + (i + 1))
                    rows = slice(HD * kv, HD * kv + HD)
                    nc.scalar.activation(qT[rows, :, SAMP + b * P:SAMP + (b + 1) * P],
                                         wide[0][rows, 0:512].rearrange("p (c n) -> p c n", c=4), copy)\
                        .then_inc(o_evac, 1)
                if first(g):
                    sample_attention()
                nc.scalar.activation(gates[:, :, lo(g, SAMP):], gates[:, :, lo(g, SAMP):], ACT.Sigmoid)\
                    .then_inc(gate_sig, 1)

            def sample_attention():
                act.wait_ge(s_max, 1)
                for t in range(2):
                    nc.scalar.activation(sS[:, t, :], sS[:, t, :], ACT.Exp, bias=sSmall[:, 2 + t:3 + t],
                                         accum_out=sSmall[:, 4 + t:5 + t])
                nc.scalar.activation(sSmall[:, 6:8], sSmall[:, 6:8], ACT.Exp).then_inc(s_exp, 1)
                for t in range(2):
                    act.wait_ge(s_pt, t + 1)
                    nc.scalar.activation(sPT[:, t, 0:256], wide[1][:, t * 512:t * 512 + 256], copy)
                    nc.scalar.activation(sPT[0:SAMP, t, 256:384], wide[1][0:SAMP, t * 512 + 256:t * 512 + 384],
                                         copy).then_inc(s_pt_evac, 1)
                act.wait_ge(s_o, 1)
                for kv in range(2):
                    rows = slice(HD * kv, HD * kv + HD)
                    for c in range(HPK):
                        src = acc[rows, 0:P].rearrange("p (s c i) -> p s c i", s=SEQS, c=HPK)[:, :, c, :]
                        nc.scalar.activation(qT[rows, c, 0:SAMP].rearrange("p (s i) -> p s i", s=SEQS), src, copy)\
                            .then_inc(s_o_evac, 1)

            def front(g):
                if first(g):
                    act.wait_ge(early_in, 15 * 16)
                    evac(0, 0, pj[0][:, X0:COLS], kT[:, P:P + GN],
                         also=((pj[0][:, 0:META], kT[:, 0:META]),
                               (pj[0][:, META:X0].rearrange("p (s i) -> p s i", s=SEQS), kX[:, :, WIN:WIN + DSEQ])))
                    evac(0, 1, pj[1][:, 0:GN], vR[:, 1:1 + BLK, :].rearrange("p b n -> p (b n)"),
                         also=((pj[1][0:META, 384:512], vR[0:META, 0, :]), (pj[1][0:SAMP, 256:384], sV[0:SAMP])))
                else:
                    act.wait_ge(carried, g)
                    evac(g, 0, pj[0][:, X0:COLS], kT[:, P:P + GN])
                    evac(g, 1, pj[1][:, 0:GN], vR[:, 1:1 + BLK, :].rearrange("p b n -> p (b n)"))
                for c in range(4):
                    if first(g):
                        evac(0, 2 + c, pj[c % 2][:, X0:COLS], poolT[:, c, HIST:],
                             also=((pj[c % 2][:, 0:META], poolT[:, c, 0:META]),
                                   (pj[c % 2][:, META:X0].rearrange("p (s i) -> p s i", s=SEQS),
                                    sPool[:, c, :, PSTATE:])))
                    else:
                        evac(g, 2 + c, pj[c % 2][:, X0:COLS], poolT[:, c, HIST:])
                for c in range(4):
                    evac(g, 6 + c, pj[c % 2][:, META if first(g) else X0:COLS], qT[:, c, lo(g, SAMP):])
                attention(g)
                act.wait_ge(mix_done, g + 1)
                act.wait_ge(consts, 16 * N_CONSTS)
                for c, ps in enumerate((pj[0], pj[1], wide[1][:, 0:512], wide[1][:, 512:1024])):
                    nc.scalar.activation(pooled[:, c, lo(g, SAMP):], ps[:, META if first(g) else X0:COLS], copy,
                                         scale=pscale[:, c:c + 1]).then_inc(mix_evac, 1)
                for b in range(BLK + first(g)):
                    act.wait_ge(ln1_var, nth(g, b))
                    rows = P if b < BLK else SAMP
                    nc.scalar.activation(moments[0:rows, 2:3], moments[0:rows, 1:2], ACT.Sqrt).then_inc(ln1_std, 1)
                for b in range(BLK + first(g)):
                    act.wait_ge(xt_ready, nth(g, b))
                    if b < BLK:
                        nc.scalar.activation(xm[:, :, X0 + b * P:X0 + (b + 1) * P],
                                             wide[b][:, :].rearrange("p (c n) -> p c n", c=DC), copy)\
                            .then_inc(xt_evac, 1)
                    else:
                        nc.scalar.activation(xm[:, :, META:X0],
                                             acc[:, 0:DC * SAMP].rearrange("p (c n) -> p c n", c=DC), copy)\
                            .then_inc(xt_evac, 1)
                with nc.scalar.Fori(0, N_QRY // WR) as it:
                    for k in (0, 1, -1, 2, -2, 3, -3, -4):
                        if k >= 0:
                            act.wait_ge(qry_ready, g * N_QRY + it * WR + (k + 1))
                            nc.scalar.activation(qyT[:, k % 2, lo(g, SAMP):],
                                                 pj[k % 2][:, META if first(g) else X0:COLS], copy)\
                                .then_inc(qry_evac, 1)
                        else:
                            u = -k - 1
                            act.wait_ge(unit_done, g * UNITS + it * WR + (ordinal(POS_QRY) + u + 1))
                            ps = wide[u // 2][:, (u % 2) * 512:(u % 2) * 512 + 384]
                            if first(g):
                                nc.scalar.activation(big[0:SAMP, bass.ds(it * (WR * P) + (2 * 2048 + u * P), P)],
                                                     ps[0:SAMP, 256:384], copy)
                            nc.scalar.activation(big[:, bass.ds(it * (WR * P) + u * P, P)], ps[:, 0:P], copy)
                            nc.scalar.activation(big[:, bass.ds(it * (WR * P) + (2048 + u * P), P)], ps[:, P:2 * P],
                                                 copy).then_inc(sc_evac, 1)
                for b in range(BLK + first(g)):
                    act.wait_ge(gmax_ready, nth(g, b))
                    rows = P if b < BLK else SAMP
                    dst = gaten[:, b, :] if b < BLK else gates_s[:, :]
                    nc.scalar.activation(dst, dst, ACT.Exp).then_inc(gexp_done, 1)

            def peer_block(n, rows):
                with nc.scalar.Fori(0, SLOTS // BODY) as it:
                    for m in range(BODY // BATCH):
                        act.wait_ge(dot_done, n * SLOTS + it * BODY + BATCH * (m + 1))
                        nc.scalar.activation(hgelu[0:rows, m % 2, :], hdot[0:rows, m % 2, :], ACT.Gelu)\
                            .then_inc(gelu_done, 1)
                        act.wait_ge(w_ready, n * (SLOTS // BATCH) + it * (BODY // BATCH) + (m + 1))
                        for j in range(BATCH):
                            k = m * BATCH + j
                            act.wait_ge(slot_free, n * SLOTS + it * BODY + (k + 1))
                            nc.scalar.activation(diag[0:rows, k % RING, 0:rows], ident[0:rows, 0:rows], copy,
                                                 scale=hw[0:rows, m % 2, j:j + 1]).then_inc(diag_done, 1)
                act.wait_ge(ln2_var, n + 1)
                nc.scalar.activation(moments2[0:rows, 2:3], moments2[0:rows, 1:2], ACT.Sqrt).then_inc(ln2_std, 1)

            def peer_pair(g):
                for b in range(BLK):
                    peer_block((g - 1) * BLK + b, P)

            front(0)
            with nc.scalar.Fori(1, GROUPS) as g:
                peer_pair(g)
                front(g)
            peer_pair(GROUPS)
            peer_block(GROUPS * BLK, SAMP)

        @block.tensor
        def _(pe):
            mm = nc.tensor.matmul

            def unit_in(g, pos, it=None):
                s = pos % WR
                v = g * (16 * LOADS[s]) + 16 * loads_upto(pos)
                pe.wait_ge(w_in_sem[s], v if it is None else v + it * 16)
                return wring[:, s, 0:D].rearrange("p (c n) -> p c n", c=DC)

            def chunk(g, pos, ps, c0, need=None, it=None):
                w = unit_in(g, pos, it)
                for c in range(DC):
                    m = mm(ps[:, c0:COLS], w[:, c, :], xm[:, c, c0:COLS], start=(c == 0), stop=(c == DC - 1))
                return m

            def position_bias():
                pe.wait_ge(bias_in, 4 * 16)
                mm(acc[0:HEADS, 0:384], tab[0:32], onehot[0:32], start=True, stop=True).then_inc(line_ps, 1)
                pe.wait_ge(consts, 16 * N_CONSTS)
                pe.wait_ge(line_ld, 16)
                for n in range(4):
                    m = mm(wide[n // 2][:, (n % 2) * 512:(n % 2) * 512 + 512], flip, att[:, n * 512:(n + 1) * 512],
                           start=True, stop=True)
                    if n % 2:
                        m.then_inc(bias_ps, 1)
                pe.wait_ge(bias_sb, 2)
                for h in range(HEADS):
                    m = mm(acc[:, 512:512 + WIN + DSEQ], sel[0:DSEQ, h, :], bias[0:DSEQ, h, 0:WIN + DSEQ],
                           start=(h == 0), stop=(h == HEADS - 1))
                m.then_inc(sbias_ps, 1)

            def attention(g):
                for i in range(4):
                    b, kv = divmod(i, 2)
                    rows = slice(HD * kv, HD * kv + HD)
                    if i == 0:
                        pe.wait_ge(proj_evac, g * PROJ + 10)
                        wait(pe, sc_evac, g * N_QRY)
                    else:
                        pe.wait_ge(o_evac, g * 4 + i)
                    for c in range(HPK):
                        m = mm(wide[0][:, c * 256:(c + 1) * 256], qT[rows, c, SAMP + b * P:SAMP + (b + 1) * P],
                               kT[rows, b * P:b * P + 2 * P], start=True, stop=True)
                    m.then_inc(score_ready, 1)
                    for n in range(4):
                        c = 4 * i + n
                        pe.wait_ge(proj_evac, g * PROJ + (10 + c - 1))
                        chunk(g, POS_IN + 8 + c, pj[c % 2], META if first(g) else X0).then_inc(unit_done, 1)
                    pe.wait_ge(p_ready, g * 4 + (i + 1))
                    if i:
                        pe.wait_ge(pt_evac, g * 4 + i)
                    for half in range(2):
                        for c in range(HPK):
                            at = half * 512 + c * P
                            m = mm(wide[1][:, at:at + P], S[i % 2][:, c * 256 + half * P:c * 256 + half * P + P],
                                   ident[:, :], is_transpose=True, start=True, stop=True)
                    m.then_inc(pt_ready, 1)
                    pe.wait_ge(pt_evac, g * 4 + (i + 1))
                    for half in range(2):
                        m = mm(wide[0][rows, 0:512], vR[:, b + half, HD * kv:HD * kv + HD],
                               PT[:, half * 512:half * 512 + 512], start=(half == 0), stop=(half == 1))
                    m.then_inc(o_ready, 1)

            def sample_attention():
                pe.wait_ge(sq_ready, 1)
                pe.wait_ge(o_evac, 4)
                for t in range(2):
                    for q in range(4):
                        pair, kv = 2 * t + q // 2, q % 2
                        rows = slice(HD * kv, HD * kv + HD)
                        out = wide[0][32 * q:32 * q + 32, t * 512:t * 512 + 288]
                        for n in range(2):
                            mm(out[:, n * WIN:(n + 1) * WIN], sQ[rows, pair, :], kX[rows, 2 * pair + n, 0:WIN],
                               start=True, stop=True)
                        m = mm(out[:, 256:288], sQ[rows, pair, :], kX[rows, :, WIN:], start=True, stop=True)
                m.then_inc(s_score, 1)
                pe.wait_ge(s_p, 1)
                pe.wait_ge(pt_evac, 4)
                for t in range(2):
                    for n in range(2):
                        mm(wide[1][:, t * 512 + n * P:t * 512 + (n + 1) * P], sS[:, t, n * P:(n + 1) * P],
                           ident[:, :], is_transpose=True, start=True, stop=True)
                    mm(wide[1][0:SAMP, t * 512 + 256:t * 512 + 384], sS[:, t, 256:288], ident[:, :],
                       is_transpose=True, start=True, stop=True).then_inc(s_pt, 1)
                pe.wait_ge(s_pt_evac, 2)
                for pair in range(4):
                    for kv in range(2):
                        t, q = pair // 2, 2 * (pair % 2) + kv
                        rows = slice(HD * kv, HD * kv + HD)
                        out = acc[rows, pair * 32:pair * 32 + 32]
                        for n in range(2):
                            mm(out, vX[:, 2 * pair + n, HD * kv:HD * kv + HD],
                               sPT[:, t, n * P + 32 * q:n * P + 32 * q + 32], start=(n == 0), stop=False)
                        m = mm(out, sV[0:SAMP, HD * kv:HD * kv + HD], sPT[0:SAMP, t, 256 + 32 * q:256 + 32 * q + 32],
                               start=False, stop=True)
                m.then_inc(s_o, 1)

            def front(g):
                pe.wait_ge(xt_in, 32 if first(g) else g * 16 + 32)
                wait(pe, qry_evac, g * N_QRY)
                chunk(g, POS_K, pj[0], lo(g, X0)).then_inc(unit_done, 1)
                w = unit_in(g, POS_V)
                parts = [(pj[1][:, b * P:(b + 1) * P], X0 + b * P, X0 + (b + 1) * P) for b in range(BLK)]
                if first(g):
                    parts += [(pj[1][0:SAMP, 256:384], META, X0), (pj[1][0:META, 384:512], 0, META)]
                for out, a, z in parts:
                    for c in range(DC):
                        m = mm(out, xm[:, c, a:z], w[:, c, :], start=(c == 0), stop=(c == DC - 1))
                m.then_inc(unit_done, 1)
                for n in range(8):
                    pe.wait_ge(proj_evac, g * PROJ + (n + 1))
                    chunk(g, POS_IN + n, pj[n % 2], (0 if n < 4 else META) if first(g) else X0).then_inc(unit_done, 1)
                attention(g)
                if first(g):
                    sample_attention()
                c0 = META if first(g) else X0
                pe.wait_ge(pool_ready, g + 1)
                pe.wait_ge(proj_evac, g * PROJ + PROJ)
                pe.wait_ge(pt_evac, g * 4 + 4)
                for c, ps in enumerate((pj[0], pj[1], wide[1][:, 0:512], wide[1][:, 512:1024])):
                    m = mm(ps[:, c0:COLS], wmix[:, c, :], pooled[:, c, lo(g, SAMP):], start=True, stop=True)
                m.then_inc(mix_done, 1)
                pe.wait_ge(mix_evac, g * 4 + 4)
                hold(pe, o_evac, g * 4 + 4)
                if first(g):
                    pe.wait_ge(s_o_evac, 8)
                with nc.tensor.Fori(0, N_UP // WR) as it:
                    for k in range(WR):
                        w = unit_in(g, POS_UP + k, it)
                        if first(g):
                            pe.wait_ge(up_read, it * WR + (k + 1))
                        else:
                            pe.wait_ge(up_read, g * N_UP + it * WR + (k + 1))
                        pa, pb = (pj[0], pj[1]) if k % 2 == 0 else (wide[1][:, 0:512], wide[1][:, 512:1024])
                        for ps, w0, src in ((pa, 0, pooled), (pb, 4, qT)):
                            for c in range(4):
                                m = mm(ps[:, c0:COLS], w[:, w0 + c, :], src[:, c, lo(g, SAMP):],
                                       start=(c == 0), stop=(c == 3))
                        m.then_inc(unit_done, 1)
                hold(pe, m_ready, g * N_UP + N_UP)
                with nc.tensor.Fori(0, 2) as it:
                    for k in range(WR):
                        s = (POS_OUT + k) % WR
                        unit_in(g, POS_OUT + k, it)
                        w = wring[:, s, 0:D].rearrange("p (c n) -> p c n", c=4)
                        for b in range(BLK + first(g)):
                            full = wide[b] if b < BLK else acc
                            rows = P if b < BLK else SAMP
                            a = X0 + b * P if b < BLK else META
                            out = full[0:rows, bass.ds(it * 512 + (k // 2) * 256, 256)]
                            for c in range(4):
                                m = mm(out, xm[:, (k % 2) * 4 + c, a:a + rows], w[:, c, :],
                                       start=(k % 2 == 0 and c == 0), stop=(k % 2 == 1 and c == 3))
                        m.then_inc(unit_done, 1)
                for b in range(BLK + first(g)):
                    pe.wait_ge(x1_ready, nth(g, b))
                    for c in range(DC):
                        if b < BLK:
                            m = mm(wide[b][:, c * P:(c + 1) * P], x1n[:, b, c * P:(c + 1) * P], ident[:, :],
                                   is_transpose=True, start=True, stop=True)
                        else:
                            m = mm(acc[:, c * SAMP:(c + 1) * SAMP], x1s[:, c * P:(c + 1) * P],
                                   ident[0:SAMP, 0:SAMP], is_transpose=True, start=True, stop=True)
                    m.then_inc(xt_ready, 1)
                hold(pe, xt_evac, nth(g, BLK - 1) + first(g))
                with nc.tensor.Fori(0, N_QRY // WR) as it:
                    for k in (0, 1, -1, 2, -2, 3, -3, -4):
                        if k >= 0:
                            if k >= 2:
                                pe.wait_ge(qry_evac, g * N_QRY + it * WR + (k - 1))
                            else:
                                wait(pe, qry_evac, g * N_QRY + it * WR)
                            chunk(g, POS_QRY + k, pj[k % 2], c0, it=it).then_inc(qry_ready, 1)
                        else:
                            u = -k - 1
                            pe.wait_ge(qry_evac, g * N_QRY + it * WR + (u + 1))
                            wait(pe, sc_evac, g * N_QRY + it * WR)
                            keys = wring[:, u, D:D + P]
                            ps = wide[u // 2][:, (u % 2) * 512:(u % 2) * 512 + 384]
                            for b in range(BLK):
                                m = mm(ps[:, b * P:(b + 1) * P], qyT[:, u % 2, SAMP + b * P:SAMP + (b + 1) * P],
                                       keys, start=True, stop=True)
                            if first(g):
                                m = mm(ps[0:SAMP, 256:384], qyT[:, u % 2, 0:SAMP], keys, start=True, stop=True)
                            m.then_inc(unit_done, 1)

            def peer_block(n, x, rows):
                pe.wait_ge(acc_read, n + 1)
                for c in range(2):
                    mm(acc[0:rows, c * 512:(c + 1) * 512], alpha_i[0:rows, 0:rows], x[:, c * 512:(c + 1) * 512],
                       start=True, stop=False)
                with nc.tensor.Fori(0, SLOTS // BODY) as it:
                    for k in range(BODY):
                        (pe.wait_ge if rows == P else partial(hold, pe))(diag_done, n * SLOTS + it * BODY + (k + 1))
                        for c in range(2):
                            m = mm(acc[0:rows, c * 512:(c + 1) * 512], diag[0:rows, k % RING, 0:rows],
                                   ring[0:rows, k % RING, D + c * 512:D + (c + 1) * 512], start=False, stop=False)
                        m.then_inc(slot_free, 1)
                for c in range(2):
                    m = mm(acc[0:rows, c * 512:(c + 1) * 512], zeros[0:rows, 0:rows], x[:, c * 512:(c + 1) * 512],
                           start=False, stop=True)
                m.then_inc(acc_done, 1)

            def peer_pair(g):
                pe.wait_ge(cur_ready, g)
                for b in range(BLK):
                    peer_block((g - 1) * BLK + b, x1c[:, b, :], P)

            pe.wait_ge(built, 1)
            position_bias()
            pe.wait_ge(sbias_sb, 1)
            front(0)
            pe.sem_inc(slot_free, RING)
            with nc.tensor.Fori(1, GROUPS) as g:
                peer_pair(g)
                front(g)
            peer_pair(GROUPS)
            pe.wait_ge(samp_ready, 1)
            peer_block(GROUPS * BLK, x1s[:, :], SAMP)

        @block.vector
        def _(dve):
            V = nc.vector

            def fence():
                dve.drain()

            def setup():
                V.memset(zeros[:, :], 0.0)
                V.memset(kT[:, 0:P], 0.0)
                V.memset(vR[:, 0, :], 0.0)
                dve.wait_ge(consts, 16 * N_CONSTS)
                V.tensor_scalar(alpha_i[:, :], ident[:, :], ALPHA, None, ALU.mult).then_inc(built, 1)
                dve.wait_ge(line_ps, 1)
                V.tensor_tensor(line[0:HEADS], acc[0:HEADS, 0:384], lmask[0:HEADS], ALU.add).then_inc(line_sb, 1)
                dve.wait_ge(early_in, 15 * 16)
                dve.wait_ge(sbias_ps, 1)
                for t in range(2):
                    for n in range(2):
                        V.tensor_tensor(sBias[:, t, n * WIN:(n + 1) * WIN], acc[:, 512:512 + WIN],
                                        sMask[:, t, n * WIN:(n + 1) * WIN], ALU.add)
                    m = V.tensor_tensor(sBias[:, t, 256:288].rearrange("p (s i) -> p s i", s=SEQS),
                                        acc[:, 512 + WIN:512 + WIN + DSEQ].unsqueeze(1).to_broadcast([P, SEQS, DSEQ]),
                                        sMask[:, t, 256:288].rearrange("p (s i) -> p s i", s=SEQS), ALU.add)
                m.then_inc(sbias_sb, 1)

            def pool_windows(g):
                dve.wait_ge(proj_evac, g * PROJ + 6)
                n = HIST + GN
                if not first(g):
                    dve.wait_ge(mix_done, g)
                src, dst = poolT, t1
                for c in range(4):
                    w = 2 ** c
                    V.tensor_tensor(dst[:, c:, 2 * w - 1:n], src[:, c:, 2 * w - 1:n], src[:, c:, w - 1:n - w], ALU.add)
                    fence()
                    V.scalar_tensor_tensor(pooled[:, c, SAMP:], dst[:, c, HIST:n], 1.0 / (2 * w), poolT[:, c, HIST:n],
                                           ALU.mult, ALU.subtract)
                    src, dst = dst, (t2 if dst is t1 else t1)
                    fence()
                if first(g):
                    e = PSTATE + DSEQ
                    for c in range(4):
                        src, dst = sPool[:, c], sT1
                        for k in range(c + 1):
                            w = 2 ** k
                            V.tensor_tensor(dst[:, :, 2 * w - 1:e], src[:, :, 2 * w - 1:e], src[:, :, w - 1:e - w],
                                            ALU.add)
                            fence()
                            src, dst = dst, (sT2 if dst is sT1 else sT1)
                        V.scalar_tensor_tensor(pooled[:, c, 0:SAMP].rearrange("p (s i) -> p s i", s=SEQS),
                                               src[:, :, PSTATE:e], 1.0 / 2 ** (c + 1), sPool[:, c, :, PSTATE:e],
                                               ALU.mult, ALU.subtract)
                        fence()
                V.tensor_copy(poolT[:, :, 0:HIST], poolT[:, :, GN:GN + HIST]).then_inc(pool_ready, 1)

            def attention(g):
                for i in range(4):
                    b, kv = divmod(i, 2)
                    s = S[i % 2]
                    bi = bias[:, 4 * kv:4 * kv + 4, :].rearrange("p h j -> p (h j)")
                    dve.wait_ge(score_ready, g * 4 + (i + 1))
                    if i >= 2:
                        dve.wait_ge(pt_ready, g * 4 + (i - 1))
                    if first(g) and b == 0:
                        s4 = s.rearrange("p (h j) -> p h j", h=HPK)
                        r4 = wide[0][:, :].rearrange("p (h j) -> p h j", h=HPK)
                        b4 = bias[:, 4 * kv:4 * kv + 4, :]
                        V.memset(s4[:, :, META:P], NEG)
                        V.scalar_tensor_tensor(s4[:, :, 0:META], r4[:, :, 0:META], SCALE, b4[:, :, P - META:P],
                                               ALU.mult, ALU.add)
                        V.scalar_tensor_tensor(s4[:, :, P:], r4[:, :, P:], SCALE, b4[:, :, P:], ALU.mult, ALU.add)
                    else:
                        V.scalar_tensor_tensor(s, wide[0][:, :], SCALE, bi, ALU.mult, ALU.add)
                    fence()
                    mx, nm, sk, den = amx[:, i % 2, :], anm[:, i % 2, :], ads[:, i % 2, :], aden[:, i % 2, :]
                    V.tensor_reduce(mx, s.rearrange("p (h j) -> p h j", h=HPK), AX.X, ALU.max)
                    fence()
                    V.tensor_tensor(mx, mx, sink[:, 4 * kv:4 * kv + 4], ALU.max)
                    fence()
                    V.tensor_scalar(nm, mx, -1.0, None, ALU.mult)
                    V.tensor_tensor(sk, sink[:, 4 * kv:4 * kv + 4], mx, ALU.subtract).then_inc(max_ready, 1)
                    dve.wait_ge(exp_done, g * 4 + (i + 1))
                    V.tensor_tensor(den, den, sk, ALU.add)
                    fence()
                    V.reciprocal(den, den)
                    fence()
                    V.tensor_tensor(s.rearrange("p (h j) -> p h j", h=HPK), s.rearrange("p (h j) -> p h j", h=HPK),
                                    den.unsqueeze(2).to_broadcast([P, HPK, 256]), ALU.mult).then_inc(p_ready, 1)

            def sample_attention():
                for s in range(SEQS):
                    m = V.tensor_copy(sQ[:, s // 2, 16 * (s % 2):16 * (s % 2) + 16].rearrange("p (c i) -> p c i", c=HPK),
                                      qT[:, :, DSEQ * s:DSEQ * s + DSEQ])
                m.then_inc(sq_ready, 1)
                mx, nm, den, sk = sSmall[:, 0:2], sSmall[:, 2:4], sSmall[:, 4:6], sSmall[:, 6:8]
                dve.wait_ge(s_score, 1)
                for t in range(2):
                    V.scalar_tensor_tensor(sS[:, t, :], wide[0][:, t * 512:t * 512 + 288], SCALE, sBias[:, t, :],
                                           ALU.mult, ALU.add)
                fence()
                V.tensor_reduce(mx, sS, AX.X, ALU.max)
                fence()
                V.tensor_tensor(mx, mx, sSink, ALU.max)
                fence()
                V.tensor_scalar(nm, mx, -1.0, None, ALU.mult)
                V.tensor_tensor(sk, sSink, mx, ALU.subtract).then_inc(s_max, 1)
                dve.wait_ge(s_exp, 1)
                V.tensor_tensor(den, den, sk, ALU.add)
                fence()
                V.reciprocal(den, den)
                fence()
                V.tensor_tensor(sS, sS, den.unsqueeze(2).to_broadcast([P, 2, 288]), ALU.mult).then_inc(s_p, 1)

            def merge(g):
                dve.wait_ge(gate_sig, g + 1)
                c0 = META if first(g) else X0
                l0 = lo(g, SAMP)
                for j in range(N_UP):
                    dve.wait_ge(unit_done, g * UNITS + (ordinal(POS_UP) + j + 1))
                    pa, pb = (pj[0], pj[1]) if j % 2 == 0 else (wide[1][:, 0:512], wide[1][:, 512:1024])
                    V.tensor_tensor(gates[:, j, l0:], gates[:, j, l0:], pa[:, c0:COLS], ALU.mult)
                    V.tensor_tensor(gates[:, 8 + j, l0:], gates[:, 8 + j, l0:], pb[:, c0:COLS], ALU.mult)\
                        .then_inc(up_read, 1)
                    fence()
                    V.tensor_tensor(xm[:, j, c0:COLS], gates[:, j, l0:], gates[:, 8 + j, l0:], ALU.add)\
                        .then_inc(m_ready, 1)

            def normalise(out, src, g_, b_, mom, st, var_sem, std_sem, count, read=None):
                rows = out.shape[0]
                V.bn_stats(st[0:rows, 0:6], src[:, 0:512])
                V.bn_stats(st[0:rows, 6:12], src[:, 512:1024])
                fence()
                V.bn_aggr(mom[0:rows, 0:2], st[0:rows, :])
                fence()
                V.tensor_scalar(mom[0:rows, 1:2], mom[0:rows, 1:2], EPS, None, ALU.add).then_inc(var_sem, 1)
                dve.wait_ge(std_sem, count)
                V.reciprocal(mom[0:rows, 3:4], mom[0:rows, 2:3])
                fence()
                m = V.tensor_scalar(out, src, mom[0:rows, 0:1], mom[0:rows, 3:4], ALU.subtract, ALU.mult)
                if read is not None:
                    m.then_inc(read, 1)
                fence()
                V.tensor_tensor(out, out, g_[0:rows], ALU.mult)
                fence()
                return V.tensor_tensor(out, out, b_[0:rows], ALU.add)

            def norm1(g):
                dve.wait_ge(unit_done, g * UNITS + (ordinal(POS_OUT) + N_OUT))
                dve.wait_ge(ln1_in, g * 32 + 32)
                dve.wait_ge(xr_in, g * 32 + 32)
                for b in range(BLK + first(g)):
                    x = x1n[:, b, :] if b < BLK else x1s[:, :]
                    y = wide[b][:, :] if b < BLK else acc[0:SAMP, :]
                    if b == BLK:
                        dve.wait_ge(xs_in, 16)
                    V.scalar_tensor_tensor(x, x, ALPHA, y, ALU.mult, ALU.add)
                    fence()
                    normalise(x, x, ln1g, ln1b, moments, stats, ln1_var, ln1_std, nth(g, b)).then_inc(x1_ready, 1)

            def top16(top, idx, vals):
                sets = range(len(vals))
                for half in range(2):
                    h8 = slice(8 * half, 8 * half + 8)
                    for n in sets:
                        V.max(top[n][:, h8], vals[n])
                    fence()
                    for n in sets:
                        V.max_index(idx[n][:, h8], top[n][:, h8], vals[n])
                    fence()
                    if half == 0:
                        for n in sets:
                            V.match_replace(vals[n], top[n][:, h8], vals[n], NEG)
                        fence()

            def retrieve(g, b):
                rows = P if b < BLK else SAMP
                sc = scores_of(b)[0:rows]
                idx = idxn[:, b, :] if b < BLK else idxs[:, :]
                gate = gaten[:, b, :] if b < BLK else gates_s[:, :]
                top16([tops[0:rows, h, c, :] for h in range(HEADS) for c in range(2)],
                      [topi[0:rows, h, c, :] for h in range(HEADS) for c in range(2)],
                      [sc[:, n * P:(n + 1) * P] for n in range(2 * HEADS)])
                V.tensor_copy(topf[0:rows], topi[0:rows])
                for h in range(HEADS):
                    V.tensor_tensor(sc[:, h * 256:(h + 1) * 256].rearrange("p (a c) -> p a c", a=TOPK),
                                    tops[0:rows, h, 0, :].unsqueeze(2).to_broadcast([rows, TOPK, TOPK]),
                                    tops[0:rows, h, 1, :].unsqueeze(1).to_broadcast([rows, TOPK, TOPK]), ALU.add)
                fence()
                top16([bests[0:rows, h, :] for h in range(HEADS)], [bestj[0:rows, h, :] for h in range(HEADS)],
                      [sc[:, h * 256:(h + 1) * 256] for h in range(HEADS)])
                hot = sc.rearrange("p (m a) -> p m a", a=TOPK)
                hot4 = sc.rearrange("p (h k a) -> p h k a", h=HEADS, k=TOPK)
                for c in range(2):
                    flat = bestj[0:rows].rearrange("p h k -> p (h k)")
                    if c == 0:
                        V.tensor_scalar(jpart[0:rows], flat, 4, None, ALU.logical_shift_right)
                    else:
                        V.tensor_scalar(jpart[0:rows], flat, 15, None, ALU.bitwise_and)
                    fence()
                    V.tensor_copy(jf[0:rows], jpart[0:rows])
                    fence()
                    V.tensor_tensor(hot, jf[0:rows].unsqueeze(2).to_broadcast([rows, SLOTS, TOPK]),
                                    iota[0:rows].unsqueeze(1).to_broadcast([rows, SLOTS, TOPK]), ALU.is_equal)
                    fence()
                    V.tensor_tensor(hot4, hot4, topf[0:rows, :, c, :].unsqueeze(2)
                                    .to_broadcast([rows, HEADS, TOPK, TOPK]), ALU.mult)
                    fence()
                    V.tensor_reduce(ipart[0:rows, c, :], hot, AX.X, ALU.add)
                    fence()
                V.scalar_tensor_tensor(idx, ipart[0:rows, 0, :], float(P), ipart[0:rows, 1, :], ALU.mult, ALU.add)
                gate3 = gate.rearrange("p (h k) -> p h k", h=HEADS)
                V.tensor_tensor(gate3, bests[0:rows], bests[0:rows, :, 0:1].to_broadcast([rows, HEADS, TOPK]),
                                ALU.subtract).then_inc(gmax_ready, 1)
                dve.wait_ge(gexp_done, nth(g, b))
                V.tensor_reduce(gsum[0:rows], gate3, AX.X, ALU.add)
                fence()
                V.reciprocal(gsum[0:rows], gsum[0:rows])
                fence()
                return V.tensor_tensor(gate3, gate3, gsum[0:rows].unsqueeze(2).to_broadcast([rows, HEADS, TOPK]),
                                       ALU.mult)

            def front(g):
                pool_windows(g)
                attention(g)
                if first(g):
                    sample_attention()
                merge(g)
                dve.wait_ge(o_ready, g * 4 + 4)
                V.tensor_copy(kT[:, 0:P], kT[:, GN:GN + P])
                V.tensor_copy(vR[:, 0, :], vR[:, BLK, :]).then_inc(carried, 1)
                norm1(g)
                hold(dve, sc_evac, g * N_QRY + N_QRY)
                for b in range(BLK):
                    retrieve(g, b)
                    fence()
                if first(g):
                    retrieve(g, BLK).then_inc(samp_ready, 1)

            def hand_over(g):
                for b in range(BLK):
                    wait(dve, y_out[b], g * 16)
                hold(dve, unit_done, g * UNITS + UNITS)
                fence()
                V.tensor_copy(idxc[:, :, :], idxn[:, :, :])
                V.tensor_copy(gatec[:, :, :], gaten[:, :, :])
                V.tensor_copy(x1c[:, :, :], x1n[:, :, :]).then_inc(cur_ready, 1)

            def peer_block(n, x, gate, rows):
                with V.Fori(0, SLOTS // BODY) as it:
                    for m in range(BODY // BATCH):
                        for j in range(BATCH):
                            k = m * BATCH + j
                            u = ring[0:rows, k % RING, 0:D]
                            dve.wait_ge(gathered[k % RING],
                                        n * (16 * SLOTS // RING) + it * 32 + 16 * (k // RING + 1))
                            V.tensor_tensor_reduce(u, u, x, 1.0, 0.0, ALU.mult, ALU.add,
                                                   hdot[0:rows, m % 2, j:j + 1]).then_inc(dot_done, 1)
                        dve.wait_ge(gelu_done, n * (SLOTS // BATCH) + it * (BODY // BATCH) + (m + 1))
                        V.tensor_tensor(hw[0:rows, m % 2, :], hgelu[0:rows, m % 2, :],
                                        gate[:, bass.ds(it * BODY + m * BATCH, BATCH)], ALU.mult).then_inc(w_ready, 1)
                dve.wait_ge(acc_done, n + 1)
                normalise(x, acc[0:rows, :], ln2g, ln2b, moments2, stats2, ln2_var, ln2_std, n + 1, read=acc_read)\
                    .then_inc(y_ready, 1)

            def peer_pair(g):
                fence()
                for b in range(BLK):
                    peer_block((g - 1) * BLK + b, x1c[:, b, :], gatec[:, b, :], P)

            setup()
            dve.nop(nofuse=True).then_inc(up_read, 2)
            front(0)
            dve.nop(nofuse=True).then_inc(acc_read, 1)
            hand_over(0)
            with V.Fori(1, GROUPS) as g:
                peer_pair(g)
                front(g)
                hand_over(g)
            peer_pair(GROUPS)
            peer_block(GROUPS * BLK, x1s[:, :], gates_s[:, :], SAMP)


def kernel(**inputs):
    import numpy as np
    import concourse.bacc as bacc
    from concourse.bass_utils import run_bass_kernel_spmd

    a = {k: np.asarray(v) for k, v in inputs.items()}

    w_in = a["w_in"][0]
    def cols(w):
        return np.ascontiguousarray(w.reshape(DC, P, P).transpose(1, 0, 2)).reshape(P, D)
    wq = w_in[:, 512:1024].reshape(D, 2, HPK, HD).transpose(0, 2, 1, 3).reshape(D, 512)
    units = [cols(w_in[:, 1024:1152]), cols(w_in[:, 1152:1280])]
    units += [cols(w_in[:, n * P:(n + 1) * P]) for n in range(4)]
    units += [cols(wq[:, n * P:(n + 1) * P]) for n in range(4)]
    units += [cols(w_in[:, 1280 + n * P:1280 + (n + 1) * P]) for n in range(16)]
    up_p = a["w_up_pool"][0].reshape(4, P, DC, P)
    up_a = a["w_up_attn"][0].reshape(2, HPK, HD, D).transpose(1, 0, 2, 3).reshape(4, P, DC, P)
    both = np.concatenate([up_p, up_a], axis=0)
    units += [both[:, :, j].transpose(1, 0, 2).reshape(P, D) for j in range(DC)]
    wo = a["w_out"][0].reshape(2, 4, P, 4, 256)
    units += [wo[h, :, :, q].transpose(1, 0, 2).reshape(P, D) for q in range(4) for h in range(2)]
    w_a = np.ascontiguousarray(np.stack(units))
    wqry = a["peer_w_query"][0]
    keys = a["peer_sub_keys"][0].reshape(2 * HEADS, P, P)
    w_q = np.stack([np.concatenate([cols(wqry[:, n * P:(n + 1) * P]), keys[n].T], axis=1) for n in range(16)])

    x = a["x_prompt"][0]
    xT = x.reshape(GROUPS, GN, DC, P).transpose(0, 3, 2, 1)
    xs = a["x_sample"].reshape(SAMP, D)
    extra = np.concatenate([a["meta_tokens"], xs], axis=0).reshape(X0, DC, P).transpose(2, 1, 0)
    sinks = a["attn_sinks"][0]
    sink_rows = np.broadcast_to(sinks.reshape(1, 2, 1, HPK, 1, 1), (2, 2, 2, HPK, DSEQ, 2)).reshape(P, 2)

    dist = 255 - np.arange(384)
    n = np.maximum(dist, 0)
    large = 16 + (np.log(np.maximum(n, 16).astype(np.float32) / 16) / np.log(8.0) * 16).astype(np.int32)
    bucket = np.where(n < 16, n, np.minimum(large, 31))
    inside = (dist >= 0) & (dist < WIN)
    onehot = ((np.arange(32)[:, None] == bucket[None, :]) & inside[None, :]).astype(np.float32)
    linemask = np.broadcast_to(np.where(inside, 0.0, NEG).astype(np.float32), (HEADS, 384))
    sel = np.zeros((DSEQ, HEADS, P), np.float32)
    smask = np.full((P, 2, 288), NEG, np.float32)
    for pr in range(2):
        for kv in range(2):
            for s in range(2):
                for h in range(HPK):
                    for i in range(DSEQ):
                        r = pr * 64 + kv * 32 + s * 16 + h * 4 + i
                        sel[i, kv * HPK + h, r] = 1.0
                        for t in range(2):
                            smask[r, t, s * WIN:(s + 1) * WIN] = 0.0
                            q = 2 * (2 * t + pr) + s
                            smask[r, t, 256 + q * DSEQ:256 + (q + 1) * DSEQ] = 0.0

    arrays = {
        "xT": xT, "xT_extra": extra, "x_rows": x.reshape(GROUPS * BLK, P, D), "xs_rows": xs, "w_a": w_a, "w_q": w_q,
        "uv": np.concatenate([a["peer_u"][0], a["peer_v"][0]], axis=1), "table": a["rel_bias_table"],
        "sinks": sinks, "sink_rows": sink_rows,
        "w_mix": a["w_pool_mix"][0].transpose(1, 0, 2), "pool_scale": a["pool_scale"][0].reshape(4, P).T,
        "ln1_g": a["ln1_g"][0], "ln1_b": a["ln1_b"][0], "ln2_g": a["ln2_g"][0], "ln2_b": a["ln2_b"][0],
        "ckT": a["cache_k"][0].reshape(SEQS, WIN, P).transpose(2, 0, 1),
        "cv_rows": a["cache_v"][0].reshape(SEQS, WIN, P).transpose(1, 0, 2),
        "cache_v": a["cache_v"][0].reshape(SEQS, WIN, P),
        "stT": a["state_pool"][0].reshape(SEQS, PSTATE, 4, P).transpose(3, 2, 0, 1),
        "ident": np.eye(P, dtype=np.float32), "flip": np.eye(P, dtype=np.float32)[::-1], "onehot": onehot,
        "linemask": linemask, "sel": sel, "smask": smask,
        "iota": np.broadcast_to(np.arange(TOPK, dtype=np.float32), (P, TOPK)),
    }
    outs = {"y_prompt": (GROUPS * BLK, P, D), "y_sample": (SAMP, D), "k_prompt": (P, P), "v_prompt": (P, P),
            "pool_prompt": (P, 4, PSTATE), "k_sample": (P, SEQS, WIN), "v_sample": (SEQS, WIN, P),
            "pool_sample": (P, 4, SEQS, PSTATE)}
    nc = bacc.Bacc("TRN2", target_bir_lowering=False, num_devices=1)
    data = {"in_" + k: np.ascontiguousarray(v) for k, v in arrays.items()}
    args = [nc.dram_tensor(k, v.shape, mybir.dt.from_np(v.dtype), kind="ExternalInput").ap() for k, v in data.items()]
    args.append(nc.dram_tensor("line_scratch", (HEADS, 384), F32, kind="Internal").ap())
    args += [nc.dram_tensor("out_" + k, s, F32, kind="ExternalOutput").ap() for k, s in outs.items()]
    layer_kernel(nc, *args)
    r = run_bass_kernel_spmd(nc, [data], core_ids=[0]).results[0]
    o = {k: r["out_" + k] for k in outs}
    return (o["y_prompt"].reshape(1, GROUPS * GN, D), o["y_sample"].reshape(SEQS, DSEQ, D),
            np.ascontiguousarray(o["k_prompt"].T).reshape(1, 1, P, 2, HD), o["v_prompt"].reshape(1, 1, P, 2, HD),
            np.ascontiguousarray(o["pool_prompt"].transpose(2, 1, 0)).reshape(1, 1, PSTATE, 512),
            np.ascontiguousarray(o["k_sample"].transpose(1, 2, 0)).reshape(1, SEQS, WIN, 2, HD),
            o["v_sample"].reshape(1, SEQS, WIN, 2, HD),
            np.ascontiguousarray(o["pool_sample"].transpose(2, 3, 1, 0)).reshape(1, SEQS, PSTATE, 512))
```

```python
from contextlib import ExitStack
from functools import partial

import concourse.bass as bass
from concourse import mybir

F32 = mybir.dt.float32
I32 = mybir.dt.int32
U32 = mybir.dt.uint32
ALU = mybir.AluOpType
ACT = mybir.ActivationFunctionType
AX = mybir.AxisListType

P = 128
D = 1024
DC = D // P
GROUPS = 4
BLK = 2
GN = BLK * P
META = 16
SAMP = 32
SEQS = 8
DSEQ = 4
X0 = META + SAMP
COLS = X0 + GN
HD = 64
HPK = 4
WIN = 128
HIST = 16
PSTATE = 15
SCALE = HD ** -0.5
ALPHA = 2.0 ** 0.25
EPS = 1e-5
NEG = -1e30
HEADS = 8
TOPK = 16
SLOTS = HEADS * TOPK
RING = 8
BODY = 2 * RING
BATCH = 4
BODIES = SLOTS // BODY
PE_SLOTS = [k for k in range(BODY) if k % BATCH != BATCH - 1]
PE_TILES = RING - RING // BATCH
DVE_TILES = RING // BATCH
QUARTERS = P // SAMP

WR = 4
POS_K, POS_V, POS_IN, POS_UP, POS_OUT, POS_QRY, POS_END = 0, 1, 4, 28, 36, 44, 60
HOLES = (2, 3)
UNITS = POS_END - len(HOLES)
N_IN = POS_UP - POS_IN
N_UP = POS_OUT - POS_UP
N_OUT = POS_QRY - POS_OUT
N_QRY = POS_END - POS_QRY
PROJ = 2 + N_IN


def ordinal(pos):
    return pos if pos < HOLES[0] else pos - len(HOLES)


def loads_upto(pos):
    return sum(1 for n in range(pos % WR, pos + 1, WR) if n not in HOLES)


LOADS = [loads_upto(POS_END - WR + s) for s in range(WR)]


def wait(eng, sem, value):
    if not isinstance(value, int) or value > 0:
        eng.wait_ge(sem, value)


def hold(eng, sem, value):
    eng.wait_ge(sem, value)
    eng.nop(nofuse=True)


def nth(g, b):
    return b + 1 if isinstance(g, int) and g == 0 else g * BLK + (b + 2)


def first(g):
    return isinstance(g, int) and g == 0


def layer_kernel(nc, xT, xT_extra, x_rows, xs_rows, w_a, w_q, uv, table, sinks, sink_rows, w_mix, pool_scale,
                 ln1_g, ln1_b, ln2_g, ln2_b, ckT, cv_rows, cache_v, stT,
                 ident_c, flip_c, onehot_c, linemask_c, sel_c, smask_c, iota_c, sel4_c,
                 line_scratch, score_scratch, y_prompt, y_sample, k_prompt, v_prompt, pool_prompt, k_sample, v_sample, pool_sample):
    with ExitStack() as ctx:
        def sb(name, shape, dt=F32):
            return ctx.enter_context(nc.sbuf_tensor(name, shape, dt))

        def sem(name):
            return ctx.enter_context(nc.semaphore(name))

        ident = sb("ident", [P, P])
        sel4 = sb("sel4", [P, SAMP])
        zeros = sb("zeros", [P, P])
        iota = sb("iota", [P, TOPK])
        bias = sb("bias", [P, HEADS, 2 * P])
        sink = sb("sink", [P, HEADS])
        wmix = sb("wmix", [P, 4, P])
        pscale = sb("pscale", [P, 4])
        ln2g = sb("ln2g", [P, D])
        ln2b = sb("ln2b", [P, D])
        wring = sb("wring", [P, WR, D + P])
        xm = sb("xm", [P, DC, COLS])
        poolT = sb("poolT", [P, 4, HIST + GN])
        pooled = sb("pooled", [P, 4, SAMP + GN])
        qT = sb("qT", [P, 4, SAMP + GN])
        kT = sb("kT", [P, P + GN])
        vR = sb("vR", [P, BLK + 1, P])
        big = sb("big", [P, 16 * (SAMP + GN)])
        att = sb("att", [P, 3072])
        amx = sb("amx", [P, 2, 4])
        anm = sb("anm", [P, 2, 4])
        ads = sb("ads", [P, 2, 4])
        aden = sb("aden", [P, 2, 4])
        stats = sb("stats", [P, 12])
        moments = sb("moments", [P, 4])
        stats2 = sb("stats2", [P, 12])
        moments2 = sb("moments2", [P, 4])
        qyT = sb("qyT", [P, 2, SAMP + GN])
        x1n = sb("x1n", [P, BLK, D])
        x1c = sb("x1c", [P, BLK, D])
        xs4 = sb("xs4", [P, D])
        x1s = xs4[0:SAMP, :]
        acc_v = sb("acc_v", [P, D])
        idxn = sb("idxn", [P, BLK, SLOTS], I32)
        idxc = sb("idxc", [P, BLK, SLOTS], I32)
        idx4 = sb("idx4", [P, SLOTS // QUARTERS], I32)
        gaten = sb("gaten", [P, BLK, SLOTS])
        gatec = sb("gatec", [P, BLK, SLOTS])
        gate4 = sb("gate4", [P, SLOTS // QUARTERS])
        idx8 = [sb(f"idx8_{n}", [P, RING], I32) for n in range(2)]
        tops = sb("tops", [P, HEADS, 2, TOPK])
        topi = sb("topi", [P, HEADS, 2, TOPK], U32)
        topf = sb("topf", [P, HEADS, 2, TOPK])
        bests = sb("bests", [P, HEADS, TOPK])
        bestj = sb("bestj", [P, HEADS, TOPK], U32)
        jpart = sb("jpart", [P, SLOTS], U32)
        jf = sb("jf", [P, SLOTS])
        ipart = sb("ipart", [P, 2, SLOTS])
        gsum = sb("gsum", [P, HEADS])
        hdot = sb("hdot", [P, 2, BATCH])
        hgelu = sb("hgelu", [P, 2, BATCH])
        hw = sb("hw", [P, 2, BATCH])
        diag = sb("diag", [P, RING, P])
        ring = sb("ring", [P, RING, 2 * D])

        def early(tile, off, *dims):
            size = 1
            for d in dims:
                size *= d
            ap = ring[:, tile, off:off + size]
            if len(dims) == 2:
                return ap.rearrange("p (a b) -> p a b", a=dims[0])
            if len(dims) == 3:
                return ap.rearrange("p (a b c) -> p a b c", a=dims[0], b=dims[1])
            return ap

        kX = early(0, 0, SEQS, WIN + DSEQ)
        sPool = early(1, 0, 4, SEQS, PSTATE + DSEQ)
        sT1 = early(1, 640, SEQS, PSTATE + DSEQ)
        sT2 = early(1, 832, SEQS, PSTATE + DSEQ)
        sQ = early(1, 1024, 4, 32)
        sBias = early(2, 0, 2, 288)
        sS = early(2, 576, 2, 288)
        sPT = early(2, 1152, 2, 384)
        sV = early(1, 1152, P)
        vX = early(3, 0, SEQS, P)
        sMask = early(3, 1024, 2, 288)
        sSmall = early(3, 1600, 16)
        sSink = early(3, 1620, 2)
        flip = early(4, 0, P)
        onehot = early(4, 128, 384)
        lmask = early(4, 512, 384)
        line = early(4, 896, 384)
        tab = early(4, 1280, HEADS)
        sel = early(5, 0, HEADS, P)
        sScores = ring[0:SAMP, 6, :]

        def scores_of(b):
            return big[:, b * 2048:(b + 1) * 2048]

        gates = big[:, :].rearrange("p (a b) -> p a b", a=16)
        S = [att[:, 0:1024], att[:, 1024:2048]]
        PT = att[:, 2048:3072]
        t1 = att[:, 0:4 * (HIST + GN)].rearrange("p (a b) -> p a b", a=4)
        t2 = att[:, 4 * (HIST + GN):8 * (HIST + GN)].rearrange("p (a b) -> p a b", a=4)
        ln1g, ln1b = att[:, 0:1024], att[:, 1024:2048]

        pj = [ctx.enter_context(nc.psum_tensor(f"pj{n}", [P, 512], F32)) for n in range(2)]
        acc = ctx.enter_context(nc.psum_tensor("acc", [P, D], F32))
        wide = [ctx.enter_context(nc.psum_tensor(f"wide{n}", [P, D], F32)) for n in range(2)]

        consts = sem("consts")
        bias_in = sem("bias_in")
        early_in = sem("early_in")
        built = sem("built")
        line_ps, line_sb, line_st, line_ld = sem("line_ps"), sem("line_sb"), sem("line_st"), sem("line_ld")
        bias_ps, bias_sb, sbias_ps, sbias_sb = sem("bias_ps"), sem("bias_sb"), sem("sbias_ps"), sem("sbias_sb")
        w_in_sem = [sem(f"w_tile{n}") for n in range(WR)]
        xt_in = sem("xt_in")
        xr_in = sem("xr_in")
        xs_in = sem("xs_in")
        ln1_in = sem("ln1_in")
        unit_done = sem("unit_done")
        proj_evac = sem("proj_evac")
        gate_sig = sem("gate_sig")
        pool_ready = sem("pool_ready")
        mix_done, mix_evac = sem("mix_done"), sem("mix_evac")
        score_ready, max_ready, exp_done = sem("score_ready"), sem("max_ready"), sem("exp_done")
        p_ready, pt_ready, pt_evac = sem("p_ready"), sem("pt_ready"), sem("pt_evac")
        o_ready, o_evac = sem("o_ready"), sem("o_evac")
        sq_ready, s_score, s_max, s_exp, s_p = sem("sq_ready"), sem("s_score"), sem("s_max"), sem("s_exp"), sem("s_p")
        s_pt, s_pt_evac, s_o, s_o_evac = sem("s_pt"), sem("s_pt_evac"), sem("s_o"), sem("s_o_evac")
        up_read, m_ready = sem("up_read"), sem("m_ready")
        y_read, ln1_var, ln1_std, x1_ready = sem("y_read"), sem("ln1_var"), sem("ln1_std"), sem("x1_ready")
        xt_ready, xt_evac = sem("xt_ready"), sem("xt_evac")
        qry_ready, qry_evac, sc_evac = sem("qry_ready"), sem("qry_evac"), sem("sc_evac")
        gmax_ready, gexp_done = sem("gmax_ready"), sem("gexp_done")
        cur_ready = [sem(f"cur_ready{n}") for n in range(BLK)]
        samp_scores, samp_got, samp_in = sem("samp_scores"), sem("samp_got"), sem("samp_in")
        x4_in = sem("x4_in")
        carried = sem("carried")
        idx_ready = sem("idx_ready")
        gathered = [sem(f"gathered{n}") for n in range(RING)]
        slot_free = sem("slot_free")
        vslot_free = sem("vslot_free")
        accv_ready = sem("accv_ready")
        dot_done, gelu_done, w_ready, diag_done = sem("dot_done"), sem("gelu_done"), sem("w_ready"), sem("diag_done")
        acc_done, acc_read = sem("acc_done"), sem("acc_read")
        ln2_var, ln2_std, y_ready = sem("ln2_var"), sem("ln2_std"), sem("y_ready")
        y_out = [sem(f"y_out{n}") for n in range(BLK)]
        ys_out = sem("ys_out")
        states_out = sem("states_out")
        early_out = sem("early_out")

        N_CONSTS = 9
        EARLY_STORES = 14

        def lo(g, width):
            return 0 if first(g) else width

        block = ctx.enter_context(nc.Block())

        @block.sync
        def _(sp):
            for dst, src in ((ident[:, :], ident_c), (iota[:, :], iota_c),
                             (sink[:, :], sinks.partition_broadcast(P)), (wmix[:, :, :], w_mix),
                             (pscale[:, :], pool_scale), (ln2g[:, :], ln2_g.partition_broadcast(P)),
                             (ln2b[:, :], ln2_b.partition_broadcast(P)), (flip, flip_c), (sel4[:, :], sel4_c)):
                sp.dma_start(dst, src).then_inc(consts, 16)

            def load_unit(g, pos, it=0):
                before = pos - WR if pos - WR not in HOLES else pos - 2 * WR
                if before >= 0:
                    wait(sp, unit_done, g * UNITS + it * WR + (ordinal(before) + 1))
                elif not first(g):
                    wait(sp, unit_done, g * UNITS + (ordinal(before + POS_END) + 1 - UNITS))
                s = pos % WR
                if pos >= POS_QRY:
                    dst, src = wring[:, s, :], w_q[bass.ds(it * WR + (pos - POS_QRY), 1)]
                else:
                    dst, src = wring[:, s, 0:D], w_a[bass.ds(it * WR + ordinal(pos), 1)]
                sp.dma_start(dst, src.rearrange("o p f -> (o p) f")).then_inc(w_in_sem[s], 16)

            def load_loop(g, pos, n):
                if pos == POS_IN:
                    for k in range(WR):
                        load_unit(g, pos + k)
                    pos, n = pos + WR, n - WR
                with nc.sync.Fori(0, n // WR) as it:
                    for k in range(WR):
                        load_unit(g, pos + k, it)

            def load_group(g):
                wait(sp, unit_done, g * UNITS)
                if first(g):
                    sp.dma_start(xm[:, :, 0:X0], xT_extra).then_inc(xt_in, 16)
                    sp.dma_start(xm[:, :, X0:COLS], xT[0]).then_inc(xt_in, 16)
                else:
                    sp.dma_start(xm[:, :, X0:COLS],
                                 xT[bass.ds(g, 1)].rearrange("o p c n -> (o p) c n")).then_inc(xt_in, 16)
                load_unit(g, POS_K)
                load_unit(g, POS_V)
                load_loop(g, POS_IN, N_IN)
                for b in range(BLK):
                    wait(sp, cur_ready[b], g)
                    sp.dma_start(x1n[:, b, :],
                                 x_rows[bass.ds(g * BLK + b, 1)].rearrange("o p d -> (o p) d")).then_inc(xr_in, 16)
                load_loop(g, POS_UP, N_UP)
                wait(sp, o_ready, g * 4 + 4)
                wait(sp, s_pt, 2)
                sp.dma_start(ln1g, ln1_g.partition_broadcast(P)).then_inc(ln1_in, 16)
                sp.dma_start(ln1b, ln1_b.partition_broadcast(P)).then_inc(ln1_in, 16)
                if not first(g):
                    store_block(g, 0)
                load_loop(g, POS_OUT, N_OUT)
                load_loop(g, POS_QRY, N_QRY)
                if not first(g):
                    store_block(g, 1)

            def store_block(g, b):
                wait(sp, y_ready, (g - 1) * BLK + (b + 1))
                dst = y_prompt[bass.ds((g - 1) * BLK + b, 1)].rearrange("o p d -> (o p) d")
                sp.dma_start(dst, x1c[:, b, :]).then_inc(y_out[b], 16)

            for dst, src in ((onehot[0:32], onehot_c), (lmask[0:HEADS], linemask_c), (tab[0:32], table),
                             (sel[0:DSEQ], sel_c)):
                sp.dma_start(dst, src).then_inc(bias_in, 16)
            sp.wait_ge(line_sb, 1)
            sp.dma_start(line_scratch, line[0:HEADS]).then_inc(line_st, 16)
            sp.wait_ge(line_st, 16)
            window = bass.AP(line_scratch.tensor, 0, [[1, P], [384, HEADS], [1, 2 * P]])
            sp.dma_start(att[:, 0:2048].rearrange("p (h j) -> p h j", h=HEADS), window).then_inc(line_ld, 16)
            for s in range(SEQS):
                sp.dma_start(kX[:, s, 0:WIN], ckT[:, s, :]).then_inc(early_in, 16)
            sp.dma_start(vX, cv_rows).then_inc(early_in, 16)
            for c in range(4):
                sp.dma_start(sPool[:, c, :, 0:PSTATE], stT[:, c]).then_inc(early_in, 16)
            sp.dma_start(sMask, smask_c).then_inc(early_in, 16)
            sp.dma_start(sSink, sink_rows).then_inc(early_in, 16)
            sp.dma_start(x1s, xs_rows).then_inc(xs_in, 16)
            load_group(0)
            sp.dma_start(v_sample[:, 0:WIN - DSEQ, :], cache_v[:, DSEQ:WIN, :]).then_inc(states_out, 16)
            sp.wait_ge(proj_evac, PROJ)
            sp.dma_start(k_sample, kX[:, :, DSEQ:DSEQ + WIN]).then_inc(early_out, 16)
            for s in range(SEQS):
                sp.dma_start(v_sample[s, WIN - DSEQ:WIN, :], sV[DSEQ * s:DSEQ * s + DSEQ]).then_inc(early_out, 16)
            for c in range(4):
                sp.dma_start(pool_sample[:, c], sPool[:, c, :, DSEQ:DSEQ + PSTATE]).then_inc(early_out, 16)

            sp.wait_ge(sc_evac, N_QRY)
            sp.dma_start(score_scratch, sScores).then_inc(early_out, 16)
            sp.wait_ge(x1_ready, BLK + 1)
            for q in range(1, QUARTERS):
                sp.dma_start(xs4[SAMP * q:SAMP * (q + 1), :], x1s).then_inc(x4_in, 16)

            with nc.sync.Fori(1, GROUPS) as g:
                load_group(g)
            sp.wait_ge(carried, GROUPS)
            sp.dma_start(k_prompt, kT[:, 0:P]).then_inc(states_out, 16)
            sp.dma_start(v_prompt, vR[:, 0, :]).then_inc(states_out, 16)
            sp.dma_start(pool_prompt, poolT[:, :, HIST - PSTATE:HIST]).then_inc(states_out, 16)
            sp.wait_ge(early_out, 16 * EARLY_STORES)
            sp.wait_ge(cur_ready[0], GROUPS)
            sp.dma_start(big[0:SAMP, 0:2048], score_scratch).then_inc(samp_scores, 16)
            sp.wait_ge(samp_got, 1)
            n = SLOTS // QUARTERS
            for q in range(QUARTERS):
                rows = slice(SAMP * q, SAMP * (q + 1))
                sp.dma_start(idx4[rows, :], idxn[0:SAMP, 0, n * q:n * (q + 1)]).then_inc(samp_in, 16)
                sp.dma_start(gate4[rows, :], gaten[0:SAMP, 0, n * q:n * (q + 1)]).then_inc(samp_in, 16)
            for b in range(BLK):
                store_block(GROUPS, b)
            sp.wait_ge(y_ready, GROUPS * BLK + 1)
            sp.dma_start(y_sample, x1s).then_inc(ys_out, 16)
            sp.wait_ge(states_out, 64)
            for b in range(BLK):
                sp.wait_ge(y_out[b], 16 * (GROUPS + b))
            sp.wait_ge(ys_out, 16)

        @block.gpsimd
        def _(pool):
            def gather_block(n, idx, bodies):
                with nc.gpsimd.Fori(0, bodies) as it:
                    for half in range(2):
                        nc.gpsimd.tensor_copy(idx8[half][:, :], idx[:, bass.ds(it * BODY + half * RING, RING)])\
                            .then_inc(idx_ready, 1)
                        hold(pool, idx_ready, n * (SLOTS // RING) + it * 2 + (half + 1))
                        for k in range(RING):
                            if k % BATCH < BATCH - 1:
                                hold(pool, slot_free, n * (BODIES * len(PE_SLOTS)) + it * len(PE_SLOTS)
                                     + (half * PE_TILES + k - k // BATCH + 1))
                            else:
                                hold(pool, vslot_free, n * (SLOTS // BATCH) + it * (BODY // BATCH)
                                     + (half * DVE_TILES + k // BATCH + 1))
                            pool.indirect_dma_start(
                                ring[:, k, :], None, uv,
                                bass.IndirectOffsetOnAxis(ap=idx8[half][:, k:k + 1], axis=0))\
                                .then_inc(gathered[k], 16)

            def gather_pair(g):
                for b in range(BLK):
                    hold(pool, cur_ready[b], g)
                    gather_block((g - 1) * BLK + b, idxc[:, b, :], BODIES)

            pool.wait_ge(early_out, 16 * EARLY_STORES)
            with nc.gpsimd.Fori(1, GROUPS) as g:
                gather_pair(g)
            gather_pair(GROUPS)
            pool.wait_ge(samp_in, 16 * 2 * QUARTERS)
            gather_block(GROUPS * BLK, idx4[:, :], BODIES // QUARTERS)

        @block.scalar
        def _(act):
            copy = ACT.Copy

            for n in range(2):
                act.wait_ge(bias_ps, n + 1)
                nc.scalar.activation(bias[:, 4 * n:4 * n + 4, :].rearrange("p h j -> p (h j)"), wide[n][:, :], copy)\
                    .then_inc(bias_sb, 1)

            def evac(g, n, src, dst, also=()):
                act.wait_ge(unit_done, g * UNITS + (n + 1))
                for s, d in also:
                    nc.scalar.activation(d, s, copy)
                nc.scalar.activation(dst, src, copy).then_inc(proj_evac, 1)

            def exps(g, i):
                act.wait_ge(max_ready, g * 4 + (i + 1))
                for h in range(HPK):
                    s = S[i % 2][:, h * 256:(h + 1) * 256]
                    nc.scalar.activation(s, s, ACT.Exp, bias=anm[:, i % 2, h:h + 1], accum_out=aden[:, i % 2, h:h + 1])
                nc.scalar.activation(ads[:, i % 2, :], ads[:, i % 2, :], ACT.Exp).then_inc(exp_done, 1)

            def attention_pass(g, i):
                b, kv = divmod(i, 2)
                exps(g, i)
                for n in range(4):
                    c = 4 * i + n
                    if c == 0 and not first(g):
                        act.wait_ge(cur_ready[1], g)
                    evac(g, 10 + c, pj[c % 2][:, META if first(g) else X0:COLS], gates[:, c, lo(g, SAMP):])
                act.wait_ge(pt_ready, g * 4 + (i + 1))
                wait(act, o_ready, g * 4 + i)
                nc.scalar.activation(PT, wide[1][:, :], copy).then_inc(pt_evac, 1)
                act.wait_ge(o_ready, g * 4 + (i + 1))
                rows = slice(HD * kv, HD * kv + HD)
                nc.scalar.activation(qT[rows, :, SAMP + b * P:SAMP + (b + 1) * P],
                                     wide[0][rows, 0:512].rearrange("p (c n) -> p c n", c=4), copy)\
                    .then_inc(o_evac, 1)

            def sample_attention():
                act.wait_ge(s_max, 1)
                for t in range(2):
                    nc.scalar.activation(sS[:, t, :], sS[:, t, :], ACT.Exp, bias=sSmall[:, 2 + t:3 + t],
                                         accum_out=sSmall[:, 4 + t:5 + t])
                nc.scalar.activation(sSmall[:, 6:8], sSmall[:, 6:8], ACT.Exp).then_inc(s_exp, 1)
                for t in range(2):
                    act.wait_ge(s_pt, t + 1)
                    nc.scalar.activation(sPT[:, t, 0:256], wide[1][:, t * 512:t * 512 + 256], copy)
                    nc.scalar.activation(sPT[0:SAMP, t, 256:384], wide[1][0:SAMP, t * 512 + 256:t * 512 + 384],
                                         copy).then_inc(s_pt_evac, 1)
                act.wait_ge(s_o, 1)
                for kv in range(2):
                    rows = slice(HD * kv, HD * kv + HD)
                    for c in range(HPK):
                        src = acc[rows, 0:P].rearrange("p (s c i) -> p s c i", s=SEQS, c=HPK)[:, :, c, :]
                        nc.scalar.activation(qT[rows, c, 0:SAMP].rearrange("p (s i) -> p s i", s=SEQS), src, copy)\
                            .then_inc(s_o_evac, 1)

            def unit_k_v_pool(g):
                if first(g):
                    act.wait_ge(early_in, 15 * 16)
                    evac(0, 0, pj[0][:, X0:COLS], kT[:, P:P + GN],
                         also=((pj[0][:, 0:META], kT[:, 0:META]),
                               (pj[0][:, META:X0].rearrange("p (s i) -> p s i", s=SEQS), kX[:, :, WIN:WIN + DSEQ])))
                    evac(0, 1, pj[1][:, 0:GN], vR[:, 1:1 + BLK, :].rearrange("p b n -> p (b n)"),
                         also=((pj[1][0:META, 384:512], vR[0:META, 0, :]), (pj[1][0:SAMP, 256:384], sV[0:SAMP])))
                else:
                    act.wait_ge(carried, g)
                    evac(g, 0, pj[0][:, X0:COLS], kT[:, P:P + GN])
                    evac(g, 1, pj[1][:, 0:GN], vR[:, 1:1 + BLK, :].rearrange("p b n -> p (b n)"))
                for c in range(4):
                    if first(g):
                        evac(0, 2 + c, pj[c % 2][:, X0:COLS], poolT[:, c, HIST:],
                             also=((pj[c % 2][:, 0:META], poolT[:, c, 0:META]),
                                   (pj[c % 2][:, META:X0].rearrange("p (s i) -> p s i", s=SEQS),
                                    sPool[:, c, :, PSTATE:])))
                    else:
                        evac(g, 2 + c, pj[c % 2][:, X0:COLS], poolT[:, c, HIST:])

            def units_q(g):
                for c in range(4):
                    evac(g, 6 + c, pj[c % 2][:, META if first(g) else X0:COLS], qT[:, c, lo(g, SAMP):])

            def gates_and_mix(g):
                if first(g):
                    sample_attention()
                nc.scalar.activation(gates[:, :, lo(g, SAMP):], gates[:, :, lo(g, SAMP):], ACT.Sigmoid)\
                    .then_inc(gate_sig, 1)
                act.wait_ge(mix_done, g + 1)
                act.wait_ge(consts, 16 * N_CONSTS)
                for c, ps in enumerate((pj[0], pj[1], wide[1][:, 0:512], wide[1][:, 512:1024])):
                    nc.scalar.activation(pooled[:, c, lo(g, SAMP):], ps[:, META if first(g) else X0:COLS], copy,
                                         scale=pscale[:, c:c + 1]).then_inc(mix_evac, 1)

            def norm1_and_x1(g):
                for b in range(BLK + first(g)):
                    act.wait_ge(ln1_var, nth(g, b))
                    rows = P if b < BLK else SAMP
                    nc.scalar.activation(moments[0:rows, 2:3], moments[0:rows, 1:2], ACT.Sqrt).then_inc(ln1_std, 1)
                for b in range(BLK + first(g)):
                    act.wait_ge(xt_ready, nth(g, b))
                    if b < BLK:
                        nc.scalar.activation(xm[:, :, X0 + b * P:X0 + (b + 1) * P],
                                             wide[b][:, :].rearrange("p (c n) -> p c n", c=DC), copy)\
                            .then_inc(xt_evac, 1)
                    else:
                        nc.scalar.activation(xm[:, :, META:X0],
                                             acc[:, 0:DC * SAMP].rearrange("p (c n) -> p c n", c=DC), copy)\
                            .then_inc(xt_evac, 1)

            def queries(g, it):
                for k in (0, 1, -1, 2, -2, 3, -3, -4):
                    if k >= 0:
                        act.wait_ge(qry_ready, g * N_QRY + it * WR + (k + 1))
                        nc.scalar.activation(qyT[:, k % 2, lo(g, SAMP):],
                                             pj[k % 2][:, META if first(g) else X0:COLS], copy)\
                            .then_inc(qry_evac, 1)
                    else:
                        u = -k - 1
                        act.wait_ge(unit_done, g * UNITS + it * WR + (ordinal(POS_QRY) + u + 1))
                        ps = wide[u // 2][:, (u % 2) * 512:(u % 2) * 512 + 384]
                        if first(g):
                            nc.scalar.activation(sScores[:, bass.ds(it * (WR * P) + u * P, P)],
                                                 ps[0:SAMP, 256:384], copy)
                        nc.scalar.activation(big[:, bass.ds(it * (WR * P) + u * P, P)], ps[:, 0:P], copy)
                        nc.scalar.activation(big[:, bass.ds(it * (WR * P) + (2048 + u * P), P)], ps[:, P:2 * P],
                                             copy).then_inc(sc_evac, 1)

            def gate_exp(gate, count):
                act.wait_ge(gmax_ready, count)
                nc.scalar.activation(gate, gate, ACT.Exp).then_inc(gexp_done, 1)

            def slots(n, it, eye=ident, width=P):
                for m in range(BODY // BATCH):
                    act.wait_ge(dot_done, n * SLOTS + it * BODY + BATCH * (m + 1))
                    nc.scalar.activation(hgelu[:, m % 2, :], hdot[:, m % 2, :], ACT.Gelu).then_inc(gelu_done, 1)
                    act.wait_ge(w_ready, n * (SLOTS // BATCH) + it * (BODY // BATCH) + (m + 1))
                    for j in range(BATCH - 1):
                        act.wait_ge(slot_free, n * (BODIES * len(PE_SLOTS)) + it * len(PE_SLOTS)
                                    + (m * (BATCH - 1) + j + 1))
                        nc.scalar.activation(diag[:, (m * BATCH + j) % RING, 0:width], eye[:, :], copy,
                                             scale=hw[:, m % 2, j:j + 1]).then_inc(diag_done, 1)

            def norm2(n, rows=P):
                act.wait_ge(ln2_var, n + 1)
                nc.scalar.activation(moments2[0:rows, 2:3], moments2[0:rows, 1:2], ACT.Sqrt).then_inc(ln2_std, 1)

            def rounds(g, body):
                body(0, 0)
                unit_k_v_pool(g)
                body(0, 1)
                units_q(g)
                if not first(g):
                    gate_exp(gaten[:, 1, :], g * BLK)
                for i in range(4):
                    body(0, 2 + i)
                    attention_pass(g, i)
                gates_and_mix(g)
                body(0, 6)
                body(0, 7)
                if not first(g):
                    norm2((g - 1) * BLK)
                body(1, 0)
                body(1, 1)
                norm1_and_x1(g)
                with nc.scalar.Fori(0, N_QRY // WR) as it:
                    body(1, it + 2)
                    queries(g, it)
                body(1, 6)
                gate_exp(gaten[:, 0, :], g * BLK + 1)
                body(1, 7)
                if not first(g):
                    norm2((g - 1) * BLK + 1)

            rounds(0, lambda b, it: None)
            with nc.scalar.Fori(1, GROUPS) as g:
                rounds(g, lambda b, it: slots((g - 1) * BLK + b, it))
            n = (GROUPS - 1) * BLK
            slots(n, 0)
            slots(n, 1)
            gate_exp(gaten[:, 1, :], GROUPS * BLK)
            slots(n, 2)
            slots(n, 3)
            gate_exp(gaten[0:SAMP, 0, :], GROUPS * BLK + 1)
            with nc.scalar.Fori(4, BODIES) as it:
                slots(n, it)
            norm2(n)
            with nc.scalar.Fori(0, BODIES) as it:
                slots(n + 1, it)
            norm2(n + 1)
            with nc.scalar.Fori(0, BODIES // QUARTERS) as it:
                slots(n + 2, it, sel4, SAMP)
            norm2(n + 2, SAMP)

        @block.tensor
        def _(pe):
            mm = nc.tensor.matmul

            def unit_in(g, pos, it=None):
                s = pos % WR
                v = g * (16 * LOADS[s]) + 16 * loads_upto(pos)
                pe.wait_ge(w_in_sem[s], v if it is None else v + it * 16)
                return wring[:, s, 0:D].rearrange("p (c n) -> p c n", c=DC)

            def chunk(g, pos, ps, c0, need=None, it=None):
                w = unit_in(g, pos, it)
                for c in range(DC):
                    m = mm(ps[:, c0:COLS], w[:, c, :], xm[:, c, c0:COLS], start=(c == 0), stop=(c == DC - 1))
                return m

            def position_bias():
                pe.wait_ge(bias_in, 4 * 16)
                mm(acc[0:HEADS, 0:384], tab[0:32], onehot[0:32], start=True, stop=True).then_inc(line_ps, 1)
                pe.wait_ge(consts, 16 * N_CONSTS)
                pe.wait_ge(line_ld, 16)
                for n in range(4):
                    m = mm(wide[n // 2][:, (n % 2) * 512:(n % 2) * 512 + 512], flip, att[:, n * 512:(n + 1) * 512],
                           start=True, stop=True)
                    if n % 2:
                        m.then_inc(bias_ps, 1)
                pe.wait_ge(bias_sb, 2)
                for h in range(HEADS):
                    m = mm(acc[:, 512:512 + WIN + DSEQ], sel[0:DSEQ, h, :], bias[0:DSEQ, h, 0:WIN + DSEQ],
                           start=(h == 0), stop=(h == HEADS - 1))
                m.then_inc(sbias_ps, 1)

            def attention_scores(g, i):
                b, kv = divmod(i, 2)
                rows = slice(HD * kv, HD * kv + HD)
                if i == 0:
                    pe.wait_ge(proj_evac, g * PROJ + 10)
                    wait(pe, sc_evac, g * N_QRY)
                else:
                    pe.wait_ge(o_evac, g * 4 + i)
                for c in range(HPK):
                    m = mm(wide[0][:, c * 256:(c + 1) * 256], qT[rows, c, SAMP + b * P:SAMP + (b + 1) * P],
                           kT[rows, b * P:b * P + 2 * P], start=True, stop=True)
                m.then_inc(score_ready, 1)

            def attention_output(g, i):
                b, kv = divmod(i, 2)
                rows = slice(HD * kv, HD * kv + HD)
                pe.wait_ge(p_ready, g * 4 + (i + 1))
                if i:
                    pe.wait_ge(pt_evac, g * 4 + i)
                for half in range(2):
                    for c in range(HPK):
                        at = half * 512 + c * P
                        m = mm(wide[1][:, at:at + P], S[i % 2][:, c * 256 + half * P:c * 256 + half * P + P],
                               ident[:, :], is_transpose=True, start=True, stop=True)
                m.then_inc(pt_ready, 1)
                pe.wait_ge(pt_evac, g * 4 + (i + 1))
                for half in range(2):
                    m = mm(wide[0][rows, 0:512], vR[:, b + half, HD * kv:HD * kv + HD],
                           PT[:, half * 512:half * 512 + 512], start=(half == 0), stop=(half == 1))
                m.then_inc(o_ready, 1)

            def gate_units(g, i):
                for n in range(4):
                    c = 4 * i + n
                    pe.wait_ge(proj_evac, g * PROJ + (10 + c - 1))
                    chunk(g, POS_IN + 8 + c, pj[c % 2], META if first(g) else X0).then_inc(unit_done, 1)

            def sample_attention():
                pe.wait_ge(sq_ready, 1)
                pe.wait_ge(o_evac, 4)
                for t in range(2):
                    for q in range(4):
                        pair, kv = 2 * t + q // 2, q % 2
                        rows = slice(HD * kv, HD * kv + HD)
                        out = wide[0][32 * q:32 * q + 32, t * 512:t * 512 + 288]
                        for n in range(2):
                            mm(out[:, n * WIN:(n + 1) * WIN], sQ[rows, pair, :], kX[rows, 2 * pair + n, 0:WIN],
                               start=True, stop=True)
                        m = mm(out[:, 256:288], sQ[rows, pair, :], kX[rows, :, WIN:], start=True, stop=True)
                m.then_inc(s_score, 1)
                pe.wait_ge(s_p, 1)
                pe.wait_ge(pt_evac, 4)
                for t in range(2):
                    for n in range(2):
                        mm(wide[1][:, t * 512 + n * P:t * 512 + (n + 1) * P], sS[:, t, n * P:(n + 1) * P],
                           ident[:, :], is_transpose=True, start=True, stop=True)
                    mm(wide[1][0:SAMP, t * 512 + 256:t * 512 + 384], sS[:, t, 256:288], ident[:, :],
                       is_transpose=True, start=True, stop=True).then_inc(s_pt, 1)
                pe.wait_ge(s_pt_evac, 2)
                for pair in range(4):
                    for kv in range(2):
                        t, q = pair // 2, 2 * (pair % 2) + kv
                        rows = slice(HD * kv, HD * kv + HD)
                        out = acc[rows, pair * 32:pair * 32 + 32]
                        for n in range(2):
                            mm(out, vX[:, 2 * pair + n, HD * kv:HD * kv + HD],
                               sPT[:, t, n * P + 32 * q:n * P + 32 * q + 32], start=(n == 0), stop=False)
                        m = mm(out, sV[0:SAMP, HD * kv:HD * kv + HD], sPT[0:SAMP, t, 256 + 32 * q:256 + 32 * q + 32],
                               start=False, stop=True)
                m.then_inc(s_o, 1)

            def units_k_v_pool(g):
                pe.wait_ge(xt_in, 32 if first(g) else g * 16 + 32)
                wait(pe, qry_evac, g * N_QRY)
                chunk(g, POS_K, pj[0], lo(g, X0)).then_inc(unit_done, 1)
                w = unit_in(g, POS_V)
                parts = [(pj[1][:, b * P:(b + 1) * P], X0 + b * P, X0 + (b + 1) * P) for b in range(BLK)]
                if first(g):
                    parts += [(pj[1][0:SAMP, 256:384], META, X0), (pj[1][0:META, 384:512], 0, META)]
                for out, a, z in parts:
                    for c in range(DC):
                        m = mm(out, xm[:, c, a:z], w[:, c, :], start=(c == 0), stop=(c == DC - 1))
                m.then_inc(unit_done, 1)
                for n in range(4):
                    pe.wait_ge(proj_evac, g * PROJ + (n + 1))
                    chunk(g, POS_IN + n, pj[n % 2], lo(g, X0)).then_inc(unit_done, 1)

            def units_q(g):
                for n in range(4, 8):
                    pe.wait_ge(proj_evac, g * PROJ + (n + 1))
                    chunk(g, POS_IN + n, pj[n % 2], META if first(g) else X0).then_inc(unit_done, 1)

            def mix(g):
                c0 = META if first(g) else X0
                pe.wait_ge(pool_ready, g + 1)
                pe.wait_ge(proj_evac, g * PROJ + PROJ)
                pe.wait_ge(pt_evac, g * 4 + 4)
                for c, ps in enumerate((pj[0], pj[1], wide[1][:, 0:512], wide[1][:, 512:1024])):
                    m = mm(ps[:, c0:COLS], wmix[:, c, :], pooled[:, c, lo(g, SAMP):], start=True, stop=True)
                m.then_inc(mix_done, 1)
                pe.wait_ge(mix_evac, g * 4 + 4)
                hold(pe, o_evac, g * 4 + 4)
                if first(g):
                    pe.wait_ge(s_o_evac, 8)

            def ups(g, it):
                c0 = META if first(g) else X0
                for k in range(WR):
                    w = unit_in(g, POS_UP + k, it)
                    pe.wait_ge(up_read, g * N_UP + it * WR + (k + 1))
                    pa, pb = (pj[0], pj[1]) if k % 2 == 0 else (wide[1][:, 0:512], wide[1][:, 512:1024])
                    for ps, w0, src in ((pa, 0, pooled), (pb, 4, qT)):
                        for c in range(4):
                            m = mm(ps[:, c0:COLS], w[:, w0 + c, :], src[:, c, lo(g, SAMP):],
                                   start=(c == 0), stop=(c == 3))
                    m.then_inc(unit_done, 1)

            def outs(g):
                hold(pe, m_ready, g * N_UP + N_UP)
                with nc.tensor.Fori(0, 2) as it:
                    for k in range(WR):
                        s = (POS_OUT + k) % WR
                        unit_in(g, POS_OUT + k, it)
                        w = wring[:, s, 0:D].rearrange("p (c n) -> p c n", c=4)
                        for b in range(BLK + first(g)):
                            full = wide[b] if b < BLK else acc
                            rows = P if b < BLK else SAMP
                            a = X0 + b * P if b < BLK else META
                            out = full[0:rows, bass.ds(it * 512 + (k // 2) * 256, 256)]
                            for c in range(4):
                                m = mm(out, xm[:, (k % 2) * 4 + c, a:a + rows], w[:, c, :],
                                       start=(k % 2 == 0 and c == 0), stop=(k % 2 == 1 and c == 3))
                        m.then_inc(unit_done, 1)

            def x1_transposes(g):
                for b in range(BLK + first(g)):
                    pe.wait_ge(x1_ready, nth(g, b))
                    for c in range(DC):
                        if b < BLK:
                            m = mm(wide[b][:, c * P:(c + 1) * P], x1n[:, b, c * P:(c + 1) * P], ident[:, :],
                                   is_transpose=True, start=True, stop=True)
                        else:
                            m = mm(acc[:, c * SAMP:(c + 1) * SAMP], x1s[:, c * P:(c + 1) * P],
                                   ident[0:SAMP, 0:SAMP], is_transpose=True, start=True, stop=True)
                    m.then_inc(xt_ready, 1)
                hold(pe, xt_evac, nth(g, BLK - 1) + first(g))

            def queries(g, it):
                for k in (0, 1, -1, 2, -2, 3, -3, -4):
                    if k >= 0:
                        if k >= 2:
                            pe.wait_ge(qry_evac, g * N_QRY + it * WR + (k - 1))
                        else:
                            wait(pe, qry_evac, g * N_QRY + it * WR)
                        chunk(g, POS_QRY + k, pj[k % 2], META if first(g) else X0, it=it).then_inc(qry_ready, 1)
                    else:
                        u = -k - 1
                        pe.wait_ge(qry_evac, g * N_QRY + it * WR + (u + 1))
                        wait(pe, sc_evac, g * N_QRY + it * WR)
                        keys = wring[:, u, D:D + P]
                        ps = wide[u // 2][:, (u % 2) * 512:(u % 2) * 512 + 384]
                        for b in range(BLK):
                            m = mm(ps[:, b * P:(b + 1) * P], qyT[:, u % 2, SAMP + b * P:SAMP + (b + 1) * P],
                                   keys, start=True, stop=True)
                        if first(g):
                            m = mm(ps[0:SAMP, 256:384], qyT[:, u % 2, 0:SAMP], keys, start=True, stop=True)
                        m.then_inc(unit_done, 1)

            def open_block(n, x, width=P):
                pe.wait_ge(acc_read, n + 1)
                for c in range(2):
                    mm(acc[0:width, c * 512:(c + 1) * 512], zeros[:, 0:width], x[:, c * 512:(c + 1) * 512],
                       start=True, stop=False)

            def slots(n, it, width=P):
                for r, k in enumerate(PE_SLOTS):
                    (pe.wait_ge if width == P else partial(hold, pe))(
                        diag_done, n * (BODIES * len(PE_SLOTS)) + it * len(PE_SLOTS) + (r + 1))
                    for c in range(2):
                        m = mm(acc[0:width, c * 512:(c + 1) * 512], diag[:, k % RING, 0:width],
                               ring[:, k % RING, D + c * 512:D + (c + 1) * 512], start=False, stop=False)
                    m.then_inc(slot_free, 1)

            def close_block(n, eye=ident, width=P):
                pe.wait_ge(accv_ready, n + 1)
                for c in range(2):
                    m = mm(acc[0:width, c * 512:(c + 1) * 512], eye[:, :], acc_v[:, c * 512:(c + 1) * 512],
                           start=False, stop=True)
                m.then_inc(acc_done, 1)

            def rounds(g, body):
                peer = not first(g)
                if peer:
                    pe.wait_ge(cur_ready[0], g)
                    open_block((g - 1) * BLK, x1c[:, 0, :])
                body(0, 0)
                units_k_v_pool(g)
                body(0, 1)
                units_q(g)
                attention_scores(g, 0)
                for i in range(4):
                    body(0, 2 + i)
                    gate_units(g, i)
                    attention_output(g, i)
                    if i < 3:
                        attention_scores(g, i + 1)
                if first(g):
                    sample_attention()
                mix(g)
                with nc.tensor.Fori(0, N_UP // WR) as it:
                    body(0, it + 6)
                    ups(g, it)
                if peer:
                    close_block((g - 1) * BLK)
                    pe.wait_ge(cur_ready[1], g)
                    open_block((g - 1) * BLK + 1, x1c[:, 1, :])
                body(1, 0)
                outs(g)
                body(1, 1)
                x1_transposes(g)
                with nc.tensor.Fori(0, N_QRY // WR) as it:
                    body(1, it + 2)
                    queries(g, it)
                body(1, 6)
                body(1, 7)
                if peer:
                    close_block((g - 1) * BLK + 1)

            pe.wait_ge(built, 1)
            position_bias()
            pe.wait_ge(sbias_sb, 1)
            rounds(0, lambda b, it: None)
            pe.sem_inc(slot_free, PE_TILES)
            with nc.tensor.Fori(1, GROUPS) as g:
                rounds(g, lambda b, it: slots((g - 1) * BLK + b, it))
            for b in range(BLK):
                n = (GROUPS - 1) * BLK + b
                pe.wait_ge(cur_ready[b], GROUPS)
                open_block(n, x1c[:, b, :])
                with nc.tensor.Fori(0, BODIES) as it:
                    slots(n, it)
                close_block(n)
            n = GROUPS * BLK
            pe.wait_ge(x4_in, 16 * (QUARTERS - 1))
            open_block(n, xs4[:, :], SAMP)
            with nc.tensor.Fori(0, BODIES // QUARTERS) as it:
                slots(n, it, SAMP)
            close_block(n, sel4, SAMP)

        @block.vector
        def _(dve):
            V = nc.vector

            def fence():
                dve.drain()

            def setup():
                V.memset(zeros[:, :], 0.0)
                V.memset(kT[:, 0:P], 0.0)
                V.memset(vR[:, 0, :], 0.0).then_inc(built, 1)
                dve.wait_ge(consts, 16 * N_CONSTS)
                dve.wait_ge(line_ps, 1)
                V.tensor_tensor(line[0:HEADS], acc[0:HEADS, 0:384], lmask[0:HEADS], ALU.add).then_inc(line_sb, 1)
                dve.wait_ge(early_in, 15 * 16)
                dve.wait_ge(sbias_ps, 1)
                for t in range(2):
                    for n in range(2):
                        V.tensor_tensor(sBias[:, t, n * WIN:(n + 1) * WIN], acc[:, 512:512 + WIN],
                                        sMask[:, t, n * WIN:(n + 1) * WIN], ALU.add)
                    m = V.tensor_tensor(sBias[:, t, 256:288].rearrange("p (s i) -> p s i", s=SEQS),
                                        acc[:, 512 + WIN:512 + WIN + DSEQ].unsqueeze(1).to_broadcast([P, SEQS, DSEQ]),
                                        sMask[:, t, 256:288].rearrange("p (s i) -> p s i", s=SEQS), ALU.add)
                m.then_inc(sbias_sb, 1)

            def pool_windows(g):
                dve.wait_ge(proj_evac, g * PROJ + 6)
                n = HIST + GN
                src, dst = poolT, t1
                for c in range(4):
                    w = 2 ** c
                    V.tensor_tensor(dst[:, c:, 2 * w - 1:n], src[:, c:, 2 * w - 1:n], src[:, c:, w - 1:n - w], ALU.add)
                    fence()
                    V.scalar_tensor_tensor(pooled[:, c, SAMP:], dst[:, c, HIST:n], 1.0 / (2 * w), poolT[:, c, HIST:n],
                                           ALU.mult, ALU.subtract)
                    src, dst = dst, (t2 if dst is t1 else t1)
                    fence()
                if first(g):
                    e = PSTATE + DSEQ
                    for c in range(4):
                        src, dst = sPool[:, c], sT1
                        for k in range(c + 1):
                            w = 2 ** k
                            V.tensor_tensor(dst[:, :, 2 * w - 1:e], src[:, :, 2 * w - 1:e], src[:, :, w - 1:e - w],
                                            ALU.add)
                            fence()
                            src, dst = dst, (sT2 if dst is sT1 else sT1)
                        V.scalar_tensor_tensor(pooled[:, c, 0:SAMP].rearrange("p (s i) -> p s i", s=SEQS),
                                               src[:, :, PSTATE:e], 1.0 / 2 ** (c + 1), sPool[:, c, :, PSTATE:e],
                                               ALU.mult, ALU.subtract)
                        fence()
                V.tensor_copy(poolT[:, :, 0:HIST], poolT[:, :, GN:GN + HIST]).then_inc(pool_ready, 1)

            def attention_pass(g, i):
                b, kv = divmod(i, 2)
                s = S[i % 2]
                bi = bias[:, 4 * kv:4 * kv + 4, :].rearrange("p h j -> p (h j)")
                dve.wait_ge(score_ready, g * 4 + (i + 1))
                if i >= 2:
                    dve.wait_ge(pt_ready, g * 4 + (i - 1))
                if first(g) and b == 0:
                    s4 = s.rearrange("p (h j) -> p h j", h=HPK)
                    r4 = wide[0][:, :].rearrange("p (h j) -> p h j", h=HPK)
                    b4 = bias[:, 4 * kv:4 * kv + 4, :]
                    V.memset(s4[:, :, META:P], NEG)
                    V.scalar_tensor_tensor(s4[:, :, 0:META], r4[:, :, 0:META], SCALE, b4[:, :, P - META:P],
                                           ALU.mult, ALU.add)
                    V.scalar_tensor_tensor(s4[:, :, P:], r4[:, :, P:], SCALE, b4[:, :, P:], ALU.mult, ALU.add)
                else:
                    V.scalar_tensor_tensor(s, wide[0][:, :], SCALE, bi, ALU.mult, ALU.add)
                fence()
                mx, nm, sk, den = amx[:, i % 2, :], anm[:, i % 2, :], ads[:, i % 2, :], aden[:, i % 2, :]
                V.tensor_reduce(mx, s.rearrange("p (h j) -> p h j", h=HPK), AX.X, ALU.max)
                fence()
                V.tensor_tensor(mx, mx, sink[:, 4 * kv:4 * kv + 4], ALU.max)
                fence()
                V.tensor_scalar(nm, mx, -1.0, None, ALU.mult)
                V.tensor_tensor(sk, sink[:, 4 * kv:4 * kv + 4], mx, ALU.subtract).then_inc(max_ready, 1)
                dve.wait_ge(exp_done, g * 4 + (i + 1))
                V.tensor_tensor(den, den, sk, ALU.add)
                fence()
                V.reciprocal(den, den)
                fence()
                V.tensor_tensor(s.rearrange("p (h j) -> p h j", h=HPK), s.rearrange("p (h j) -> p h j", h=HPK),
                                den.unsqueeze(2).to_broadcast([P, HPK, 256]), ALU.mult).then_inc(p_ready, 1)

            def sample_attention():
                for s in range(SEQS):
                    m = V.tensor_copy(sQ[:, s // 2, 16 * (s % 2):16 * (s % 2) + 16].rearrange("p (c i) -> p c i", c=HPK),
                                      qT[:, :, DSEQ * s:DSEQ * s + DSEQ])
                m.then_inc(sq_ready, 1)
                mx, nm, den, sk = sSmall[:, 0:2], sSmall[:, 2:4], sSmall[:, 4:6], sSmall[:, 6:8]
                dve.wait_ge(s_score, 1)
                for t in range(2):
                    V.scalar_tensor_tensor(sS[:, t, :], wide[0][:, t * 512:t * 512 + 288], SCALE, sBias[:, t, :],
                                           ALU.mult, ALU.add)
                fence()
                V.tensor_reduce(mx, sS, AX.X, ALU.max)
                fence()
                V.tensor_tensor(mx, mx, sSink, ALU.max)
                fence()
                V.tensor_scalar(nm, mx, -1.0, None, ALU.mult)
                V.tensor_tensor(sk, sSink, mx, ALU.subtract).then_inc(s_max, 1)
                dve.wait_ge(s_exp, 1)
                V.tensor_tensor(den, den, sk, ALU.add)
                fence()
                V.reciprocal(den, den)
                fence()
                V.tensor_tensor(sS, sS, den.unsqueeze(2).to_broadcast([P, 2, 288]), ALU.mult).then_inc(s_p, 1)

            def merge(g, chunks):
                dve.wait_ge(gate_sig, g + 1)
                c0 = META if first(g) else X0
                l0 = lo(g, SAMP)
                for j in chunks:
                    dve.wait_ge(unit_done, g * UNITS + (ordinal(POS_UP) + j + 1))
                    pa, pb = (pj[0], pj[1]) if j % 2 == 0 else (wide[1][:, 0:512], wide[1][:, 512:1024])
                    V.tensor_tensor(gates[:, j, l0:], gates[:, j, l0:], pa[:, c0:COLS], ALU.mult)
                    V.tensor_tensor(gates[:, 8 + j, l0:], gates[:, 8 + j, l0:], pb[:, c0:COLS], ALU.mult)\
                        .then_inc(up_read, 1)
                    fence()
                    V.tensor_tensor(xm[:, j, c0:COLS], gates[:, j, l0:], gates[:, 8 + j, l0:], ALU.add)\
                        .then_inc(m_ready, 1)

            def normalise(out, src, g_, b_, mom, st, var_sem, std_sem, count, read=None):
                rows = out.shape[0]
                V.bn_stats(st[0:rows, 0:6], src[:, 0:512])
                V.bn_stats(st[0:rows, 6:12], src[:, 512:1024])
                fence()
                V.bn_aggr(mom[0:rows, 0:2], st[0:rows, :])
                fence()
                V.tensor_scalar(mom[0:rows, 1:2], mom[0:rows, 1:2], EPS, None, ALU.add).then_inc(var_sem, 1)
                dve.wait_ge(std_sem, count)
                V.reciprocal(mom[0:rows, 3:4], mom[0:rows, 2:3])
                fence()
                m = V.tensor_scalar(out, src, mom[0:rows, 0:1], mom[0:rows, 3:4], ALU.subtract, ALU.mult)
                if read is not None:
                    m.then_inc(read, 1)
                fence()
                V.tensor_tensor(out, out, g_[0:rows], ALU.mult)
                fence()
                return V.tensor_tensor(out, out, b_[0:rows], ALU.add)

            def norm1(g):
                dve.wait_ge(unit_done, g * UNITS + (ordinal(POS_OUT) + N_OUT))
                dve.wait_ge(ln1_in, g * 32 + 32)
                dve.wait_ge(xr_in, g * 32 + 32)
                for b in range(BLK + first(g)):
                    x = x1n[:, b, :] if b < BLK else x1s
                    y = wide[b][:, :] if b < BLK else acc[0:SAMP, :]
                    if b == BLK:
                        dve.wait_ge(xs_in, 16)
                    V.scalar_tensor_tensor(x, x, ALPHA, y, ALU.mult, ALU.add)
                    fence()
                    normalise(x, x, ln1g, ln1b, moments, stats, ln1_var, ln1_std, nth(g, b)).then_inc(x1_ready, 1)

            def top16(top, idx, vals):
                sets = range(len(vals))
                for half in range(2):
                    h8 = slice(8 * half, 8 * half + 8)
                    for n in sets:
                        V.max(top[n][:, h8], vals[n])
                    fence()
                    for n in sets:
                        V.max_index(idx[n][:, h8], top[n][:, h8], vals[n])
                    fence()
                    if half == 0:
                        for n in sets:
                            V.match_replace(vals[n], top[n][:, h8], vals[n], NEG)
                        fence()

            def retrieve_halves(sc, rows, heads):
                sets = [(h, c) for h in heads for c in range(2)]
                top16([tops[0:rows, h, c, :] for h, c in sets], [topi[0:rows, h, c, :] for h, c in sets],
                      [sc[:, (2 * h + c) * P:(2 * h + c + 1) * P] for h, c in sets])

            def retrieve_sums(sc, rows):
                V.tensor_copy(topf[0:rows], topi[0:rows])
                for h in range(HEADS):
                    V.tensor_tensor(sc[:, h * 256:(h + 1) * 256].rearrange("p (a c) -> p a c", a=TOPK),
                                    tops[0:rows, h, 0, :].unsqueeze(2).to_broadcast([rows, TOPK, TOPK]),
                                    tops[0:rows, h, 1, :].unsqueeze(1).to_broadcast([rows, TOPK, TOPK]), ALU.add)
                fence()

            def retrieve_best(sc, rows, idx, gate, count):
                top16([bests[0:rows, h, :] for h in range(HEADS)], [bestj[0:rows, h, :] for h in range(HEADS)],
                      [sc[:, h * 256:(h + 1) * 256] for h in range(HEADS)])
                hot = sc.rearrange("p (m a) -> p m a", a=TOPK)
                hot4 = sc.rearrange("p (h k a) -> p h k a", h=HEADS, k=TOPK)
                for c in range(2):
                    flat = bestj[0:rows].rearrange("p h k -> p (h k)")
                    if c == 0:
                        V.tensor_scalar(jpart[0:rows], flat, 4, None, ALU.logical_shift_right)
                    else:
                        V.tensor_scalar(jpart[0:rows], flat, 15, None, ALU.bitwise_and)
                    fence()
                    V.tensor_copy(jf[0:rows], jpart[0:rows])
                    fence()
                    V.tensor_tensor(hot, jf[0:rows].unsqueeze(2).to_broadcast([rows, SLOTS, TOPK]),
                                    iota[0:rows].unsqueeze(1).to_broadcast([rows, SLOTS, TOPK]), ALU.is_equal)
                    fence()
                    V.tensor_tensor(hot4, hot4, topf[0:rows, :, c, :].unsqueeze(2)
                                    .to_broadcast([rows, HEADS, TOPK, TOPK]), ALU.mult)
                    fence()
                    V.tensor_reduce(ipart[0:rows, c, :], hot, AX.X, ALU.add)
                    fence()
                V.scalar_tensor_tensor(idx, ipart[0:rows, 0, :], float(P), ipart[0:rows, 1, :], ALU.mult, ALU.add)
                gate3 = gate.rearrange("p (h k) -> p h k", h=HEADS)
                V.tensor_tensor(gate3, bests[0:rows], bests[0:rows, :, 0:1].to_broadcast([rows, HEADS, TOPK]),
                                ALU.subtract).then_inc(gmax_ready, 1)
                dve.wait_ge(gexp_done, count)
                V.tensor_reduce(gsum[0:rows], gate3, AX.X, ALU.add)
                fence()
                V.reciprocal(gsum[0:rows], gsum[0:rows])
                fence()
                return V.tensor_tensor(gate3, gate3, gsum[0:rows].unsqueeze(2).to_broadcast([rows, HEADS, TOPK]),
                                       ALU.mult)

            def hand_over(g, b, idle):
                wait(dve, y_out[b], idle)
                V.tensor_copy(idxc[:, b, :], idxn[:, b, :])
                V.tensor_copy(gatec[:, b, :], gaten[:, b, :])
                V.tensor_copy(x1c[:, b, :], x1n[:, b, :]).then_inc(cur_ready[b], 1)

            def open_block(n, x, share=ALPHA):
                fence()
                V.tensor_scalar(acc_v[:, :], x, share, None, ALU.mult)

            def slots(n, it, x, gate):
                def dots(m):
                    for j in range(BATCH):
                        k = m * BATCH + j
                        u = ring[:, k % RING, 0:D]
                        dve.wait_ge(gathered[k % RING], n * (16 * SLOTS // RING) + it * 32 + 16 * (k // RING + 1))
                        V.tensor_tensor_reduce(u, u, x, 1.0, 0.0, ALU.mult, ALU.add, hdot[:, m % 2, j:j + 1])\
                            .then_inc(dot_done, 1)

                def weigh(m):
                    tile = (m * BATCH + BATCH - 1) % RING
                    dve.wait_ge(gelu_done, n * (SLOTS // BATCH) + it * (BODY // BATCH) + (m + 1))
                    V.tensor_tensor(hw[:, m % 2, :], hgelu[:, m % 2, :],
                                    gate[:, bass.ds(it * BODY + m * BATCH, BATCH)], ALU.mult).then_inc(w_ready, 1)
                    fence()
                    V.scalar_tensor_tensor(acc_v[:, :], ring[:, tile, D:2 * D], hw[:, m % 2, BATCH - 1:BATCH],
                                           acc_v[:, :], ALU.mult, ALU.add).then_inc(vslot_free, 1)

                for m in range(BODY // BATCH):
                    dots(m)
                    weigh(m)

            def close_block(n, x, width=P):
                dve.drain().then_inc(accv_ready, 1)
                dve.wait_ge(acc_done, n + 1)
                normalise(x, acc[0:width, :], ln2g, ln2b, moments2, stats2, ln2_var, ln2_std, n + 1, read=acc_read)\
                    .then_inc(y_ready, 1)

            def rounds(g, body):
                peer = not first(g)
                sa, sb_ = scores_of(0), scores_of(1)
                if peer:
                    open_block((g - 1) * BLK, x1c[:, 0, :])
                body(0, 0)
                if peer:
                    hold(dve, sc_evac, g * N_QRY)
                    retrieve_halves(sb_, P, range(HEADS))
                    retrieve_sums(sb_, P)
                body(0, 1)
                if peer:
                    retrieve_best(sb_, P, idxn[:, 1, :], gaten[:, 1, :], g * BLK)
                    fence()
                    hand_over(g - 1, 1, g * 16)
                pool_windows(g)
                for i in range(4):
                    body(0, 2 + i)
                    attention_pass(g, i)
                if first(g):
                    sample_attention()
                body(0, 6)
                merge(g, range(0, 4))
                body(0, 7)
                merge(g, range(4, 8))
                dve.wait_ge(o_ready, g * 4 + 4)
                V.tensor_copy(kT[:, 0:P], kT[:, GN:GN + P])
                V.tensor_copy(vR[:, 0, :], vR[:, BLK, :]).then_inc(carried, 1)
                if peer:
                    close_block((g - 1) * BLK, x1c[:, 0, :])
                    open_block((g - 1) * BLK + 1, x1c[:, 1, :])
                body(1, 0)
                body(1, 1)
                norm1(g)
                body(1, 2)
                body(1, 3)
                body(1, 4)
                hold(dve, sc_evac, g * N_QRY + 8)
                retrieve_halves(sa, P, range(0, 4))
                body(1, 5)
                hold(dve, sc_evac, g * N_QRY + 12)
                retrieve_halves(sa, P, range(4, 6))
                body(1, 6)
                hold(dve, sc_evac, g * N_QRY + 16)
                retrieve_halves(sa, P, range(6, 8))
                retrieve_sums(sa, P)
                retrieve_best(sa, P, idxn[:, 0, :], gaten[:, 0, :], g * BLK + 1)
                fence()
                hand_over(g, 0, g * 16)
                body(1, 7)
                if peer:
                    close_block((g - 1) * BLK + 1, x1c[:, 1, :])

            setup()
            dve.nop(nofuse=True).then_inc(up_read, 2)
            dve.nop(nofuse=True).then_inc(y_out[1], 16)
            dve.nop(nofuse=True).then_inc(vslot_free, DVE_TILES)
            rounds(0, lambda b, it: None)
            dve.drain().then_inc(acc_read, 1)
            with V.Fori(1, GROUPS) as g:
                rounds(g, lambda b, it: slots((g - 1) * BLK + b, it, x1c[:, b, :], gatec[:, b, :]))
            n = (GROUPS - 1) * BLK
            x, gate = x1c[:, 0, :], gatec[:, 0, :]
            open_block(n, x)
            slots(n, 0, x, gate)
            retrieve_halves(scores_of(1), P, range(HEADS))
            retrieve_sums(scores_of(1), P)
            slots(n, 1, x, gate)
            retrieve_best(scores_of(1), P, idxn[:, 1, :], gaten[:, 1, :], GROUPS * BLK)
            fence()
            hand_over(GROUPS - 1, 1, GROUPS * 16)
            slots(n, 2, x, gate)
            dve.wait_ge(samp_scores, 16)
            retrieve_halves(scores_of(0)[0:SAMP], SAMP, range(HEADS))
            retrieve_sums(scores_of(0)[0:SAMP], SAMP)
            slots(n, 3, x, gate)
            retrieve_best(scores_of(0)[0:SAMP], SAMP, idxn[0:SAMP, 0, :], gaten[0:SAMP, 0, :], GROUPS * BLK + 1)\
                .then_inc(samp_got, 1)
            with V.Fori(4, BODIES) as it:
                slots(n, it, x, gate)
            close_block(n, x)
            x, gate = x1c[:, 1, :], gatec[:, 1, :]
            open_block(n + 1, x)
            with V.Fori(0, BODIES) as it:
                slots(n + 1, it, x, gate)
            close_block(n + 1, x)
            dve.wait_ge(x4_in, 16 * (QUARTERS - 1))
            dve.wait_ge(samp_in, 16 * 2 * QUARTERS)
            open_block(n + 2, xs4[:, :], ALPHA / QUARTERS)
            with V.Fori(0, BODIES // QUARTERS) as it:
                slots(n + 2, it, xs4[:, :], gate4[:, :])
            close_block(n + 2, x1s, SAMP)


def kernel(**inputs):
    import numpy as np
    import concourse.bacc as bacc
    from concourse.bass_utils import run_bass_kernel_spmd

    a = {k: np.asarray(v) for k, v in inputs.items()}

    w_in = a["w_in"][0]
    def cols(w):
        return np.ascontiguousarray(w.reshape(DC, P, P).transpose(1, 0, 2)).reshape(P, D)
    wq = w_in[:, 512:1024].reshape(D, 2, HPK, HD).transpose(0, 2, 1, 3).reshape(D, 512)
    units = [cols(w_in[:, 1024:1152]), cols(w_in[:, 1152:1280])]
    units += [cols(w_in[:, n * P:(n + 1) * P]) for n in range(4)]
    units += [cols(wq[:, n * P:(n + 1) * P]) for n in range(4)]
    units += [cols(w_in[:, 1280 + n * P:1280 + (n + 1) * P]) for n in range(16)]
    up_p = a["w_up_pool"][0].reshape(4, P, DC, P)
    up_a = a["w_up_attn"][0].reshape(2, HPK, HD, D).transpose(1, 0, 2, 3).reshape(4, P, DC, P)
    both = np.concatenate([up_p, up_a], axis=0)
    units += [both[:, :, j].transpose(1, 0, 2).reshape(P, D) for j in range(DC)]
    wo = a["w_out"][0].reshape(2, 4, P, 4, 256)
    units += [wo[h, :, :, q].transpose(1, 0, 2).reshape(P, D) for q in range(4) for h in range(2)]
    w_a = np.ascontiguousarray(np.stack(units))
    wqry = a["peer_w_query"][0]
    keys = a["peer_sub_keys"][0].reshape(2 * HEADS, P, P)
    w_q = np.stack([np.concatenate([cols(wqry[:, n * P:(n + 1) * P]), keys[n].T], axis=1) for n in range(16)])

    x = a["x_prompt"][0]
    xT = x.reshape(GROUPS, GN, DC, P).transpose(0, 3, 2, 1)
    xs = a["x_sample"].reshape(SAMP, D)
    extra = np.concatenate([a["meta_tokens"], xs], axis=0).reshape(X0, DC, P).transpose(2, 1, 0)
    sinks = a["attn_sinks"][0]
    sink_rows = np.broadcast_to(sinks.reshape(1, 2, 1, HPK, 1, 1), (2, 2, 2, HPK, DSEQ, 2)).reshape(P, 2)

    dist = 255 - np.arange(384)
    n = np.maximum(dist, 0)
    large = 16 + (np.log(np.maximum(n, 16).astype(np.float32) / 16) / np.log(8.0) * 16).astype(np.int32)
    bucket = np.where(n < 16, n, np.minimum(large, 31))
    inside = (dist >= 0) & (dist < WIN)
    onehot = ((np.arange(32)[:, None] == bucket[None, :]) & inside[None, :]).astype(np.float32)
    linemask = np.broadcast_to(np.where(inside, 0.0, NEG).astype(np.float32), (HEADS, 384))
    sel = np.zeros((DSEQ, HEADS, P), np.float32)
    smask = np.full((P, 2, 288), NEG, np.float32)
    for pr in range(2):
        for kv in range(2):
            for s in range(2):
                for h in range(HPK):
                    for i in range(DSEQ):
                        r = pr * 64 + kv * 32 + s * 16 + h * 4 + i
                        sel[i, kv * HPK + h, r] = 1.0
                        for t in range(2):
                            smask[r, t, s * WIN:(s + 1) * WIN] = 0.0
                            q = 2 * (2 * t + pr) + s
                            smask[r, t, 256 + q * DSEQ:256 + (q + 1) * DSEQ] = 0.0

    arrays = {
        "xT": xT, "xT_extra": extra, "x_rows": x.reshape(GROUPS * BLK, P, D), "xs_rows": xs, "w_a": w_a, "w_q": w_q,
        "uv": np.concatenate([a["peer_u"][0], a["peer_v"][0]], axis=1), "table": a["rel_bias_table"],
        "sinks": sinks, "sink_rows": sink_rows,
        "w_mix": a["w_pool_mix"][0].transpose(1, 0, 2), "pool_scale": a["pool_scale"][0].reshape(4, P).T,
        "ln1_g": a["ln1_g"][0], "ln1_b": a["ln1_b"][0], "ln2_g": a["ln2_g"][0], "ln2_b": a["ln2_b"][0],
        "ckT": a["cache_k"][0].reshape(SEQS, WIN, P).transpose(2, 0, 1),
        "cv_rows": a["cache_v"][0].reshape(SEQS, WIN, P).transpose(1, 0, 2),
        "cache_v": a["cache_v"][0].reshape(SEQS, WIN, P),
        "stT": a["state_pool"][0].reshape(SEQS, PSTATE, 4, P).transpose(3, 2, 0, 1),
        "ident": np.eye(P, dtype=np.float32), "flip": np.eye(P, dtype=np.float32)[::-1], "onehot": onehot,
        "linemask": linemask, "sel": sel, "smask": smask,
        "iota": np.broadcast_to(np.arange(TOPK, dtype=np.float32), (P, TOPK)),
        "sel4": np.tile(np.eye(SAMP, dtype=np.float32), (QUARTERS, 1)),
    }
    outs = {"y_prompt": (GROUPS * BLK, P, D), "y_sample": (SAMP, D), "k_prompt": (P, P), "v_prompt": (P, P),
            "pool_prompt": (P, 4, PSTATE), "k_sample": (P, SEQS, WIN), "v_sample": (SEQS, WIN, P),
            "pool_sample": (P, 4, SEQS, PSTATE)}
    nc = bacc.Bacc("TRN2", target_bir_lowering=False, num_devices=1)
    data = {"in_" + k: np.ascontiguousarray(v) for k, v in arrays.items()}
    args = [nc.dram_tensor(k, v.shape, mybir.dt.from_np(v.dtype), kind="ExternalInput").ap() for k, v in data.items()]
    args.append(nc.dram_tensor("line_scratch", (HEADS, 384), F32, kind="Internal").ap())
    args.append(nc.dram_tensor("score_scratch", (SAMP, 2048), F32, kind="Internal").ap())
    args += [nc.dram_tensor("out_" + k, s, F32, kind="ExternalOutput").ap() for k, s in outs.items()]
    layer_kernel(nc, *args)
    r = run_bass_kernel_spmd(nc, [data], core_ids=[0]).results[0]
    o = {k: r["out_" + k] for k in outs}
    return (o["y_prompt"].reshape(1, GROUPS * GN, D), o["y_sample"].reshape(SEQS, DSEQ, D),
            np.ascontiguousarray(o["k_prompt"].T).reshape(1, 1, P, 2, HD), o["v_prompt"].reshape(1, 1, P, 2, HD),
            np.ascontiguousarray(o["pool_prompt"].transpose(2, 1, 0)).reshape(1, 1, PSTATE, 512),
            np.ascontiguousarray(o["k_sample"].transpose(1, 2, 0)).reshape(1, SEQS, WIN, 2, HD),
            o["v_sample"].reshape(1, SEQS, WIN, 2, HD),
            np.ascontiguousarray(o["pool_sample"].transpose(2, 3, 1, 0)).reshape(1, SEQS, PSTATE, 512))
```

```python
from contextlib import ExitStack
from functools import partial

import concourse.bass as bass
from concourse import mybir

F32 = mybir.dt.float32
I32 = mybir.dt.int32
U32 = mybir.dt.uint32
ALU = mybir.AluOpType
ACT = mybir.ActivationFunctionType
AX = mybir.AxisListType

P = 128
D = 1024
DC = D // P
GROUPS = 4
BLK = 2
GN = BLK * P
META = 16
SAMP = 32
SEQS = 8
DSEQ = 4
X0 = META + SAMP
COLS = X0 + GN
HD = 64
HPK = 4
WIN = 128
HIST = 16
PSTATE = 15
SCALE = HD ** -0.5
ALPHA = 2.0 ** 0.25
EPS = 1e-5
NEG = -1e30
HEADS = 8
TOPK = 16
SLOTS = HEADS * TOPK
RING = 8
BODY = 2 * RING
BATCH = 4
BODIES = SLOTS // BODY
PE_SLOTS = [k for k in range(BODY) if k % BATCH != BATCH - 1]
PE_TILES = RING - RING // BATCH
DVE_TILES = RING // BATCH
QUARTERS = P // SAMP

WR = 4
POS_K, POS_V, POS_IN, POS_UP, POS_OUT, POS_QRY, POS_END = 0, 1, 2, 26, 34, 42, 60
HOLES = (58, 59)
UNITS = POS_END - len(HOLES)
N_IN = POS_UP - POS_IN
N_UP = POS_OUT - POS_UP
N_OUT = POS_QRY - POS_OUT
N_QRY = HOLES[0] - POS_QRY
FIRST_OVER_B = HEADS * 2 * P // (SAMP + GN)
PROJ = 2 + N_IN


def ordinal(pos):
    return pos if pos < HOLES[0] else pos - len(HOLES)


def loads_upto(pos):
    return sum(1 for n in range(pos % WR, pos + 1, WR) if n not in HOLES)


LOADS = [loads_upto(POS_END - WR + s) for s in range(WR)]


def wait(eng, sem, value):
    if not isinstance(value, int) or value > 0:
        eng.wait_ge(sem, value)


def hold(eng, sem, value):
    eng.wait_ge(sem, value)
    eng.nop(nofuse=True)


def nth(g, b):
    return b + 1 if isinstance(g, int) and g == 0 else g * BLK + (b + 2)


def first(g):
    return isinstance(g, int) and g == 0


def batches(half):
    n = BODY // BATCH // 2
    return range(2 * n) if half is None else range(half * n, half * n + n)


QUERY_STEPS = ((0, 1, -1, -2), (2, 3, -3, -4))


def layer_kernel(nc, xT, xT_extra, x_rows, xs_rows, w_a, w_q, uv, table, sinks, sink_rows, w_mix, pool_scale,
                 ln1_g, ln1_b, ln2_g, ln2_b, ckT, cv_rows, cache_v, stT,
                 ident_c, flip_c, onehot_c, linemask_c, sel_c, smask_c, iota_c, sel4_c,
                 line_scratch, score_scratch, y_prompt, y_sample, k_prompt, v_prompt, pool_prompt, k_sample, v_sample, pool_sample):
    with ExitStack() as ctx:
        def sb(name, shape, dt=F32):
            return ctx.enter_context(nc.sbuf_tensor(name, shape, dt))

        def sem(name):
            return ctx.enter_context(nc.semaphore(name))

        ident = sb("ident", [P, P])
        sel4 = sb("sel4", [P, SAMP])
        zeros = sb("zeros", [P, P])
        iota = sb("iota", [P, TOPK])
        bias = sb("bias", [P, HEADS, 2 * P])
        sink = sb("sink", [P, HEADS])
        wmix = sb("wmix", [P, 4, P])
        pscale = sb("pscale", [P, 4])
        ln2g = sb("ln2g", [P, D])
        ln2b = sb("ln2b", [P, D])
        wring = sb("wring", [P, WR, D + P])
        xm = sb("xm", [P, DC, COLS])
        poolT = sb("poolT", [P, 4, HIST + GN])
        pooled = sb("pooled", [P, 4, SAMP + GN])
        qT = sb("qT", [P, 4, SAMP + GN])
        kT = sb("kT", [P, P + GN])
        vR = sb("vR", [P, BLK + 1, P])
        big = sb("big", [P, 16 * (SAMP + GN)])
        att = sb("att", [P, 3072])
        amx = sb("amx", [P, 2, 4])
        anm = sb("anm", [P, 2, 4])
        ads = sb("ads", [P, 2, 4])
        aden = sb("aden", [P, 2, 4])
        stats = sb("stats", [P, 12])
        moments = sb("moments", [P, 4])
        stats2 = sb("stats2", [P, 12])
        moments2 = sb("moments2", [P, 4])
        qyT = sb("qyT", [P, 2, SAMP + GN])
        x1n = sb("x1n", [P, BLK, D])
        x1c = sb("x1c", [P, BLK, D])
        xs4 = sb("xs4", [P, D])
        x1s = xs4[0:SAMP, :]
        acc_v = sb("acc_v", [P, D])
        idxn = sb("idxn", [P, BLK, SLOTS], I32)
        idxc = sb("idxc", [P, BLK, SLOTS], I32)
        idx4 = sb("idx4", [P, SLOTS // QUARTERS], I32)
        gaten = sb("gaten", [P, BLK, SLOTS])
        gatec = sb("gatec", [P, BLK, SLOTS])
        gate4 = sb("gate4", [P, SLOTS // QUARTERS])
        idx8 = [sb(f"idx8_{n}", [P, RING], I32) for n in range(2)]
        tops = sb("tops", [P, HEADS, 2, TOPK])
        topi = sb("topi", [P, HEADS, 2, TOPK], U32)
        topf = sb("topf", [P, HEADS, 2, TOPK])
        bests = sb("bests", [P, HEADS, TOPK])
        bestj = sb("bestj", [P, HEADS, TOPK], U32)
        jpart = sb("jpart", [P, SLOTS], U32)
        jf = sb("jf", [P, SLOTS])
        ipart = sb("ipart", [P, 2, SLOTS])
        gsum = sb("gsum", [P, HEADS])
        hdot = sb("hdot", [P, 2, BATCH])
        hgelu = sb("hgelu", [P, 2, BATCH])
        hw = sb("hw", [P, 2, BATCH])
        diag = sb("diag", [P, RING, P])
        ring = sb("ring", [P, RING, 2 * D])

        def early(tile, off, *dims):
            size = 1
            for d in dims:
                size *= d
            ap = ring[:, tile, off:off + size]
            if len(dims) == 2:
                return ap.rearrange("p (a b) -> p a b", a=dims[0])
            if len(dims) == 3:
                return ap.rearrange("p (a b c) -> p a b c", a=dims[0], b=dims[1])
            return ap

        kX = early(0, 0, SEQS, WIN + DSEQ)
        sPool = early(1, 0, 4, SEQS, PSTATE + DSEQ)
        sT1 = early(1, 640, SEQS, PSTATE + DSEQ)
        sT2 = early(1, 832, SEQS, PSTATE + DSEQ)
        sQ = early(1, 1024, 4, 32)
        sBias = early(2, 0, 2, 288)
        sS = early(2, 576, 2, 288)
        sPT = early(2, 1152, 2, 384)
        sV = early(1, 1152, P)
        vX = early(3, 0, SEQS, P)
        sMask = early(3, 1024, 2, 288)
        sSmall = early(3, 1600, 16)
        sSink = early(3, 1620, 2)
        flip = early(4, 0, P)
        onehot = early(4, 128, 384)
        lmask = early(4, 512, 384)
        line = early(4, 896, 384)
        tab = early(4, 1280, HEADS)
        sel = early(5, 0, HEADS, P)
        sScores = att[0:SAMP, 0:2048]

        def scores_of(b):
            return big[:, b * 2048:(b + 1) * 2048]

        gates = big[:, :].rearrange("p (a b) -> p a b", a=16)
        S = [att[:, 0:1024], att[:, 1024:2048]]
        PT = att[:, 2048:3072]
        t1 = att[:, 0:4 * (HIST + GN)].rearrange("p (a b) -> p a b", a=4)
        t2 = att[:, 4 * (HIST + GN):8 * (HIST + GN)].rearrange("p (a b) -> p a b", a=4)
        ln1g, ln1b = att[:, 0:1024], att[:, 1024:2048]

        pj = [ctx.enter_context(nc.psum_tensor(f"pj{n}", [P, 512], F32)) for n in range(2)]
        acc = ctx.enter_context(nc.psum_tensor("acc", [P, D], F32))
        wide = [ctx.enter_context(nc.psum_tensor(f"wide{n}", [P, D], F32)) for n in range(2)]

        consts = sem("consts")
        bias_in = sem("bias_in")
        early_in = sem("early_in")
        cleared = sem("cleared")
        line_ps, line_sb, line_st, line_ld = sem("line_ps"), sem("line_sb"), sem("line_st"), sem("line_ld")
        bias_ps, bias_sb, sbias_ps, sbias_sb = sem("bias_ps"), sem("bias_sb"), sem("sbias_ps"), sem("sbias_sb")
        w_in_sem = [sem(f"w_tile{n}") for n in range(WR)]
        xt_in = sem("xt_in")
        xr_in = sem("xr_in")
        xs_in = sem("xs_in")
        ln1_in = sem("ln1_in")
        unit_done = sem("unit_done")
        proj_evac = sem("proj_evac")
        gate_sig = sem("gate_sig")
        pool_ready = sem("pool_ready")
        mix_done, mix_evac = sem("mix_done"), sem("mix_evac")
        score_ready, max_ready, exp_done = sem("score_ready"), sem("max_ready"), sem("exp_done")
        p_ready, pt_ready, pt_evac = sem("p_ready"), sem("pt_ready"), sem("pt_evac")
        o_ready, o_evac = sem("o_ready"), sem("o_evac")
        sq_ready, s_score, s_max, s_exp, s_p = sem("sq_ready"), sem("s_score"), sem("s_max"), sem("s_exp"), sem("s_p")
        s_pt, s_pt_evac, s_o, s_o_evac = sem("s_pt"), sem("s_pt_evac"), sem("s_o"), sem("s_o_evac")
        up_read, m_ready = sem("up_read"), sem("m_ready")
        y_read, ln1_var, ln1_std, x1_ready = sem("y_read"), sem("ln1_var"), sem("ln1_std"), sem("x1_ready")
        xt_ready, xt_evac = sem("xt_ready"), sem("xt_evac")
        qry_ready, qry_evac, sc_evac = sem("qry_ready"), sem("qry_evac"), sem("sc_evac")
        gmax_ready, gexp_done = sem("gmax_ready"), sem("gexp_done")
        cur_ready = [sem(f"cur_ready{n}") for n in range(BLK)]
        samp_scores, samp_got, samp_in = sem("samp_scores"), sem("samp_got"), sem("samp_in")
        x4_in = sem("x4_in")
        carried = sem("carried")
        idx_ready = sem("idx_ready")
        gathered = [sem(f"gathered{n}") for n in range(RING)]
        slot_free = sem("slot_free")
        vslot_free = sem("vslot_free")
        accv_ready = sem("accv_ready")
        dot_done, gelu_done, w_ready, diag_done = sem("dot_done"), sem("gelu_done"), sem("w_ready"), sem("diag_done")
        acc_done, acc_read = sem("acc_done"), sem("acc_read")
        ln2_var, ln2_std, y_ready = sem("ln2_var"), sem("ln2_std"), sem("y_ready")
        y_out = [sem(f"y_out{n}") for n in range(BLK)]
        ys_out = sem("ys_out")
        states_out = sem("states_out")
        early_out = sem("early_out")
        score_out = sem("score_out")
        first_ready = [sem(f"first_ready{n}") for n in range(BLK)]

        N_CONSTS = 9
        EARLY_STORES = 13

        def lo(g, width):
            return 0 if first(g) else width

        block = ctx.enter_context(nc.Block())

        @block.sync
        def _(sp):
            def load_unit(g, pos, it=0):
                before, done = pos - WR, g * UNITS + it * WR
                if before < 0:
                    before, done = before + POS_END, done - UNITS
                    before -= WR if before in HOLES else 0
                if pos >= WR or not first(g):
                    wait(sp, unit_done, done + (ordinal(before) + 1))
                s = pos % WR
                if pos >= POS_QRY:
                    dst, src = wring[:, s, :], w_q[bass.ds(it * WR + (pos - POS_QRY), 1)]
                else:
                    dst, src = wring[:, s, 0:D], w_a[bass.ds(it * WR + ordinal(pos), 1)]
                sp.dma_start(dst, src.rearrange("o p f -> (o p) f")).then_inc(w_in_sem[s], 16)

            def load_loop(g, pos, n):
                with nc.sync.Fori(0, n // WR) as it:
                    for k in range(WR):
                        load_unit(g, pos + k, it)

            def load_first(g):
                wait(sp, unit_done, g * UNITS)
                if first(g):
                    sp.dma_start(xm[:, :, 0:X0], xT_extra).then_inc(xt_in, 16)
                    sp.dma_start(xm[:, :, X0:COLS], xT[0]).then_inc(xt_in, 16)
                else:
                    sp.dma_start(xm[:, :, X0:COLS],
                                 xT[bass.ds(g, 1)].rearrange("o p c n -> (o p) c n")).then_inc(xt_in, 16)
                for pos in range(POS_K, WR):
                    load_unit(g, pos)

            def load_rest(g):
                first_loop = WR + (POS_UP - WR) % WR
                for pos in range(WR, first_loop):
                    load_unit(g, pos)
                load_loop(g, first_loop, POS_UP - first_loop)
                for b in range(BLK):
                    wait(sp, cur_ready[b], g)
                    sp.dma_start(x1n[:, b, :],
                                 x_rows[bass.ds(g * BLK + b, 1)].rearrange("o p d -> (o p) d")).then_inc(xr_in, 16)
                load_loop(g, POS_UP, N_UP)
                wait(sp, o_ready, g * 4 + 4)
                wait(sp, s_pt, 2)
                sp.dma_start(ln1g, ln1_g.partition_broadcast(P)).then_inc(ln1_in, 16)
                sp.dma_start(ln1b, ln1_b.partition_broadcast(P)).then_inc(ln1_in, 16)
                load_loop(g, POS_OUT, N_OUT)
                if first(g):
                    store_states()
                else:
                    store_block(g, 0)
                load_loop(g, POS_QRY, N_QRY)

            def store_states():
                sp.dma_start(v_sample[:, 0:WIN - DSEQ, :], cache_v[:, DSEQ:WIN, :]).then_inc(states_out, 16)
                sp.wait_ge(early_in, 15 * 16)
                sp.wait_ge(proj_evac, PROJ)
                sp.dma_start(k_sample, kX[:, :, DSEQ:DSEQ + WIN]).then_inc(early_out, 16)
                for s in range(SEQS):
                    sp.dma_start(v_sample[s, WIN - DSEQ:WIN, :], sV[DSEQ * s:DSEQ * s + DSEQ]).then_inc(early_out, 16)
                for c in range(4):
                    sp.dma_start(pool_sample[:, c], sPool[:, c, :, DSEQ:DSEQ + PSTATE]).then_inc(early_out, 16)

            def store_block(g, b):
                wait(sp, y_ready, (g - 1) * BLK + (b + 1))
                dst = y_prompt[bass.ds((g - 1) * BLK + b, 1)].rearrange("o p d -> (o p) d")
                sp.dma_start(dst, x1c[:, b, :]).then_inc(y_out[b], 16)

            for dst, src in ((onehot[0:32], onehot_c), (lmask[0:HEADS], linemask_c), (tab[0:32], table),
                             (sel[0:DSEQ], sel_c)):
                sp.dma_start(dst, src).then_inc(bias_in, 16)
            load_first(0)
            sp.wait_ge(line_sb, 1)
            sp.dma_start(line_scratch, line[0:HEADS]).then_inc(line_st, 16)
            for dst, src in ((ident[:, :], ident_c), (iota[:, :], iota_c),
                             (sink[:, :], sinks.partition_broadcast(P)), (wmix[:, :, :], w_mix),
                             (pscale[:, :], pool_scale), (ln2g[:, :], ln2_g.partition_broadcast(P)),
                             (ln2b[:, :], ln2_b.partition_broadcast(P)), (flip, flip_c), (sel4[:, :], sel4_c)):
                sp.dma_start(dst, src).then_inc(consts, 16)
            sp.wait_ge(line_st, 16)
            window = bass.AP(line_scratch.tensor, 0, [[1, P], [384, HEADS], [1, 2 * P]])
            sp.dma_start(att[:, 0:2048].rearrange("p (h j) -> p h j", h=HEADS), window).then_inc(line_ld, 16)
            for s in range(SEQS):
                sp.dma_start(kX[:, s, 0:WIN], ckT[:, s, :]).then_inc(early_in, 16)
            sp.dma_start(vX, cv_rows).then_inc(early_in, 16)
            for c in range(4):
                sp.dma_start(sPool[:, c, :, 0:PSTATE], stT[:, c]).then_inc(early_in, 16)
            sp.dma_start(sMask, smask_c).then_inc(early_in, 16)
            sp.dma_start(sSink, sink_rows).then_inc(early_in, 16)
            sp.dma_start(x1s, xs_rows).then_inc(xs_in, 16)
            load_rest(0)
            sp.wait_ge(sc_evac, N_QRY)
            sp.dma_start(score_scratch, sScores).then_inc(score_out, 16)
            sp.wait_ge(x1_ready, BLK + 1)
            for q in range(1, QUARTERS):
                sp.dma_start(xs4[SAMP * q:SAMP * (q + 1), :], x1s).then_inc(x4_in, 16)

            load_first(1)
            with nc.sync.Fori(1, GROUPS - 1) as g:
                load_rest(g)
                load_first(g + 1)
                store_block(g, 1)
            load_rest(GROUPS - 1)
            store_block(GROUPS - 1, 1)
            sp.wait_ge(carried, GROUPS)
            sp.dma_start(k_prompt, kT[:, 0:P]).then_inc(states_out, 16)
            sp.dma_start(v_prompt, vR[:, 0, :]).then_inc(states_out, 16)
            sp.dma_start(pool_prompt, poolT[:, :, HIST - PSTATE:HIST]).then_inc(states_out, 16)
            sp.wait_ge(early_out, 16 * EARLY_STORES)
            sp.wait_ge(score_out, 16)
            sp.wait_ge(cur_ready[0], GROUPS)
            sp.dma_start(big[0:SAMP, 0:2048], score_scratch).then_inc(samp_scores, 16)
            sp.wait_ge(samp_got, 1)
            n = SLOTS // QUARTERS
            for q in range(QUARTERS):
                rows = slice(SAMP * q, SAMP * (q + 1))
                sp.dma_start(idx4[rows, :], idxn[0:SAMP, 0, n * q:n * (q + 1)]).then_inc(samp_in, 16)
                sp.dma_start(gate4[rows, :], gaten[0:SAMP, 0, n * q:n * (q + 1)]).then_inc(samp_in, 16)
            for b in range(BLK):
                store_block(GROUPS, b)
            sp.wait_ge(y_ready, GROUPS * BLK + 1)
            sp.dma_start(y_sample, x1s).then_inc(ys_out, 16)
            sp.wait_ge(states_out, 64)
            for b in range(BLK):
                sp.wait_ge(y_out[b], 16 * (GROUPS + b))
            sp.wait_ge(ys_out, 16)

        @block.gpsimd
        def _(pool):
            def gather_block(n, idx, bodies, ready=None):
                with nc.gpsimd.Fori(0, bodies) as it:
                    for half in range(2):
                        if ready and half == 1:
                            hold(pool, *ready)
                        nc.gpsimd.tensor_copy(idx8[half][:, :], idx[:, bass.ds(it * BODY + half * RING, RING)])\
                            .then_inc(idx_ready, 1)
                        hold(pool, idx_ready, n * (SLOTS // RING) + it * 2 + (half + 1))
                        for k in range(RING):
                            if k % BATCH < BATCH - 1:
                                hold(pool, slot_free, n * (BODIES * len(PE_SLOTS)) + it * len(PE_SLOTS)
                                     + (half * PE_TILES + k - k // BATCH + 1))
                            else:
                                hold(pool, vslot_free, n * (SLOTS // BATCH) + it * (BODY // BATCH)
                                     + (half * DVE_TILES + k // BATCH + 1))
                            pool.indirect_dma_start(
                                ring[:, k, :], None, uv,
                                bass.IndirectOffsetOnAxis(ap=idx8[half][:, k:k + 1], axis=0))\
                                .then_inc(gathered[k], 16)

            def gather_pair(g):
                for b in range(BLK):
                    hold(pool, first_ready[b], g)
                    gather_block((g - 1) * BLK + b, idxc[:, b, :], BODIES, (cur_ready[b], g))

            pool.wait_ge(early_out, 16 * EARLY_STORES)
            with nc.gpsimd.Fori(1, GROUPS) as g:
                gather_pair(g)
            gather_pair(GROUPS)
            pool.wait_ge(samp_in, 16 * 2 * QUARTERS)
            gather_block(GROUPS * BLK, idx4[:, :], BODIES // QUARTERS)

        @block.scalar
        def _(act):
            copy = ACT.Copy

            def position_bias():
                for n in range(2):
                    act.wait_ge(bias_ps, n + 1)
                    nc.scalar.activation(bias[:, 4 * n:4 * n + 4, :].rearrange("p h j -> p (h j)"), wide[n][:, :],
                                         copy).then_inc(bias_sb, 1)

            def evac(g, n, src, dst, also=()):
                act.wait_ge(unit_done, g * UNITS + (n + 1))
                for s, d in also:
                    nc.scalar.activation(d, s, copy)
                nc.scalar.activation(dst, src, copy).then_inc(proj_evac, 1)

            def exps(g, i):
                act.wait_ge(max_ready, g * 4 + (i + 1))
                for h in range(HPK):
                    s = S[i % 2][:, h * 256:(h + 1) * 256]
                    nc.scalar.activation(s, s, ACT.Exp, bias=anm[:, i % 2, h:h + 1], accum_out=aden[:, i % 2, h:h + 1])
                nc.scalar.activation(ads[:, i % 2, :], ads[:, i % 2, :], ACT.Exp).then_inc(exp_done, 1)

            def gate_units(g, units):
                for c in units:
                    if c == FIRST_OVER_B and not first(g):
                        act.wait_ge(cur_ready[1], g)
                    evac(g, 10 + c, pj[c % 2][:, META if first(g) else X0:COLS], gates[:, c, lo(g, SAMP):])

            def attention_output(g, i):
                b, kv = divmod(i, 2)
                act.wait_ge(pt_ready, g * 4 + (i + 1))
                wait(act, o_ready, g * 4 + i)
                nc.scalar.activation(PT, wide[1][:, :], copy).then_inc(pt_evac, 1)
                act.wait_ge(o_ready, g * 4 + (i + 1))
                rows = slice(HD * kv, HD * kv + HD)
                nc.scalar.activation(qT[rows, :, SAMP + b * P:SAMP + (b + 1) * P],
                                     wide[0][rows, 0:512].rearrange("p (c n) -> p c n", c=4), copy)\
                    .then_inc(o_evac, 1)

            def sample_attention():
                act.wait_ge(s_max, 1)
                for t in range(2):
                    nc.scalar.activation(sS[:, t, :], sS[:, t, :], ACT.Exp, bias=sSmall[:, 2 + t:3 + t],
                                         accum_out=sSmall[:, 4 + t:5 + t])
                nc.scalar.activation(sSmall[:, 6:8], sSmall[:, 6:8], ACT.Exp).then_inc(s_exp, 1)
                for t in range(2):
                    act.wait_ge(s_pt, t + 1)
                    nc.scalar.activation(sPT[:, t, 0:256], wide[1][:, t * 512:t * 512 + 256], copy)
                    nc.scalar.activation(sPT[0:SAMP, t, 256:384], wide[1][0:SAMP, t * 512 + 256:t * 512 + 384],
                                         copy).then_inc(s_pt_evac, 1)
                act.wait_ge(s_o, 1)
                for kv in range(2):
                    rows = slice(HD * kv, HD * kv + HD)
                    for c in range(HPK):
                        src = acc[rows, 0:P].rearrange("p (s c i) -> p s c i", s=SEQS, c=HPK)[:, :, c, :]
                        nc.scalar.activation(qT[rows, c, 0:SAMP].rearrange("p (s i) -> p s i", s=SEQS), src, copy)\
                            .then_inc(s_o_evac, 1)

            def units_k_v(g):
                if first(g):
                    evac(0, 0, pj[0][:, X0:COLS], kT[:, P:P + GN],
                         also=((pj[0][:, 0:META], kT[:, 0:META]),
                               (pj[0][:, META:X0].rearrange("p (s i) -> p s i", s=SEQS), kX[:, :, WIN:WIN + DSEQ])))
                    evac(0, 1, pj[1][:, 0:GN], vR[:, 1:1 + BLK, :].rearrange("p b n -> p (b n)"),
                         also=((pj[1][0:META, 384:512], vR[0:META, 0, :]), (pj[1][0:SAMP, 256:384], sV[0:SAMP])))
                else:
                    act.wait_ge(carried, g)
                    evac(g, 0, pj[0][:, X0:COLS], kT[:, P:P + GN])
                    evac(g, 1, pj[1][:, 0:GN], vR[:, 1:1 + BLK, :].rearrange("p b n -> p (b n)"))

            def units_pool(g, chunks):
                for c in chunks:
                    if first(g):
                        evac(0, 2 + c, pj[c % 2][:, X0:COLS], poolT[:, c, HIST:],
                             also=((pj[c % 2][:, 0:META], poolT[:, c, 0:META]),
                                   (pj[c % 2][:, META:X0].rearrange("p (s i) -> p s i", s=SEQS),
                                    sPool[:, c, :, PSTATE:])))
                    else:
                        evac(g, 2 + c, pj[c % 2][:, X0:COLS], poolT[:, c, HIST:])

            def units_q(g, chunks):
                for c in chunks:
                    evac(g, 6 + c, pj[c % 2][:, META if first(g) else X0:COLS], qT[:, c, lo(g, SAMP):])

            def mix(g):
                act.wait_ge(mix_done, g + 1)
                act.wait_ge(consts, 16 * N_CONSTS)
                for c, ps in enumerate((pj[0], pj[1], wide[1][:, 0:512], wide[1][:, 512:1024])):
                    nc.scalar.activation(pooled[:, c, lo(g, SAMP):], ps[:, META if first(g) else X0:COLS], copy,
                                         scale=pscale[:, c:c + 1]).then_inc(mix_evac, 1)

            def sigmoids(g, half):
                for branch in range(2):
                    part = gates[:, 8 * branch + 4 * half:8 * branch + 4 * half + 4, lo(g, SAMP):]
                    nc.scalar.activation(part, part, ACT.Sigmoid).then_inc(gate_sig, 1)

            def norm1(g, b):
                act.wait_ge(ln1_var, nth(g, b))
                rows = P if b < BLK else SAMP
                nc.scalar.activation(moments[0:rows, 2:3], moments[0:rows, 1:2], ACT.Sqrt).then_inc(ln1_std, 1)

            def x1_transposes(g):
                for b in range(BLK + first(g)):
                    act.wait_ge(xt_ready, nth(g, b))
                    if b < BLK:
                        nc.scalar.activation(xm[:, :, X0 + b * P:X0 + (b + 1) * P],
                                             wide[b][:, :].rearrange("p (c n) -> p c n", c=DC), copy)\
                            .then_inc(xt_evac, 1)
                    else:
                        nc.scalar.activation(xm[:, :, META:X0],
                                             acc[:, 0:DC * SAMP].rearrange("p (c n) -> p c n", c=DC), copy)\
                            .then_inc(xt_evac, 1)

            def queries(g, it, half):
                for k in QUERY_STEPS[half]:
                    if k >= 0:
                        act.wait_ge(qry_ready, g * N_QRY + it * WR + (k + 1))
                        nc.scalar.activation(qyT[:, k % 2, lo(g, SAMP):],
                                             pj[k % 2][:, META if first(g) else X0:COLS], copy)\
                            .then_inc(qry_evac, 1)
                    else:
                        u = -k - 1
                        act.wait_ge(unit_done, g * UNITS + it * WR + (ordinal(POS_QRY) + u + 1))
                        ps = wide[u // 2][:, (u % 2) * 512:(u % 2) * 512 + 384]
                        if first(g):
                            nc.scalar.activation(sScores[:, bass.ds(it * (WR * P) + u * P, P)],
                                                 ps[0:SAMP, 256:384], copy)
                        nc.scalar.activation(big[:, bass.ds(it * (WR * P) + u * P, P)], ps[:, 0:P], copy)
                        nc.scalar.activation(big[:, bass.ds(it * (WR * P) + (2048 + u * P), P)], ps[:, P:2 * P],
                                             copy).then_inc(sc_evac, 1)

            def gate_exp(gate, count):
                act.wait_ge(gmax_ready, count)
                nc.scalar.activation(gate, gate, ACT.Exp).then_inc(gexp_done, 1)

            def slots(n, it, half=None, eye=ident, width=P):
                for m in batches(half):
                    act.wait_ge(dot_done, n * SLOTS + it * BODY + BATCH * (m + 1))
                    nc.scalar.activation(hgelu[:, m % 2, :], hdot[:, m % 2, :], ACT.Gelu).then_inc(gelu_done, 1)
                    act.wait_ge(w_ready, n * (SLOTS // BATCH) + it * (BODY // BATCH) + (m + 1))
                    for j in range(BATCH - 1):
                        act.wait_ge(slot_free, n * (BODIES * len(PE_SLOTS)) + it * len(PE_SLOTS)
                                    + (m * (BATCH - 1) + j + 1))
                        nc.scalar.activation(diag[:, (m * BATCH + j) % RING, 0:width], eye[:, :], copy,
                                             scale=hw[:, m % 2, j:j + 1]).then_inc(diag_done, 1)

            def copy_sum(n, x):
                act.wait_ge(acc_done, n + 2)
                nc.scalar.activation(x, acc[0:x.shape[0], :], copy).then_inc(acc_read, 1)

            def norm2(n, rows=P):
                act.wait_ge(ln2_var, n + 1)
                nc.scalar.activation(moments2[0:rows, 2:3], moments2[0:rows, 1:2], ACT.Sqrt).then_inc(ln2_std, 1)

            def rounds(g, body):
                body(0, 0, 0)
                units_k_v(g)
                if first(g):
                    position_bias()
                units_pool(g, range(0, 1))
                body(0, 0, 1)
                units_pool(g, range(1, 4))
                body(0, 1, 0)
                units_q(g, range(0, 2))
                body(0, 1, 1)
                units_q(g, range(2, 4))
                for i in range(4):
                    body(0, 2 + i, 0)
                    if i == 0 and not first(g):
                        gate_exp(gaten[:, 1, :], g * BLK)
                    exps(g, i)
                    gate_units(g, range(4 * i, 4 * i + 2))
                    body(0, 2 + i, 1)
                    gate_units(g, range(4 * i + 2, 4 * i + 4))
                    attention_output(g, i)
                if first(g):
                    sample_attention()
                body(0, 6, 0)
                mix(g)
                sigmoids(g, 0)
                body(0, 6, 1)
                sigmoids(g, 1)
                body(0, 7, 0)
                body(0, 7, 1)
                if not first(g):
                    copy_sum((g - 1) * BLK, x1c[:, 0, :])
                body(1, 0, 0)
                if not first(g):
                    norm2((g - 1) * BLK)
                body(1, 0, 1)
                body(1, 1, 0)
                norm1(g, 0)
                body(1, 1, 1)
                norm1(g, 1)
                if first(g):
                    norm1(g, 2)
                x1_transposes(g)
                with nc.scalar.Fori(0, N_QRY // WR) as it:
                    for half in range(2):
                        body(1, it + 2, half)
                        queries(g, it, half)
                body(1, 6, 0)
                body(1, 6, 1)
                gate_exp(gaten[:, 0, :], g * BLK + 1)
                body(1, 7, 0)
                body(1, 7, 1)
                if not first(g):
                    copy_sum((g - 1) * BLK + 1, x1c[:, 1, :])
                    norm2((g - 1) * BLK + 1)

            rounds(0, lambda b, it, half: None)
            with nc.scalar.Fori(1, GROUPS) as g:
                rounds(g, lambda b, it, half: slots((g - 1) * BLK + b, it, half))
            n = (GROUPS - 1) * BLK
            slots(n, 0)
            slots(n, 1)
            gate_exp(gaten[:, 1, :], GROUPS * BLK)
            slots(n, 2)
            with nc.scalar.Fori(3, BODIES - 1) as it:
                slots(n, it)
            gate_exp(gaten[0:SAMP, 0, :], GROUPS * BLK + 1)
            slots(n, BODIES - 1)
            copy_sum(n, x1c[:, 0, :])
            slots(n + 1, 0)
            norm2(n)
            with nc.scalar.Fori(1, BODIES) as it:
                slots(n + 1, it)
            copy_sum(n + 1, x1c[:, 1, :])
            slots(n + 2, 0, eye=sel4, width=SAMP)
            norm2(n + 1)
            slots(n + 2, 1, eye=sel4, width=SAMP)
            copy_sum(n + 2, x1s)
            norm2(n + 2, SAMP)

        @block.tensor
        def _(pe):
            mm = nc.tensor.matmul

            def unit_in(g, pos, it=None):
                s = pos % WR
                v = g * (16 * LOADS[s]) + 16 * loads_upto(pos)
                pe.wait_ge(w_in_sem[s], v if it is None else v + it * 16)
                return wring[:, s, 0:D].rearrange("p (c n) -> p c n", c=DC)

            def chunk(g, pos, ps, c0, it=None):
                w = unit_in(g, pos, it)
                for c in range(DC):
                    m = mm(ps[:, c0:COLS], w[:, c, :], xm[:, c, c0:COLS], start=(c == 0), stop=(c == DC - 1))
                return m

            def bias_line():
                pe.wait_ge(bias_in, 4 * 16)
                mm(acc[0:HEADS, 0:384], tab[0:32], onehot[0:32], start=True, stop=True).then_inc(line_ps, 1)

            def position_bias():
                pe.wait_ge(consts, 16 * N_CONSTS)
                pe.wait_ge(line_ld, 16)
                for n in range(4):
                    m = mm(wide[n // 2][:, (n % 2) * 512:(n % 2) * 512 + 512], flip, att[:, n * 512:(n + 1) * 512],
                           start=True, stop=True)
                    if n % 2:
                        m.then_inc(bias_ps, 1)
                pe.wait_ge(bias_sb, 2)
                for h in range(HEADS):
                    m = mm(acc[:, 512:512 + WIN + DSEQ], sel[0:DSEQ, h, :], bias[0:DSEQ, h, 0:WIN + DSEQ],
                           start=(h == 0), stop=(h == HEADS - 1))
                m.then_inc(sbias_ps, 1)

            def attention_scores(g, i):
                b, kv = divmod(i, 2)
                rows = slice(HD * kv, HD * kv + HD)
                if i == 0:
                    pe.wait_ge(proj_evac, g * PROJ + 10)
                    wait(pe, sc_evac, g * N_QRY)
                else:
                    pe.wait_ge(o_evac, g * 4 + i)
                for c in range(HPK):
                    m = mm(wide[0][:, c * 256:(c + 1) * 256], qT[rows, c, SAMP + b * P:SAMP + (b + 1) * P],
                           kT[rows, b * P:b * P + 2 * P], start=True, stop=True)
                m.then_inc(score_ready, 1)

            def attention_output(g, i):
                b, kv = divmod(i, 2)
                rows = slice(HD * kv, HD * kv + HD)
                pe.wait_ge(p_ready, g * 4 + (i + 1))
                if i:
                    pe.wait_ge(pt_evac, g * 4 + i)
                for half in range(2):
                    for c in range(HPK):
                        at = half * 512 + c * P
                        m = mm(wide[1][:, at:at + P], S[i % 2][:, c * 256 + half * P:c * 256 + half * P + P],
                               ident[:, :], is_transpose=True, start=True, stop=True)
                m.then_inc(pt_ready, 1)
                pe.wait_ge(pt_evac, g * 4 + (i + 1))
                for half in range(2):
                    m = mm(wide[0][rows, 0:512], vR[:, b + half, HD * kv:HD * kv + HD],
                           PT[:, half * 512:half * 512 + 512], start=(half == 0), stop=(half == 1))
                m.then_inc(o_ready, 1)

            def gate_units(g, units):
                for c in units:
                    pe.wait_ge(proj_evac, g * PROJ + (10 + c - 1))
                    chunk(g, POS_IN + 8 + c, pj[c % 2], META if first(g) else X0).then_inc(unit_done, 1)

            def sample_attention():
                pe.wait_ge(sbias_sb, 1)
                pe.wait_ge(sq_ready, 1)
                pe.wait_ge(o_evac, 4)
                for t in range(2):
                    for q in range(4):
                        pair, kv = 2 * t + q // 2, q % 2
                        rows = slice(HD * kv, HD * kv + HD)
                        out = wide[0][32 * q:32 * q + 32, t * 512:t * 512 + 288]
                        for n in range(2):
                            mm(out[:, n * WIN:(n + 1) * WIN], sQ[rows, pair, :], kX[rows, 2 * pair + n, 0:WIN],
                               start=True, stop=True)
                        m = mm(out[:, 256:288], sQ[rows, pair, :], kX[rows, :, WIN:], start=True, stop=True)
                m.then_inc(s_score, 1)
                pe.wait_ge(s_p, 1)
                pe.wait_ge(pt_evac, 4)
                for t in range(2):
                    for n in range(2):
                        mm(wide[1][:, t * 512 + n * P:t * 512 + (n + 1) * P], sS[:, t, n * P:(n + 1) * P],
                           ident[:, :], is_transpose=True, start=True, stop=True)
                    mm(wide[1][0:SAMP, t * 512 + 256:t * 512 + 384], sS[:, t, 256:288], ident[:, :],
                       is_transpose=True, start=True, stop=True).then_inc(s_pt, 1)
                pe.wait_ge(s_pt_evac, 2)
                for pair in range(4):
                    for kv in range(2):
                        t, q = pair // 2, 2 * (pair % 2) + kv
                        rows = slice(HD * kv, HD * kv + HD)
                        out = acc[rows, pair * 32:pair * 32 + 32]
                        for n in range(2):
                            mm(out, vX[:, 2 * pair + n, HD * kv:HD * kv + HD],
                               sPT[:, t, n * P + 32 * q:n * P + 32 * q + 32], start=(n == 0), stop=False)
                        m = mm(out, sV[0:SAMP, HD * kv:HD * kv + HD], sPT[0:SAMP, t, 256 + 32 * q:256 + 32 * q + 32],
                               start=False, stop=True)
                m.then_inc(s_o, 1)

            def units_k_v(g):
                pe.wait_ge(xt_in, 32 if first(g) else g * 16 + 32)
                wait(pe, qry_evac, g * N_QRY)
                chunk(g, POS_K, pj[0], lo(g, X0)).then_inc(unit_done, 1)
                w = unit_in(g, POS_V)
                parts = [(pj[1][:, b * P:(b + 1) * P], X0 + b * P, X0 + (b + 1) * P) for b in range(BLK)]
                if first(g):
                    parts += [(pj[1][0:SAMP, 256:384], META, X0), (pj[1][0:META, 384:512], 0, META)]
                for out, a, z in parts:
                    for c in range(DC):
                        m = mm(out, xm[:, c, a:z], w[:, c, :], start=(c == 0), stop=(c == DC - 1))
                m.then_inc(unit_done, 1)

            def units_pool(g, chunks):
                for n in chunks:
                    pe.wait_ge(proj_evac, g * PROJ + (n + 1))
                    chunk(g, POS_IN + n, pj[n % 2], lo(g, X0)).then_inc(unit_done, 1)

            def units_q(g, chunks):
                for n in range(4 + chunks[0], 4 + chunks[-1] + 1):
                    pe.wait_ge(proj_evac, g * PROJ + (n + 1))
                    chunk(g, POS_IN + n, pj[n % 2], META if first(g) else X0).then_inc(unit_done, 1)

            def mix(g):
                c0 = META if first(g) else X0
                pe.wait_ge(pool_ready, g + 1)
                pe.wait_ge(proj_evac, g * PROJ + PROJ)
                pe.wait_ge(pt_evac, g * 4 + 4)
                for c, ps in enumerate((pj[0], pj[1], wide[1][:, 0:512], wide[1][:, 512:1024])):
                    m = mm(ps[:, c0:COLS], wmix[:, c, :], pooled[:, c, lo(g, SAMP):], start=True, stop=True)
                m.then_inc(mix_done, 1)

            def branches_ready(g):
                pe.wait_ge(mix_evac, g * 4 + 4)
                hold(pe, o_evac, g * 4 + 4)
                if first(g):
                    pe.wait_ge(s_o_evac, 8)

            def ups(g, it, half):
                c0 = META if first(g) else X0
                for k in (2 * half, 2 * half + 1):
                    w = unit_in(g, POS_UP + k, it)
                    pe.wait_ge(up_read, g * N_UP + it * WR + (k + 1))
                    pa, pb = (pj[0], pj[1]) if k % 2 == 0 else (wide[1][:, 0:512], wide[1][:, 512:1024])
                    for ps, w0, src in ((pa, 0, pooled), (pb, 4, qT)):
                        for c in range(4):
                            m = mm(ps[:, c0:COLS], w[:, w0 + c, :], src[:, c, lo(g, SAMP):],
                                   start=(c == 0), stop=(c == 3))
                    m.then_inc(unit_done, 1)

            def outs(g, it):
                hold(pe, m_ready, g * N_UP + N_UP)
                for k in range(WR):
                    s = (POS_OUT + k) % WR
                    unit_in(g, POS_OUT + k, it)
                    w = wring[:, s, 0:D].rearrange("p (c n) -> p c n", c=4)
                    for b in range(BLK + first(g)):
                        full = wide[b] if b < BLK else acc
                        rows = P if b < BLK else SAMP
                        a = X0 + b * P if b < BLK else META
                        out = full[0:rows, it * 512 + (k // 2) * 256:it * 512 + (k // 2 + 1) * 256]
                        for c in range(4):
                            m = mm(out, xm[:, (k % 2) * 4 + c, a:a + rows], w[:, c, :],
                                   start=(k % 2 == 0 and c == 0), stop=(k % 2 == 1 and c == 3))
                    m.then_inc(unit_done, 1)

            def x1_transposes(g):
                for b in range(BLK + first(g)):
                    pe.wait_ge(x1_ready, nth(g, b))
                    for c in range(DC):
                        if b < BLK:
                            m = mm(wide[b][:, c * P:(c + 1) * P], x1n[:, b, c * P:(c + 1) * P], ident[:, :],
                                   is_transpose=True, start=True, stop=True)
                        else:
                            m = mm(acc[:, c * SAMP:(c + 1) * SAMP], x1s[:, c * P:(c + 1) * P],
                                   ident[0:SAMP, 0:SAMP], is_transpose=True, start=True, stop=True)
                    m.then_inc(xt_ready, 1)
                hold(pe, xt_evac, nth(g, BLK - 1) + first(g))

            def queries(g, it, half):
                for k in QUERY_STEPS[half]:
                    if k >= 0:
                        if k >= 2:
                            pe.wait_ge(qry_evac, g * N_QRY + it * WR + (k - 1))
                        else:
                            wait(pe, qry_evac, g * N_QRY + it * WR)
                        chunk(g, POS_QRY + k, pj[k % 2], META if first(g) else X0, it=it).then_inc(qry_ready, 1)
                    else:
                        u = -k - 1
                        pe.wait_ge(qry_evac, g * N_QRY + it * WR + (u + 1))
                        wait(pe, sc_evac, g * N_QRY + it * WR)
                        keys = wring[:, (POS_QRY + u) % WR, D:D + P]
                        ps = wide[u // 2][:, (u % 2) * 512:(u % 2) * 512 + 384]
                        for b in range(BLK):
                            m = mm(ps[:, b * P:(b + 1) * P], qyT[:, u % 2, SAMP + b * P:SAMP + (b + 1) * P],
                                   keys, start=True, stop=True)
                        if first(g):
                            m = mm(ps[0:SAMP, 256:384], qyT[:, u % 2, 0:SAMP], keys, start=True, stop=True)
                        m.then_inc(unit_done, 1)

            def open_block(n, x, width=P):
                pe.wait_ge(acc_read, n + 1)
                for c in range(2):
                    mm(acc[0:width, c * 512:(c + 1) * 512], zeros[:, 0:width], x[:, c * 512:(c + 1) * 512],
                       start=True, stop=False)

            def slots(n, it, half=None, width=P):
                for r, k in enumerate(PE_SLOTS):
                    if k // BATCH not in batches(half):
                        continue
                    (pe.wait_ge if width == P else partial(hold, pe))(
                        diag_done, n * (BODIES * len(PE_SLOTS)) + it * len(PE_SLOTS) + (r + 1))
                    for c in range(2):
                        m = mm(acc[0:width, c * 512:(c + 1) * 512], diag[:, k % RING, 0:width],
                               ring[:, k % RING, D + c * 512:D + (c + 1) * 512], start=False, stop=False)
                    m.then_inc(slot_free, 1)

            def close_block(n, eye=ident, width=P):
                pe.wait_ge(accv_ready, n + 1)
                for c in range(2):
                    m = mm(acc[0:width, c * 512:(c + 1) * 512], eye[:, :], acc_v[:, c * 512:(c + 1) * 512],
                           start=False, stop=True)
                m.then_inc(acc_done, 1)

            def rounds(g, body):
                peer = not first(g)
                if peer:
                    pe.wait_ge(cur_ready[0], g)
                    open_block((g - 1) * BLK, x1c[:, 0, :])
                body(0, 0, 0)
                units_k_v(g)
                if first(g):
                    position_bias()
                units_pool(g, range(0, 1))
                body(0, 0, 1)
                units_pool(g, range(1, 4))
                body(0, 1, 0)
                units_q(g, range(0, 2))
                body(0, 1, 1)
                units_q(g, range(2, 4))
                attention_scores(g, 0)
                for i in range(4):
                    body(0, 2 + i, 0)
                    gate_units(g, range(4 * i, 4 * i + 2))
                    body(0, 2 + i, 1)
                    gate_units(g, range(4 * i + 2, 4 * i + 4))
                    attention_output(g, i)
                    if i < 3:
                        attention_scores(g, i + 1)
                if first(g):
                    sample_attention()
                mix(g)
                body(0, 6, 0)
                branches_ready(g)
                ups(g, 0, 0)
                body(0, 6, 1)
                ups(g, 0, 1)
                body(0, 7, 0)
                ups(g, 1, 0)
                body(0, 7, 1)
                if peer:
                    close_block((g - 1) * BLK)
                ups(g, 1, 1)
                if peer:
                    pe.wait_ge(cur_ready[1], g)
                    open_block((g - 1) * BLK + 1, x1c[:, 1, :])
                for half in range(2):
                    body(1, 0, half)
                    outs(g, half)
                body(1, 1, 0)
                body(1, 1, 1)
                x1_transposes(g)
                if first(g):
                    pe.sem_inc(slot_free, PE_TILES)
                with nc.tensor.Fori(0, N_QRY // WR) as it:
                    for half in range(2):
                        body(1, it + 2, half)
                        queries(g, it, half)
                for it in (6, 7):
                    body(1, it, 0)
                    body(1, it, 1)
                if peer:
                    close_block((g - 1) * BLK + 1)

            pe.wait_ge(cleared, 1)
            bias_line()
            rounds(0, lambda b, it, half: None)
            pe.sem_inc(acc_done, 1)
            with nc.tensor.Fori(1, GROUPS) as g:
                rounds(g, lambda b, it, half: slots((g - 1) * BLK + b, it, half))
            for b in range(BLK):
                n = (GROUPS - 1) * BLK + b
                pe.wait_ge(cur_ready[b], GROUPS)
                open_block(n, x1c[:, b, :])
                with nc.tensor.Fori(0, BODIES) as it:
                    slots(n, it)
                close_block(n)
            n = GROUPS * BLK
            pe.wait_ge(x4_in, 16 * (QUARTERS - 1))
            open_block(n, xs4[:, :], SAMP)
            with nc.tensor.Fori(0, BODIES // QUARTERS) as it:
                slots(n, it, width=SAMP)
            close_block(n, sel4, SAMP)

        @block.vector
        def _(dve):
            V = nc.vector

            def fence():
                dve.drain()

            def setup():
                V.memset(zeros[:, :], 0.0)
                V.memset(kT[:, 0:P], 0.0)
                V.memset(vR[:, 0, :], 0.0).then_inc(cleared, 1)
                dve.wait_ge(line_ps, 1)
                V.tensor_tensor(line[0:HEADS], acc[0:HEADS, 0:384], lmask[0:HEADS], ALU.add).then_inc(line_sb, 1)

            def sample_bias():
                dve.wait_ge(consts, 16 * N_CONSTS)
                dve.wait_ge(early_in, 15 * 16)
                dve.wait_ge(sbias_ps, 1)
                for t in range(2):
                    for n in range(2):
                        V.tensor_tensor(sBias[:, t, n * WIN:(n + 1) * WIN], acc[:, 512:512 + WIN],
                                        sMask[:, t, n * WIN:(n + 1) * WIN], ALU.add)
                    m = V.tensor_tensor(sBias[:, t, 256:288].rearrange("p (s i) -> p s i", s=SEQS),
                                        acc[:, 512 + WIN:512 + WIN + DSEQ].unsqueeze(1).to_broadcast([P, SEQS, DSEQ]),
                                        sMask[:, t, 256:288].rearrange("p (s i) -> p s i", s=SEQS), ALU.add)
                m.then_inc(sbias_sb, 1)

            def pool_windows(g):
                dve.wait_ge(proj_evac, g * PROJ + 6)
                if not first(g):
                    dve.wait_ge(score_out, 16)
                n = HIST + GN
                src, dst = poolT, t1
                for c in range(4):
                    w = 2 ** c
                    V.tensor_tensor(dst[:, c:, 2 * w - 1:n], src[:, c:, 2 * w - 1:n], src[:, c:, w - 1:n - w], ALU.add)
                    fence()
                    V.scalar_tensor_tensor(pooled[:, c, SAMP:], dst[:, c, HIST:n], 1.0 / (2 * w), poolT[:, c, HIST:n],
                                           ALU.mult, ALU.subtract)
                    src, dst = dst, (t2 if dst is t1 else t1)
                    fence()
                if first(g):
                    e = PSTATE + DSEQ
                    for c in range(4):
                        src, dst = sPool[:, c], sT1
                        for k in range(c + 1):
                            w = 2 ** k
                            V.tensor_tensor(dst[:, :, 2 * w - 1:e], src[:, :, 2 * w - 1:e], src[:, :, w - 1:e - w],
                                            ALU.add)
                            fence()
                            src, dst = dst, (sT2 if dst is sT1 else sT1)
                        V.scalar_tensor_tensor(pooled[:, c, 0:SAMP].rearrange("p (s i) -> p s i", s=SEQS),
                                               src[:, :, PSTATE:e], 1.0 / 2 ** (c + 1), sPool[:, c, :, PSTATE:e],
                                               ALU.mult, ALU.subtract)
                        fence()
                V.tensor_copy(poolT[:, :, 0:HIST], poolT[:, :, GN:GN + HIST]).then_inc(pool_ready, 1)

            def attention_pass(g, i):
                b, kv = divmod(i, 2)
                s = S[i % 2]
                bi = bias[:, 4 * kv:4 * kv + 4, :].rearrange("p h j -> p (h j)")
                dve.wait_ge(score_ready, g * 4 + (i + 1))
                if i >= 2:
                    dve.wait_ge(pt_ready, g * 4 + (i - 1))
                if first(g) and b == 0:
                    s4 = s.rearrange("p (h j) -> p h j", h=HPK)
                    r4 = wide[0][:, :].rearrange("p (h j) -> p h j", h=HPK)
                    b4 = bias[:, 4 * kv:4 * kv + 4, :]
                    V.memset(s4[:, :, META:P], NEG)
                    V.scalar_tensor_tensor(s4[:, :, 0:META], r4[:, :, 0:META], SCALE, b4[:, :, P - META:P],
                                           ALU.mult, ALU.add)
                    V.scalar_tensor_tensor(s4[:, :, P:], r4[:, :, P:], SCALE, b4[:, :, P:], ALU.mult, ALU.add)
                else:
                    V.scalar_tensor_tensor(s, wide[0][:, :], SCALE, bi, ALU.mult, ALU.add)
                fence()
                mx, nm, sk, den = amx[:, i % 2, :], anm[:, i % 2, :], ads[:, i % 2, :], aden[:, i % 2, :]
                V.tensor_reduce(mx, s.rearrange("p (h j) -> p h j", h=HPK), AX.X, ALU.max)
                fence()
                V.tensor_tensor(mx, mx, sink[:, 4 * kv:4 * kv + 4], ALU.max)
                fence()
                V.tensor_scalar(nm, mx, -1.0, None, ALU.mult)
                V.tensor_tensor(sk, sink[:, 4 * kv:4 * kv + 4], mx, ALU.subtract).then_inc(max_ready, 1)
                dve.wait_ge(exp_done, g * 4 + (i + 1))
                V.tensor_tensor(den, den, sk, ALU.add)
                fence()
                V.reciprocal(den, den)
                fence()
                V.tensor_tensor(s.rearrange("p (h j) -> p h j", h=HPK), s.rearrange("p (h j) -> p h j", h=HPK),
                                den.unsqueeze(2).to_broadcast([P, HPK, 256]), ALU.mult).then_inc(p_ready, 1)

            def sample_attention():
                for s in range(SEQS):
                    m = V.tensor_copy(sQ[:, s // 2, 16 * (s % 2):16 * (s % 2) + 16].rearrange("p (c i) -> p c i", c=HPK),
                                      qT[:, :, DSEQ * s:DSEQ * s + DSEQ])
                m.then_inc(sq_ready, 1)
                mx, nm, den, sk = sSmall[:, 0:2], sSmall[:, 2:4], sSmall[:, 4:6], sSmall[:, 6:8]
                dve.wait_ge(s_score, 1)
                for t in range(2):
                    V.scalar_tensor_tensor(sS[:, t, :], wide[0][:, t * 512:t * 512 + 288], SCALE, sBias[:, t, :],
                                           ALU.mult, ALU.add)
                fence()
                V.tensor_reduce(mx, sS, AX.X, ALU.max)
                fence()
                V.tensor_tensor(mx, mx, sSink, ALU.max)
                fence()
                V.tensor_scalar(nm, mx, -1.0, None, ALU.mult)
                V.tensor_tensor(sk, sSink, mx, ALU.subtract).then_inc(s_max, 1)
                dve.wait_ge(s_exp, 1)
                V.tensor_tensor(den, den, sk, ALU.add)
                fence()
                V.reciprocal(den, den)
                fence()
                V.tensor_tensor(sS, sS, den.unsqueeze(2).to_broadcast([P, 2, 288]), ALU.mult).then_inc(s_p, 1)

            def merge(g, chunks):
                dve.wait_ge(gate_sig, g * 4 + (4 if chunks[0] >= 4 else 2))
                c0 = META if first(g) else X0
                l0 = lo(g, SAMP)
                for j in chunks:
                    dve.wait_ge(unit_done, g * UNITS + (ordinal(POS_UP) + j + 1))
                    pa, pb = (pj[0], pj[1]) if j % 2 == 0 else (wide[1][:, 0:512], wide[1][:, 512:1024])
                    V.tensor_tensor(gates[:, j, l0:], gates[:, j, l0:], pa[:, c0:COLS], ALU.mult)
                    V.tensor_tensor(gates[:, 8 + j, l0:], gates[:, 8 + j, l0:], pb[:, c0:COLS], ALU.mult)\
                        .then_inc(up_read, 1)
                    fence()
                    V.tensor_tensor(xm[:, j, c0:COLS], gates[:, j, l0:], gates[:, 8 + j, l0:], ALU.add)\
                        .then_inc(m_ready, 1)

            def normalise(out, src, g_, b_, mom, st, var_sem, std_sem, count):
                rows = out.shape[0]
                V.bn_stats(st[0:rows, 0:6], src[:, 0:512])
                V.bn_stats(st[0:rows, 6:12], src[:, 512:1024])
                fence()
                V.bn_aggr(mom[0:rows, 0:2], st[0:rows, :])
                fence()
                V.tensor_scalar(mom[0:rows, 1:2], mom[0:rows, 1:2], EPS, None, ALU.add).then_inc(var_sem, 1)
                dve.wait_ge(std_sem, count)
                V.reciprocal(mom[0:rows, 3:4], mom[0:rows, 2:3])
                fence()
                V.tensor_scalar(out, src, mom[0:rows, 0:1], mom[0:rows, 3:4], ALU.subtract, ALU.mult)
                fence()
                V.tensor_tensor(out, out, g_[0:rows], ALU.mult)
                fence()
                return V.tensor_tensor(out, out, b_[0:rows], ALU.add)

            def norm1(g, blocks):
                dve.wait_ge(unit_done, g * UNITS + (ordinal(POS_OUT) + N_OUT))
                dve.wait_ge(ln1_in, g * 32 + 32)
                dve.wait_ge(xr_in, g * 32 + 32)
                for b in blocks:
                    x = x1n[:, b, :] if b < BLK else x1s
                    y = wide[b][:, :] if b < BLK else acc[0:SAMP, :]
                    if b == BLK:
                        dve.wait_ge(xs_in, 16)
                    V.scalar_tensor_tensor(x, x, ALPHA, y, ALU.mult, ALU.add)
                    fence()
                    normalise(x, x, ln1g, ln1b, moments, stats, ln1_var, ln1_std, nth(g, b)).then_inc(x1_ready, 1)

            def top16(top, idx, vals):
                sets = range(len(vals))
                for half in range(2):
                    h8 = slice(8 * half, 8 * half + 8)
                    for n in sets:
                        V.max(top[n][:, h8], vals[n])
                    fence()
                    for n in sets:
                        V.max_index(idx[n][:, h8], top[n][:, h8], vals[n])
                    fence()
                    if half == 0:
                        for n in sets:
                            V.match_replace(vals[n], top[n][:, h8], vals[n], NEG)
                        fence()

            def retrieve_heads(sc, rows, heads):
                sets = [(h, c) for h in heads for c in range(2)]
                top16([tops[0:rows, h, c, :] for h, c in sets], [topi[0:rows, h, c, :] for h, c in sets],
                      [sc[:, (2 * h + c) * P:(2 * h + c + 1) * P] for h, c in sets])
                for h in heads:
                    V.tensor_tensor(sc[:, h * 256:(h + 1) * 256].rearrange("p (a c) -> p a c", a=TOPK),
                                    tops[0:rows, h, 0, :].unsqueeze(2).to_broadcast([rows, TOPK, TOPK]),
                                    tops[0:rows, h, 1, :].unsqueeze(1).to_broadcast([rows, TOPK, TOPK]), ALU.add)
                fence()
                top16([bests[0:rows, h, :] for h in heads], [bestj[0:rows, h, :] for h in heads],
                      [sc[:, h * 256:(h + 1) * 256] for h in heads])

            def retrieve_indices(sc, rows, idx, heads):
                hs = slice(heads[0], heads[-1] + 1)
                ks = slice(heads[0] * TOPK, (heads[-1] + 1) * TOPK)
                count = len(heads) * TOPK
                V.tensor_copy(topf[0:rows, hs], topi[0:rows, hs])
                own = sc[:, ks.start * TOPK:ks.stop * TOPK]
                hot = own.rearrange("p (m a) -> p m a", a=TOPK)
                hot4 = own.rearrange("p (h k a) -> p h k a", h=len(heads), k=TOPK)
                flat = bestj[0:rows, hs].rearrange("p h k -> p (h k)")
                for c in range(2):
                    if c == 0:
                        V.tensor_scalar(jpart[0:rows, ks], flat, 4, None, ALU.logical_shift_right)
                    else:
                        V.tensor_scalar(jpart[0:rows, ks], flat, 15, None, ALU.bitwise_and)
                    fence()
                    V.tensor_copy(jf[0:rows, ks], jpart[0:rows, ks])
                    fence()
                    V.tensor_tensor(hot, jf[0:rows, ks].unsqueeze(2).to_broadcast([rows, count, TOPK]),
                                    iota[0:rows].unsqueeze(1).to_broadcast([rows, count, TOPK]), ALU.is_equal)
                    fence()
                    V.tensor_tensor(hot4, hot4, topf[0:rows, hs, c, :].unsqueeze(2)
                                    .to_broadcast([rows, len(heads), TOPK, TOPK]), ALU.mult)
                    fence()
                    V.tensor_reduce(ipart[0:rows, c, ks], hot, AX.X, ALU.add)
                    fence()
                V.scalar_tensor_tensor(idx[:, ks], ipart[0:rows, 0, ks], float(P), ipart[0:rows, 1, ks],
                                       ALU.mult, ALU.add)

            def start_gates(rows, gate):
                fence()
                V.tensor_tensor(gate.rearrange("p (h k) -> p h k", h=HEADS), bests[0:rows],
                                bests[0:rows, :, 0:1].to_broadcast([rows, HEADS, TOPK]),
                                ALU.subtract).then_inc(gmax_ready, 1)

            def end_gates(rows, gate, count):
                gate3 = gate.rearrange("p (h k) -> p h k", h=HEADS)
                dve.wait_ge(gexp_done, count)
                V.tensor_reduce(gsum[0:rows], gate3, AX.X, ALU.add)
                fence()
                V.reciprocal(gsum[0:rows], gsum[0:rows])
                fence()
                return V.tensor_tensor(gate3, gate3, gsum[0:rows].unsqueeze(2).to_broadcast([rows, HEADS, TOPK]),
                                       ALU.mult)

            def hand_over(g, b, idle):
                wait(dve, y_out[b], idle)
                if b == 0 and first(g):
                    V.tensor_copy(idxc[:, b, RING:], idxn[:, b, RING:])
                else:
                    V.tensor_copy(idxc[:, b, :], idxn[:, b, :]).then_inc(first_ready[b], 1)
                V.tensor_copy(gatec[:, b, :], gaten[:, b, :])
                V.tensor_copy(x1c[:, b, :], x1n[:, b, :]).then_inc(cur_ready[b], 1)

            def open_block(n, x, share):
                dve.wait_ge(acc_done, n + 1)
                V.tensor_scalar(acc_v[:, :], x, share, None, ALU.mult)

            def slots(n, it, x, gate, half=None, share=ALPHA):
                opens = isinstance(it, int) and it == 0 and half != 1

                def dots(m):
                    for j in range(BATCH):
                        k = m * BATCH + j
                        u = ring[:, k % RING, 0:D]
                        dve.wait_ge(gathered[k % RING], n * (16 * SLOTS // RING) + it * 32 + 16 * (k // RING + 1))
                        V.tensor_tensor_reduce(u, u, x, 1.0, 0.0, ALU.mult, ALU.add, hdot[:, m % 2, j:j + 1])\
                            .then_inc(dot_done, 1)

                def weigh(m):
                    tile = (m * BATCH + BATCH - 1) % RING
                    dve.wait_ge(gelu_done, n * (SLOTS // BATCH) + it * (BODY // BATCH) + (m + 1))
                    V.tensor_tensor(hw[:, m % 2, :], hgelu[:, m % 2, :],
                                    gate[:, bass.ds(it * BODY + m * BATCH, BATCH)], ALU.mult).then_inc(w_ready, 1)
                    fence()
                    V.scalar_tensor_tensor(acc_v[:, :], ring[:, tile, D:2 * D], hw[:, m % 2, BATCH - 1:BATCH],
                                           acc_v[:, :], ALU.mult, ALU.add).then_inc(vslot_free, 1)

                for m in batches(half):
                    dots(m)
                    if opens and m == 0:
                        open_block(n, x, share)
                    weigh(m)

            def close_block():
                dve.drain().then_inc(accv_ready, 1)

            def norm2(n, x):
                dve.wait_ge(acc_read, n + 2)
                normalise(x, x, ln2g, ln2b, moments2, stats2, ln2_var, ln2_std, n + 1).then_inc(y_ready, 1)

            def retrieve_b(step, g):
                sc, idx = scores_of(1), idxn[:, 1, :]
                if step < 4:
                    retrieve_heads(sc, P, range(2 * step, 2 * step + 2))
                if step == 3:
                    start_gates(P, gaten[:, 1, :])
                if step in (4, 5):
                    heads = {4: range(0, 4), 5: range(4, 8)}[step]
                    retrieve_indices(sc, P, idx, heads)
                if step == 5:
                    end_gates(P, gaten[:, 1, :], g * BLK)
                    fence()
                    hand_over(g - 1, 1, g * 16)

            def rounds(g, body):
                peer = not first(g)
                sa, sb_ = scores_of(0), scores_of(1)
                for step in range(4):
                    body(0, step // 2, step % 2)
                    if peer:
                        retrieve_b(step, g)
                    if step == 2:
                        if first(g):
                            sample_bias()
                        pool_windows(g)
                for i in range(4):
                    body(0, 2 + i, 0)
                    attention_pass(g, i)
                    if i == 0 and peer:
                        retrieve_b(4, g)
                    body(0, 2 + i, 1)
                    if i == 0 and peer:
                        retrieve_b(5, g)
                if first(g):
                    sample_attention()
                body(0, 6, 0)
                body(0, 6, 1)
                merge(g, range(0, 2))
                body(0, 7, 0)
                merge(g, range(2, 4))
                dve.wait_ge(o_ready, g * 4 + 4)
                V.tensor_copy(kT[:, 0:P], kT[:, GN:GN + P])
                V.tensor_copy(vR[:, 0, :], vR[:, BLK, :]).then_inc(carried, 1)
                body(0, 7, 1)
                if peer:
                    close_block()
                merge(g, range(4, 6))
                body(1, 0, 0)
                merge(g, range(6, 8))
                if peer:
                    norm2((g - 1) * BLK, x1c[:, 0, :])
                body(1, 0, 1)
                body(1, 1, 0)
                norm1(g, range(0, 1))
                body(1, 1, 1)
                norm1(g, range(1, BLK + first(g)))
                if first(g):
                    dve.nop(nofuse=True).then_inc(vslot_free, DVE_TILES)
                body(1, 2, 0)
                body(1, 2, 1)
                idx = idxn[:, 0, :]
                for step, heads in enumerate((range(0, 1), range(1, 2), range(2, 3), range(3, 4), range(4, 6),
                                              range(6, 7))):
                    body(1, 3 + step // 2, step % 2)
                    hold(dve, sc_evac, g * N_QRY + 2 * heads[-1] + 2)
                    retrieve_heads(sa, P, heads)
                    if step == 4 and first(g):
                        V.tensor_copy(idxc[:, 0, 0:RING], idx[:, 0:RING]).then_inc(first_ready[0], 1)
                    if step == 3:
                        retrieve_indices(sa, P, idx, range(0, 4))
                    if step == 5:
                        retrieve_indices(sa, P, idx, range(4, 6))
                body(1, 6, 0)
                hold(dve, sc_evac, g * N_QRY + N_QRY)
                retrieve_heads(sa, P, range(7, 8))
                start_gates(P, gaten[:, 0, :])
                body(1, 6, 1)
                retrieve_indices(sa, P, idx, range(6, 8))
                body(1, 7, 0)
                end_gates(P, gaten[:, 0, :], g * BLK + 1)
                fence()
                hand_over(g, 0, g * 16)
                body(1, 7, 1)
                if peer:
                    close_block()
                    norm2((g - 1) * BLK + 1, x1c[:, 1, :])

            setup()
            dve.nop(nofuse=True).then_inc(up_read, 2)
            dve.nop(nofuse=True).then_inc(y_out[1], 16)
            rounds(0, lambda b, it, half: None)
            dve.drain().then_inc(acc_read, 1)
            with V.Fori(1, GROUPS) as g:
                rounds(g, lambda b, it, half: slots((g - 1) * BLK + b, it, x1c[:, b, :], gatec[:, b, :], half))
            n = (GROUPS - 1) * BLK
            x, gate = x1c[:, 0, :], gatec[:, 0, :]
            ss = scores_of(0)[0:SAMP]
            for step in range(2 * BODIES):
                slots(n, step // 2, x, gate, step % 2)
                if step < 6:
                    retrieve_b(step, GROUPS)
                elif step < 6 + HEADS:
                    if step == 6:
                        dve.wait_ge(samp_scores, 16)
                    retrieve_heads(ss, SAMP, range(step - 6, step - 5))
                    if step in (8, 10, 12):
                        retrieve_indices(ss, SAMP, idxn[0:SAMP, 0, :], range(step - 8, step - 6))
                    if step == 5 + HEADS:
                        start_gates(SAMP, gaten[0:SAMP, 0, :])
                elif step == 6 + HEADS:
                    retrieve_indices(ss, SAMP, idxn[0:SAMP, 0, :], range(6, 8))
                else:
                    end_gates(SAMP, gaten[0:SAMP, 0, :], GROUPS * BLK + 1).then_inc(samp_got, 1)
            close_block()
            xb, gate = x1c[:, 1, :], gatec[:, 1, :]
            slots(n + 1, 0, xb, gate)
            norm2(n, x)
            with V.Fori(1, BODIES) as it:
                slots(n + 1, it, xb, gate)
            close_block()
            dve.wait_ge(x4_in, 16 * (QUARTERS - 1))
            dve.wait_ge(samp_in, 16 * 2 * QUARTERS)
            slots(n + 2, 0, xs4[:, :], gate4[:, :], share=ALPHA / QUARTERS)
            norm2(n + 1, xb)
            slots(n + 2, 1, xs4[:, :], gate4[:, :])
            close_block()
            norm2(n + 2, x1s)


def kernel(**inputs):
    import numpy as np
    import concourse.bacc as bacc
    from concourse.bass_utils import run_bass_kernel_spmd

    a = {k: np.asarray(v) for k, v in inputs.items()}

    w_in = a["w_in"][0]
    def cols(w):
        return np.ascontiguousarray(w.reshape(DC, P, P).transpose(1, 0, 2)).reshape(P, D)
    wq = w_in[:, 512:1024].reshape(D, 2, HPK, HD).transpose(0, 2, 1, 3).reshape(D, 512)
    units = [cols(w_in[:, 1024:1152]), cols(w_in[:, 1152:1280])]
    units += [cols(w_in[:, n * P:(n + 1) * P]) for n in range(4)]
    units += [cols(wq[:, n * P:(n + 1) * P]) for n in range(4)]
    units += [cols(w_in[:, 1280 + n * P:1280 + (n + 1) * P]) for n in range(16)]
    up_p = a["w_up_pool"][0].reshape(4, P, DC, P)
    up_a = a["w_up_attn"][0].reshape(2, HPK, HD, D).transpose(1, 0, 2, 3).reshape(4, P, DC, P)
    both = np.concatenate([up_p, up_a], axis=0)
    units += [both[:, :, j].transpose(1, 0, 2).reshape(P, D) for j in range(DC)]
    wo = a["w_out"][0].reshape(2, 4, P, 4, 256)
    units += [wo[h, :, :, q].transpose(1, 0, 2).reshape(P, D) for q in range(4) for h in range(2)]
    w_a = np.ascontiguousarray(np.stack(units))
    wqry = a["peer_w_query"][0]
    keys = a["peer_sub_keys"][0].reshape(2 * HEADS, P, P)
    w_q = np.stack([np.concatenate([cols(wqry[:, n * P:(n + 1) * P]), keys[n].T], axis=1) for n in range(16)])

    x = a["x_prompt"][0]
    xT = x.reshape(GROUPS, GN, DC, P).transpose(0, 3, 2, 1)
    xs = a["x_sample"].reshape(SAMP, D)
    extra = np.concatenate([a["meta_tokens"], xs], axis=0).reshape(X0, DC, P).transpose(2, 1, 0)
    sinks = a["attn_sinks"][0]
    sink_rows = np.broadcast_to(sinks.reshape(1, 2, 1, HPK, 1, 1), (2, 2, 2, HPK, DSEQ, 2)).reshape(P, 2)

    dist = 255 - np.arange(384)
    n = np.maximum(dist, 0)
    large = 16 + (np.log(np.maximum(n, 16).astype(np.float32) / 16) / np.log(8.0) * 16).astype(np.int32)
    bucket = np.where(n < 16, n, np.minimum(large, 31))
    inside = (dist >= 0) & (dist < WIN)
    onehot = ((np.arange(32)[:, None] == bucket[None, :]) & inside[None, :]).astype(np.float32)
    linemask = np.broadcast_to(np.where(inside, 0.0, NEG).astype(np.float32), (HEADS, 384))
    sel = np.zeros((DSEQ, HEADS, P), np.float32)
    smask = np.full((P, 2, 288), NEG, np.float32)
    for pr in range(2):
        for kv in range(2):
            for s in range(2):
                for h in range(HPK):
                    for i in range(DSEQ):
                        r = pr * 64 + kv * 32 + s * 16 + h * 4 + i
                        sel[i, kv * HPK + h, r] = 1.0
                        for t in range(2):
                            smask[r, t, s * WIN:(s + 1) * WIN] = 0.0
                            q = 2 * (2 * t + pr) + s
                            smask[r, t, 256 + q * DSEQ:256 + (q + 1) * DSEQ] = 0.0

    arrays = {
        "xT": xT, "xT_extra": extra, "x_rows": x.reshape(GROUPS * BLK, P, D), "xs_rows": xs, "w_a": w_a, "w_q": w_q,
        "uv": np.concatenate([a["peer_u"][0], a["peer_v"][0]], axis=1), "table": a["rel_bias_table"],
        "sinks": sinks, "sink_rows": sink_rows,
        "w_mix": a["w_pool_mix"][0].transpose(1, 0, 2), "pool_scale": a["pool_scale"][0].reshape(4, P).T,
        "ln1_g": a["ln1_g"][0], "ln1_b": a["ln1_b"][0], "ln2_g": a["ln2_g"][0], "ln2_b": a["ln2_b"][0],
        "ckT": a["cache_k"][0].reshape(SEQS, WIN, P).transpose(2, 0, 1),
        "cv_rows": a["cache_v"][0].reshape(SEQS, WIN, P).transpose(1, 0, 2),
        "cache_v": a["cache_v"][0].reshape(SEQS, WIN, P),
        "stT": a["state_pool"][0].reshape(SEQS, PSTATE, 4, P).transpose(3, 2, 0, 1),
        "ident": np.eye(P, dtype=np.float32), "flip": np.eye(P, dtype=np.float32)[::-1], "onehot": onehot,
        "linemask": linemask, "sel": sel, "smask": smask,
        "iota": np.broadcast_to(np.arange(TOPK, dtype=np.float32), (P, TOPK)),
        "sel4": np.tile(np.eye(SAMP, dtype=np.float32), (QUARTERS, 1)),
    }
    outs = {"y_prompt": (GROUPS * BLK, P, D), "y_sample": (SAMP, D), "k_prompt": (P, P), "v_prompt": (P, P),
            "pool_prompt": (P, 4, PSTATE), "k_sample": (P, SEQS, WIN), "v_sample": (SEQS, WIN, P),
            "pool_sample": (P, 4, SEQS, PSTATE)}
    nc = bacc.Bacc("TRN2", target_bir_lowering=False, num_devices=1)
    data = {"in_" + k: np.ascontiguousarray(v) for k, v in arrays.items()}
    args = [nc.dram_tensor(k, v.shape, mybir.dt.from_np(v.dtype), kind="ExternalInput").ap() for k, v in data.items()]
    args.append(nc.dram_tensor("line_scratch", (HEADS, 384), F32, kind="Internal").ap())
    args.append(nc.dram_tensor("score_scratch", (SAMP, 2048), F32, kind="Internal").ap())
    args += [nc.dram_tensor("out_" + k, s, F32, kind="ExternalOutput").ap() for k, s in outs.items()]
    layer_kernel(nc, *args)
    r = run_bass_kernel_spmd(nc, [data], core_ids=[0]).results[0]
    o = {k: r["out_" + k] for k in outs}
    return (o["y_prompt"].reshape(1, GROUPS * GN, D), o["y_sample"].reshape(SEQS, DSEQ, D),
            np.ascontiguousarray(o["k_prompt"].T).reshape(1, 1, P, 2, HD), o["v_prompt"].reshape(1, 1, P, 2, HD),
            np.ascontiguousarray(o["pool_prompt"].transpose(2, 1, 0)).reshape(1, 1, PSTATE, 512),
            np.ascontiguousarray(o["k_sample"].transpose(1, 2, 0)).reshape(1, SEQS, WIN, 2, HD),
            o["v_sample"].reshape(1, SEQS, WIN, 2, HD),
            np.ascontiguousarray(o["pool_sample"].transpose(2, 3, 1, 0)).reshape(1, SEQS, PSTATE, 512))
```
